# Optimizing a Trainium2 kernel written in Bass

```python
import math
import jax, jax.numpy as jnp
from jax import lax
import numpy as np

D_MODEL = 2048
BATCH = 1
SEQ = 512
DEPTH = 1
DEC_BATCH = 8
DEC_SEQ = 8
PAST_LEN = 4096
PAGE_SIZE = 128

D_HEAD = 128
H_SB = 4
H_DSA = 6
KV_DSA = 2
H_NSA = 6
KV_NSA = 2
G_DSA = H_DSA // KV_DSA
G_NSA = H_NSA // KV_NSA
D_MIX = (H_SB + H_DSA + H_NSA) * D_HEAD
IDX_HEADS = 4
IDX_DIM = 64
DSA_TOPK = 256
CMP_BLOCK = 32
SLC_BLOCK = 64
SLC_TOPN = 16
WINDOW = 512
NUM_BUCKETS = 32
MAX_DISTANCE = 1024
Q_BLOCK = 128
EPS = 1e-6
NEG = -1e30
POS_PAD = 1 << 30

SPLITS = (
    ('sb_q', (H_SB, D_HEAD)), ('sb_k', (H_SB, D_HEAD)), ('sb_v', (H_SB, D_HEAD)), ('sb_g', (H_SB * D_HEAD,)),
    ('dsa_q', (H_DSA, D_HEAD)), ('dsa_k', (KV_DSA, D_HEAD)), ('dsa_v', (KV_DSA, D_HEAD)), ('dsa_g', (H_DSA * D_HEAD,)),
    ('idx_q', (IDX_HEADS, IDX_DIM)), ('idx_k', (IDX_DIM,)), ('idx_w', (IDX_HEADS,)),
    ('nsa_q', (H_NSA, D_HEAD)), ('nsa_kc', (KV_NSA, D_HEAD)), ('nsa_vc', (KV_NSA, D_HEAD)),
    ('nsa_ks', (KV_NSA, D_HEAD)), ('nsa_vs', (KV_NSA, D_HEAD)), ('nsa_kw', (KV_NSA, D_HEAD)),
    ('nsa_vw', (KV_NSA, D_HEAD)), ('nsa_g', (H_NSA * D_HEAD,)), ('nsa_bg', (3, H_NSA)),
)
D_IN = sum(math.prod(s) for _, s in SPLITS)
QUERY_KEYS = ('sb_q', 'sb_g', 'dsa_q', 'dsa_g', 'idx_q', 'idx_w', 'nsa_q', 'nsa_g', 'nsa_bg')

kernel_name = 'hybrid_stickbreak_dsa_nsa_step'

def rmsnorm(x, g):
    xf = x.astype(jnp.float32)
    y = xf * lax.rsqrt(jnp.mean(xf * xf, axis=-1, keepdims=True) + EPS)
    return (y * g.astype(jnp.float32)).astype(x.dtype)

def masked_softmax(logits, mask):
    logits = jnp.where(mask, logits.astype(jnp.float32), NEG)
    m = jnp.max(logits, axis=-1, keepdims=True)
    e = jnp.where(mask, jnp.exp(logits - m), 0.0)
    return e / jnp.maximum(jnp.sum(e, axis=-1, keepdims=True), 1e-30)

def t5_bucket(dist):
    n = jnp.maximum(dist, 0)
    exact = NUM_BUCKETS // 2
    nf = jnp.maximum(n, 1).astype(jnp.float32)
    large = exact + (jnp.log(nf / exact) / math.log(MAX_DISTANCE / exact) * (NUM_BUCKETS - exact)).astype(jnp.int32)
    large = jnp.minimum(large, NUM_BUCKETS - 1)
    return jnp.where(n < exact, n, large)

def grouped_bias(table, dist, n_kv):
    b = table[t5_bucket(dist)]
    tq, l, h = b.shape
    return b.reshape(tq, l, n_kv, h // n_kv).transpose(0, 2, 3, 1)[None]

def project(h, w_in):
    bsz, t = h.shape[:2]
    p = h @ w_in
    out, off = {}, 0
    for name, shape in SPLITS:
        width = math.prod(shape)
        out[name] = p[..., off:off + width].reshape(bsz, t, *shape)
        off += width
    return out

def compress(kv, pe, w1, w2):
    bsz, l = kv.shape[:2]
    nc = l // CMP_BLOCK
    blk = kv[:, :nc * CMP_BLOCK].reshape(bsz, nc, CMP_BLOCK, 2, KV_NSA, D_HEAD) + pe
    blk = blk.transpose(0, 1, 3, 4, 2, 5).reshape(bsz, nc, 2, KV_NSA, CMP_BLOCK * D_HEAD)
    hid = jax.nn.silu(jnp.einsum('bcpki,pkie->bcpke', blk, w1))
    return jnp.einsum('bcpke,pkef->bcpkf', hid, w2)

def stick_breaking(q, k, v, q_pos, k_pos):
    z = jnp.einsum('bqhd,bkhd->bhqk', q, k).astype(jnp.float32) * (D_HEAD ** -0.5)
    causal = k_pos[None, :] < q_pos[:, None]
    log_keep = jnp.where(causal, jax.nn.log_sigmoid(-z), 0.0)
    log_after = lax.cumsum(log_keep, axis=3, reverse=True) - log_keep
    a = jnp.where(causal, jnp.exp(jax.nn.log_sigmoid(z) + log_after), 0.0)
    return jnp.einsum('bhqk,bkhd->bqhd', a.astype(v.dtype), v)

def dsa_attention(q, iq, iw, k, v, ik, q_pos, k_pos, table):
    bsz, tq = q.shape[:2]
    l = k.shape[1]
    top = min(DSA_TOPK, l // 4)
    s = jnp.einsum('bqhi,bki->bqhk', iq, ik)
    score = jnp.einsum('bqhk,bqh->bqk', jax.nn.relu(s), iw).astype(jnp.float32)
    causal = k_pos[None, :] <= q_pos[:, None]
    score = jnp.where(causal[None], score, -jnp.inf)
    vals, idx = lax.top_k(score, top)
    valid = jnp.isfinite(vals)
    k_sel = jax.vmap(lambda a, i: a[i])(k, idx)
    v_sel = jax.vmap(lambda a, i: a[i])(v, idx)
    pos_sel = k_pos[idx]
    qg = q.reshape(bsz, tq, KV_DSA, G_DSA, D_HEAD)
    logits = jnp.einsum('bqkgd,bqskd->bqkgs', qg, k_sel).astype(jnp.float32) * (D_HEAD ** -0.5)
    bias = table[t5_bucket(q_pos[None, :, None] - pos_sel)]
    bias = bias.reshape(bsz, tq, top, KV_DSA, G_DSA).transpose(0, 1, 3, 4, 2)
    p = masked_softmax(logits + bias, valid[:, :, None, None, :])
    o = jnp.einsum('bqkgs,bqskd->bqkgd', p.astype(v.dtype), v_sel)
    return o.reshape(bsz, tq, H_DSA, D_HEAD)

def nsa_attention(q, gates, cmp_k, cmp_v, slc_k, slc_v, win_k, win_v, q_pos, k_pos, win_pos, table):
    bsz, tq = q.shape[:2]
    l = slc_k.shape[1]
    nc = cmp_k.shape[1]
    scale = D_HEAD ** -0.5
    dt = q.dtype
    qg = q.reshape(bsz, tq, KV_NSA, G_NSA, D_HEAD)
    cmp_end = k_pos[CMP_BLOCK - 1::CMP_BLOCK]
    lc = jnp.einsum('bqkgd,bckd->bqkgc', qg, cmp_k).astype(jnp.float32) * scale
    lc = lc + grouped_bias(table, q_pos[:, None] - cmp_end[None, :], KV_NSA)
    pc = masked_softmax(lc, (cmp_end[None, :] <= q_pos[:, None])[None, :, None, None, :])
    o_cmp = jnp.einsum('bqkgc,bckd->bqkgd', pc.astype(dt), cmp_v)
    ns = -(-l // SLC_BLOCK)
    imp = jnp.sum(pc, axis=3)
    imp = jnp.pad(imp, ((0, 0), (0, 0), (0, 0), (0, 2 * ns - nc))).reshape(bsz, tq, KV_NSA, ns, 2).sum(-1)
    blk = jnp.arange(ns, dtype=jnp.int32)[None, :]
    q_blk = (q_pos // SLC_BLOCK)[:, None]
    adm = (blk <= q_blk)[None, :, None, :]
    forced = ((blk == 0) | (blk == q_blk) | (blk == q_blk - 1))[None, :, None, :]
    score = jnp.where(adm, jnp.where(forced, 1e4, imp), -jnp.inf)
    n_sel = min(SLC_TOPN, ns)
    vals, sel = lax.top_k(score, n_sel)
    sel_ok = jnp.isfinite(vals)
    pad = ns * SLC_BLOCK - l

    def blocks(a):
        a = jnp.pad(a, ((0, 0), (0, pad), (0, 0), (0, 0)))
        return a.reshape(bsz, ns, SLC_BLOCK, KV_NSA, D_HEAD).transpose(0, 3, 1, 2, 4)

    bi = jnp.arange(bsz)[:, None, None, None]
    hi = jnp.arange(KV_NSA)[None, None, :, None]
    ks = blocks(slc_k)[bi, hi, sel]
    vs = blocks(slc_v)[bi, hi, sel]
    pos_blk = jnp.pad(k_pos, (0, pad), constant_values=POS_PAD).reshape(ns, SLC_BLOCK)[sel]
    ok = (pos_blk <= q_pos[None, :, None, None, None]) & sel_ok[..., None]
    ls = jnp.einsum('bqkgd,bqknsd->bqkgns', qg, ks).astype(jnp.float32) * scale
    tbl = table.reshape(NUM_BUCKETS, KV_NSA, G_NSA).transpose(1, 0, 2)
    bs = tbl[jnp.arange(KV_NSA)[None, None, :, None, None], t5_bucket(q_pos[None, :, None, None, None] - pos_blk)]
    bs = jnp.moveaxis(bs, -1, 3)
    ls = (ls + bs).reshape(bsz, tq, KV_NSA, G_NSA, n_sel * SLC_BLOCK)
    ps = masked_softmax(ls, ok.reshape(bsz, tq, KV_NSA, 1, n_sel * SLC_BLOCK))
    o_slc = jnp.einsum('bqkgs,bqksd->bqkgd', ps.astype(dt), vs.reshape(bsz, tq, KV_NSA, n_sel * SLC_BLOCK, D_HEAD))
    lw = jnp.einsum('bqkgd,bwkd->bqkgw', qg, win_k).astype(jnp.float32) * scale
    lw = lw + grouped_bias(table, q_pos[:, None] - win_pos[None, :], KV_NSA)
    wmask = (win_pos[None, :] <= q_pos[:, None]) & (q_pos[:, None] - win_pos[None, :] < WINDOW)
    pw = masked_softmax(lw, wmask[None, :, None, None, :])
    o_win = jnp.einsum('bqkgw,bwkd->bqkgd', pw.astype(dt), win_v)
    g = jax.nn.sigmoid(gates.astype(jnp.float32)).astype(dt).reshape(bsz, tq, 3, KV_NSA, G_NSA, 1)
    o = g[:, :, 0] * o_cmp + g[:, :, 1] * o_slc + g[:, :, 2] * o_win
    return o.reshape(bsz, tq, H_NSA, D_HEAD)

def build_keys(sb_kv, dsa_kv, idx_k, nsa_kv, pe, w1, w2):
    cmp = compress(nsa_kv[:, :, :2], pe, w1, w2)
    return dict(sb_k=sb_kv[:, :, 0], sb_v=sb_kv[:, :, 1], dsa_k=dsa_kv[:, :, 0], dsa_v=dsa_kv[:, :, 1],
                idx_k=idx_k, cmp_k=cmp[:, :, 0], cmp_v=cmp[:, :, 1], slc_k=nsa_kv[:, :, 2], slc_v=nsa_kv[:, :, 3])

def mix(qd, q_pos, kd, k_pos, win_kv, win_pos, rel_bias):
    bsz, tq = qd['sb_g'].shape[:2]
    o_sb = stick_breaking(qd['sb_q'], kd['sb_k'], kd['sb_v'], q_pos, k_pos)
    o_dsa = dsa_attention(qd['dsa_q'], qd['idx_q'], qd['idx_w'], kd['dsa_k'], kd['dsa_v'], kd['idx_k'],
                          q_pos, k_pos, rel_bias[:, :H_DSA])
    o_nsa = nsa_attention(qd['nsa_q'], qd['nsa_bg'], kd['cmp_k'], kd['cmp_v'], kd['slc_k'], kd['slc_v'],
                          win_kv[:, :, 0], win_kv[:, :, 1], q_pos, k_pos, win_pos, rel_bias[:, H_DSA:])
    return jnp.concatenate([
        o_sb.reshape(bsz, tq, -1) * jax.nn.silu(qd['sb_g']),
        o_dsa.reshape(bsz, tq, -1) * jax.nn.silu(qd['dsa_g']),
        o_nsa.reshape(bsz, tq, -1) * jax.nn.silu(qd['nsa_g']),
    ], axis=-1)

def new_rows(p):
    sb = jnp.stack([p['sb_k'], p['sb_v']], axis=2)
    dsa = jnp.stack([p['dsa_k'], p['dsa_v']], axis=2)
    nsa = jnp.stack([p['nsa_kc'], p['nsa_vc'], p['nsa_ks'], p['nsa_vs']], axis=2)
    win = jnp.stack([p['nsa_kw'], p['nsa_vw']], axis=2)
    return sb, dsa, p['idx_k'], nsa, win

def prompt_layer(x, w_in, w_out, g_pre, g_post, pe, w1, w2, rel_bias):
    bsz, s, _ = x.shape
    p = project(rmsnorm(x, g_pre), w_in)
    sb, dsa, idx, nsa, win = new_rows(p)
    kd = build_keys(sb, dsa, idx, nsa, pe, w1, w2)
    k_pos = jnp.arange(s, dtype=jnp.int32)
    win_pad = jnp.pad(win, ((0, 0), (WINDOW, 0), (0, 0), (0, 0), (0, 0)))
    nq = s // Q_BLOCK
    qblocks = {n: jnp.swapaxes(p[n].reshape(bsz, nq, Q_BLOCK, *p[n].shape[2:]), 0, 1) for n in QUERY_KEYS}

    def block(args):
        qd, start = args
        q_pos = start + jnp.arange(Q_BLOCK, dtype=jnp.int32)
        win_blk = lax.dynamic_slice_in_dim(win_pad, start, WINDOW + Q_BLOCK, axis=1)
        win_pos = start - WINDOW + jnp.arange(WINDOW + Q_BLOCK, dtype=jnp.int32)
        return mix(qd, q_pos, kd, k_pos, win_blk, win_pos, rel_bias)

    o = lax.map(block, (qblocks, jnp.arange(nq, dtype=jnp.int32) * Q_BLOCK))
    o = jnp.swapaxes(o, 0, 1).reshape(bsz, s, D_MIX)
    y = x + rmsnorm(o @ w_out, g_post)
    return y, (sb, dsa, idx, nsa, win[:, s - min(WINDOW, s):])

def sample_layer(x, c_sb, c_dsa, c_idx, c_nsa, s_win, page_table, w_in, w_out, g_pre, g_post, pe, w1, w2, rel_bias):
    bsz, t, _ = x.shape
    p = project(rmsnorm(x, g_pre), w_in)
    sb, dsa, idx, nsa, win = new_rows(p)

    def with_past(cache, new):
        past = cache[page_table].reshape(bsz, -1, *cache.shape[2:])
        return jnp.concatenate([past, new.astype(past.dtype)], axis=1)

    kd = build_keys(with_past(c_sb, sb), with_past(c_dsa, dsa), with_past(c_idx, idx), with_past(c_nsa, nsa), pe, w1, w2)
    past_len = page_table.shape[1] * PAGE_SIZE
    k_pos = jnp.arange(past_len + t, dtype=jnp.int32)
    q_pos = past_len + jnp.arange(t, dtype=jnp.int32)
    win_all = jnp.concatenate([s_win, win.astype(s_win.dtype)], axis=1)
    win_pos = past_len - s_win.shape[1] + jnp.arange(win_all.shape[1], dtype=jnp.int32)
    o = mix(p, q_pos, kd, k_pos, win_all, win_pos, rel_bias)
    y = x + rmsnorm(o @ w_out, g_post)
    keep = min(WINDOW, past_len + t)
    return y, (sb, dsa, idx, nsa, win_all[:, win_all.shape[1] - keep:])

def setup_inputs(seed: int = 0) -> dict:
    key = jax.random.key(seed)
    ks = jax.random.split(key, 18)
    n_pages = PAST_LEN // PAGE_SIZE
    n_pool = (DEC_BATCH * n_pages * 5) // 4
    win_keep = min(WINDOW, PAST_LEN)
    nrm = jax.random.normal
    f32 = jnp.float32
    page_table = jax.random.permutation(ks[7], n_pool)[:DEC_BATCH * n_pages].reshape(DEC_BATCH, n_pages).astype(jnp.int32)
    return {
        'x_prompt': nrm(ks[0], (BATCH, SEQ, D_MODEL), f32),
        'x_sample': nrm(ks[1], (DEC_BATCH, DEC_SEQ, D_MODEL), f32),
        'cache_sb_kv': nrm(ks[2], (DEPTH, n_pool, PAGE_SIZE, 2, H_SB, D_HEAD), f32),
        'cache_dsa_kv': nrm(ks[3], (DEPTH, n_pool, PAGE_SIZE, 2, KV_DSA, D_HEAD), f32),
        'cache_dsa_idx': nrm(ks[4], (DEPTH, n_pool, PAGE_SIZE, IDX_DIM), f32),
        'cache_nsa_kv': nrm(ks[5], (DEPTH, n_pool, PAGE_SIZE, 4, KV_NSA, D_HEAD), f32),
        'state_nsa_win': nrm(ks[6], (DEPTH, DEC_BATCH, win_keep, 2, KV_NSA, D_HEAD), f32),
        'page_table': page_table,
        'w_in': nrm(ks[8], (DEPTH, D_MODEL, D_IN), f32) * D_MODEL ** -0.5,
        'w_out': nrm(ks[9], (DEPTH, D_MIX, D_MODEL), f32) * D_MIX ** -0.5,
        'norm_pre': 1.0 + 0.1 * nrm(ks[10], (DEPTH, D_MODEL), f32),
        'norm_post': 1.0 + 0.1 * nrm(ks[11], (DEPTH, D_MODEL), f32),
        'cmp_pe': 0.5 * nrm(ks[12], (DEPTH, CMP_BLOCK, 2, KV_NSA, D_HEAD), f32),
        'cmp_w1': nrm(ks[13], (DEPTH, 2, KV_NSA, CMP_BLOCK * D_HEAD, D_HEAD), f32) * (CMP_BLOCK * D_HEAD) ** -0.5,
        'cmp_w2': nrm(ks[14], (DEPTH, 2, KV_NSA, D_HEAD, D_HEAD), f32) * D_HEAD ** -0.5,
        'rel_bias': 0.5 * nrm(ks[15], (NUM_BUCKETS, H_DSA + H_NSA), f32),
    }

def reference(x_prompt, x_sample, cache_sb_kv, cache_dsa_kv, cache_dsa_idx, cache_nsa_kv, state_nsa_win,
              page_table, w_in, w_out, norm_pre, norm_post, cmp_pe, cmp_w1, cmp_w2, rel_bias):
    hp, hs = x_prompt, x_sample
    rows_p, rows_s = [], []
    for l in range(DEPTH):
        hp, rp = prompt_layer(hp, w_in[l], w_out[l], norm_pre[l], norm_post[l],
                              cmp_pe[l], cmp_w1[l], cmp_w2[l], rel_bias)
        hs, rs = sample_layer(hs, cache_sb_kv[l], cache_dsa_kv[l], cache_dsa_idx[l], cache_nsa_kv[l],
                              state_nsa_win[l], page_table, w_in[l], w_out[l], norm_pre[l], norm_post[l],
                              cmp_pe[l], cmp_w1[l], cmp_w2[l], rel_bias)
        rows_p.append(rp)
        rows_s.append(rs)
    sb_p = jnp.stack([r[0] for r in rows_p])
    sb_s = jnp.stack([r[0] for r in rows_s])
    dsa_p = jnp.stack([r[1] for r in rows_p])
    dsa_s = jnp.stack([r[1] for r in rows_s])
    idx_p = jnp.stack([r[2] for r in rows_p])
    idx_s = jnp.stack([r[2] for r in rows_s])
    nsa_p = jnp.stack([r[3] for r in rows_p])
    nsa_s = jnp.stack([r[3] for r in rows_s])
    win_p = jnp.stack([r[4] for r in rows_p])
    win_s = jnp.stack([r[4] for r in rows_s])
    return (hp, hs, sb_p, sb_s, dsa_p, dsa_s, idx_p, idx_s, nsa_p, nsa_s, win_p, win_s)


_drawn_inputs = setup_inputs


def setup_inputs(seed=0):
    import zlib

    import numpy as np

    out = dict(_drawn_inputs(seed))
    spreads = {}
    factors = {}
    for name, (base, spread) in spreads.items():
        noise = np.random.default_rng([zlib.crc32(name.encode()), seed]).standard_normal(out[name].shape)
        drawn = base * np.exp(spread * noise) if base else spread * noise
        out[name] = __import__('jax').numpy.asarray(drawn.astype(out[name].dtype))
    for name, factor in factors.items():
        out[name] = (out[name] * factor).astype(out[name].dtype)
    return out
```

```python
import math
from contextlib import ExitStack

import numpy as np
import concourse.bass as bass
from concourse import mybir

F32 = mybir.dt.float32
BF16 = mybir.dt.bfloat16
I32 = mybir.dt.int32
ALU = mybir.AluOpType
ACT = mybir.ActivationFunctionType
AX = mybir.AxisListType

P = 128
D = 2048
SEQ = 512
NB, NT = 8, 8
NS = NB * NT
PAST = 4096
NPG = PAST // P
KEYS = PAST + NT
DH = 128
NBUCK = 32
HB = 12
WIN = 512
CMPB, SLCB = 32, 64
NC = PAST // CMPB
NSB = 65
TOPK_S, TOPK_P = 256, 128
SLC_TOPN = 16
EPS = 1e-6
NEG = -1e30
GONE = -3e38
SCALE = DH ** -0.5
DIN = 7510
KT_IN = D // P
TOK = SEQ + NS
CH = 512
NCH = PAST // CH
PPC = CH // P

SB_Q, SB_K, SB_V, SB_G = 0, 512, 1024, 1536
DSA_Q, DSA_K, DSA_V, DSA_G = 2048, 2816, 3072, 3328
IDX_Q, IDX_K, IDX_W = 4096, 4352, 4416
NSA_Q, NSA_KC, NSA_KS, NSA_VS, NSA_KW, NSA_VW, NSA_G, NSA_BG = 4420, 5188, 5700, 5956, 6212, 6468, 6724, 7492

DMAX = PAST + NT - 1
LINE = DMAX + P
XW = SEQ + P
XL = XW + P - 1

C_ID = 0
C_NM = C_ID + P
C_STRICT = C_NM + NT
C_WM = C_STRICT + NT
C_SELI = C_WM + NT
C_SELG = C_SELI + 2 * NS
C_SELE = C_SELG + 4 * P
C_SELD = C_SELE + 4 * P
C_KEPT = C_SELD + 4 * P
C_PM = C_KEPT
C_CM = C_PM + XW
C_TRI = C_CM + 4 * 16
C_END = C_TRI + P


def bucket(dist):
    n = np.maximum(dist, 0)
    nf = np.maximum(n, 1).astype(np.float32)
    large = 16 + (np.log(nf / np.float32(16)) / np.float32(math.log(64)) * np.float32(16)).astype(np.int32)
    return np.where(n < 16, n, np.minimum(large, NBUCK - 1))


def constants():
    c = np.zeros((P, C_END), np.float32)
    p = np.arange(P)[:, None]
    c[:, C_ID:C_ID + P] = np.eye(P)
    x = np.arange(XW)[None]
    c[:, C_PM:C_PM + XW] = np.where((p - x + SEQ >= 0) & (p - x + SEQ < WIN), 0, NEG)
    t, j = p % NT, np.arange(NT)[None]
    c[:, C_NM:C_NM + NT] = np.where(j > t, NEG, 0)
    c[:, C_STRICT:C_STRICT + NT] = j < t
    c[:, C_WM:C_WM + NT] = np.where(j <= t, NEG, 0)
    for g in range(2):
        for r in range(P):
            b, _, tt = g * 4 + r // 32, r % 32 // 8, r % 8
            c[r, C_SELI + g * NS + b * NT + tt] = 1
    for g in range(4):
        for r in range(P):
            b2, q = divmod(r, 64)
            if q < 48:
                kv, tt = q // 24, q % 8
                b = 2 * g + b2
                c[r, C_SELG + g * P + b * 16 + kv * 8 + tt] = 1
                c[b * 16 + kv * 8 + tt, C_SELE + g * P + r] = 1
                c[b * NT + tt, C_SELD + g * P + r] = 1
    for i in range(4):
        e = np.arange(16)[None] * CMPB + CMPB - 1
        c[:, C_CM + i * 16:C_CM + i * 16 + 16] = e <= i * P + p
    c[:, C_TRI:C_TRI + P] = np.arange(P)[None] < p
    onehot = np.zeros((NBUCK, LINE), np.float32)
    y = np.arange(LINE)
    onehot[bucket(DMAX - y), y] = 1
    return c, onehot


class Kept:
    pass


class Io:
    pass


class Scope:

    def __init__(self, nc, ctx, tag):
        self.nc, self.ctx, self.tag, self.sems = nc, ctx, tag, []
        ctx.callback(self.clear)

    def sb(self, name, shape, dt=F32):
        return self.ctx.enter_context(self.nc.sbuf_tensor(f"{self.tag}_{name}", shape, dt))

    def ps(self, name, shape, dt=F32):
        return self.ctx.enter_context(self.nc.psum_tensor(f"{self.tag}_{name}", shape, dt))

    def sem(self, name):
        self.sems.append(self.nc.alloc_semaphore(f"{self.tag}_{name}"))
        return self.sems[-1]

    def clear(self):
        if self.sems:
            self.nc.clear_and_free_semaphores(self.sems)
            self.nc.all_engine_barrier()


def setup_and_norm(nc, io, kept, hT):
    with ExitStack() as ctx:
        s = Scope(nc, ctx, "norm")
        x = s.sb("x", [P, 2, D])
        sq = s.sb("sq", [P, D])
        ss = s.sb("ss", [P, 5])
        rstd = s.sb("rstd", [P, 5])
        gcol = s.sb("gcol", [P, KT_IN])
        table = s.sb("table", [NBUCK, HB])
        onehot = s.sb("onehot", [NBUCK, LINE])
        line = s.sb("line", [HB, LINE])
        tp = [s.ps(f"tp{i}", [P, 4, P]) for i in range(2)]
        lp = [s.ps(f"lp{i}", [HB, CH]) for i in range(2)]
        consts_in, gain_in, table_in, onehot_in = s.sem("consts_in"), s.sem("gain_in"), s.sem("table_in"), s.sem("onehot_in")
        x_in = [s.sem(f"x_in{i}") for i in range(2)]
        squared, rooted, scaled, normed = s.sem("squared"), s.sem("rooted"), s.sem("scaled"), s.sem("normed")
        turned, hT_written = s.sem("turned"), s.sem("hT_written")
        line_done, line_copied, line_out = s.sem("line_done"), s.sem("line_copied"), s.sem("line_out")
        bf_ready, pt_in = s.sem("bf_ready"), s.sem("pt_in")
        block = ctx.enter_context(nc.Block())
        rows = [P, P, P, P, NS]
        pieces = [(c, min(CH, LINE - c)) for c in range(0, LINE, CH)]

        @block.sync
        def _(sp):
            sp.dma_start(kept.consts[:], io.consts[:, 0:C_KEPT]).then_inc(consts_in, 16)
            for m in range(5):
                if m >= 2:
                    sp.wait_ge(turned, 4 * (m - 1))
                src = io.xp[m * P:(m + 1) * P, :] if m < 4 else io.xs
                sp.dma_start(x[0:rows[m], m % 2, :], src).then_inc(x_in[m % 2], 16)
                if m == 1:
                    sp.dma_start(table[:], io.rel_bias).then_inc(table_in, 16)
                    sp.dma_start(onehot[:], io.onehot).then_inc(onehot_in, 16)
                    sp.dma_start(kept.pages[:], io.page_table.rearrange("b n -> (b n)").rearrange("(a n) -> a n", a=1)).then_inc(pt_in, 16)
            sp.wait_ge(line_copied, len(pieces))
            sp.dma_start(io.line, line[:]).then_inc(line_out, 16)
            sp.wait_ge(line_out, 16)
            sp.wait_ge(pt_in, 16)

        @block.gpsimd
        def _(pool):
            with nc.allow_non_contiguous_dma(reason="a small column"):
                pool.dma_start(gcol[:], io.norm_pre.rearrange("(k p) -> p k", p=P)).then_inc(gain_in, 16)
            pool.wait_ge(gain_in, 16)

        @block.scalar
        def _(act):
            act.preload_act_table_set("natural_log_exp_and_others")
            for m in range(5):
                act.wait_ge(x_in[m % 2], 16 * (m // 2 + 1))
                if m:
                    act.wait_ge(squared, m)
                act.activation(sq[0:rows[m], :], x[0:rows[m], m % 2, :], ACT.Square,
                               accum_out=ss[0:rows[m], m:m + 1]).then_inc(squared, 1)
                act.wait_ge(scaled, m + 1)
                act.activation(rstd[0:rows[m], m:m + 1], rstd[0:rows[m], m:m + 1], ACT.Ln).then_inc(rooted, 1)
                act.wait_ge(rooted, 2 * m + 1)
                act.activation(rstd[0:rows[m], m:m + 1], rstd[0:rows[m], m:m + 1], ACT.Exp, scale=-0.5).then_inc(rooted, 1)
            for n, (c, w) in enumerate(pieces):
                act.wait_ge(line_done, n + 1)
                act.copy(line[:, c:c + w], lp[n % 2][:, 0:w]).then_inc(line_copied, 1)

        @block.tensor
        def _(pe):
            pe.wait_ge(consts_in, 16)
            for m in range(5):
                pe.wait_ge(normed, m + 1)
                for q in range(4):
                    n = 4 * m + q
                    if n >= 2:
                        pe.wait_ge(hT_written, n - 1)
                    for k in range(4):
                        last = pe.transpose(tp[n % 2][:, k, 0:rows[m]], x[0:rows[m], m % 2, (4 * q + k) * P:(4 * q + k + 1) * P],
                                            kept.ident[0:rows[m], 0:rows[m]])
                    last.then_inc(turned, 1)
            pe.wait_ge(table_in, 16)
            pe.wait_ge(onehot_in, 16)
            for n, (c, w) in enumerate(pieces):
                if n >= 2:
                    pe.wait_ge(line_copied, n - 1)
                pe.matmul(lp[n % 2][:, 0:w], table[:], onehot[:, c:c + w], start=True, stop=True).then_inc(line_done, 1)

        @block.vector
        def _(dve):
            dve.wait_ge(consts_in, 16)
            dve.tensor_copy(kept.sel_e[:], kept.consts[:, C_SELE:C_SELE + 4 * P]).then_inc(bf_ready, 1)
            dve.tensor_copy(kept.sel_d[:], kept.consts[0:NS, C_SELD:C_SELD + 4 * P]).then_inc(bf_ready, 1)
            dve.tensor_copy(kept.ident_b[:], kept.ident).then_inc(bf_ready, 1)
            dve.memset(kept.ones[:], 1.0).then_inc(bf_ready, 1)

            def norm(m):
                r = rows[m]
                dve.wait_ge(squared, m + 1)
                dve.tensor_scalar(rstd[0:r, m:m + 1], ss[0:r, m:m + 1], 1.0 / D, EPS, ALU.mult, ALU.add).then_inc(scaled, 1)
                dve.wait_ge(rooted, 2 * m + 2)
                dve.tensor_scalar(x[0:r, m % 2, :], x[0:r, m % 2, :], rstd[0:r, m:m + 1], None, ALU.mult).then_inc(normed, 1)

            norm(0)
            dve.wait_ge(gain_in, 16)
            for m in range(5):
                if m < 4:
                    norm(m + 1)
                r = rows[m]
                for q in range(4):
                    n = 4 * m + q
                    dve.wait_ge(turned, n + 1)
                    dve.tensor_tensor(hT[:, 4 * q:4 * q + 4, m * P:m * P + r], tp[n % 2][:, :, 0:r],
                                      gcol[:, 4 * q:4 * q + 4].unsqueeze(2).to_broadcast([P, 4, r]), ALU.mult).then_inc(hT_written, 1)


def project_in(nc, io, hT):
    with ExitStack() as ctx:
        s = Scope(nc, ctx, "proj")
        w = [s.sb(f"w{i}", [P, KT_IN, CH]) for i in range(2)]
        out = [s.sb(f"out{i}", [P, 5, CH]) for i in range(2)]
        acc = [s.ps(f"acc{m}", [P, CH]) for m in range(5)]
        w_in = [s.sem(f"w_in{i}") for i in range(2)]
        w_used, summed, copied = s.sem("w_used"), s.sem("summed"), s.sem("copied")
        out_stored = [s.sem(f"out_stored{i}") for i in range(2)]
        block = ctx.enter_context(nc.Block())
        rows = [P, P, P, P, NS]
        CREDIT = 5 + 1
        whole = DIN // CH
        tail = DIN - whole * CH
        assert whole % 2 == 0

        def load_w(sp, u, col, width):
            src = io.w_in.rearrange("(k p) n -> p k n", p=P)
            for q in range(4):
                sp.dma_start(w[u][:, 4 * q:4 * q + 4, 0:width], src[:, 4 * q:4 * q + 4, col]).then_inc(w_in[u], 16)

        @block.sync
        def _(sp):
            with sp.Fori(0, whole // 2) as i:
                for u in range(2):
                    sp.wait_ge(summed, i * 10 + 5 * u + 1)
                    load_w(sp, u, bass.ds((i * 2 + u) * CH, CH), CH)
            sp.wait_ge(summed, 5 * whole + 1)
            load_w(sp, 0, slice(whole * CH, DIN), tail)

        @block.tensor
        def _(pe):
            pe.nop().then_inc(summed, CREDIT)

            def chunk(u, fills, n_waits, width):
                pe.wait_ge(w_in[u], fills)
                for m in range(5):
                    pe.wait_ge(copied, n_waits + m)
                    for k in range(KT_IN):
                        last = pe.matmul(acc[m][0:rows[m], 0:width], hT[:, k, m * P:m * P + rows[m]], w[u][:, k, 0:width],
                                         start=(k == 0), stop=(k == KT_IN - 1))
                    last.then_inc(summed, 1)

            with pe.Fori(0, whole // 2) as i:
                for u in range(2):
                    chunk(u, i * 64 + 64, i * 10 + 5 * u + 2, CH)
            chunk(0, 64 * (whole // 2 + 1), 5 * whole + 2, tail)

        def evacuate(eng, m, u, summed_by, stored_by, width):
            eng.wait_ge(summed, summed_by)
            eng.wait_ge(out_stored[u], stored_by)
            copy = eng.copy if eng is nc.scalar else eng.tensor_copy
            copy(out[u][0:rows[m], m, 0:width], acc[m][0:rows[m], 0:width]).then_inc(copied, 1)

        @block.vector
        def _(dve):
            dve.nop().then_inc(copied, CREDIT)
            with dve.Fori(0, whole // 2) as i:
                for u in range(2):
                    for m in range(5):
                        evacuate(dve, m, u, i * 10 + 5 * u + m + 1 + CREDIT, i * 32 + 16, CH)
            for m in range(5):
                evacuate(dve, m, 0, 5 * whole + m + 1 + CREDIT, 32 * (whole // 2) + 16, tail)

        @block.scalar
        def _(act):
            for u in range(2):
                act.nop().then_inc(out_stored[u], 16)

            def store(u, col, width, copied_by):
                act.wait_ge(copied, copied_by)
                act.dma_start(io.proj[0:SEQ, col].rearrange("(m p) n -> p m n", p=P), out[u][:, 0:4, 0:width]).then_inc(out_stored[u], 16)
                act.dma_start(io.proj[SEQ:TOK, col], out[u][0:NS, 4, 0:width]).then_inc(out_stored[u], 16)

            with act.Fori(0, whole // 2) as i:
                for u in range(2):
                    store(u, bass.ds((i * 2 + u) * CH, CH), CH, i * 10 + 5 * u + 5 + CREDIT)
            store(0, slice(whole * CH, DIN), tail, 5 * whole + 5 + CREDIT)
            act.wait_ge(out_stored[0], 32 * (whole // 2 + 1) + 16)
            act.wait_ge(out_stored[1], 32 * (whole // 2) + 16)


def prepare(nc, io, kept, keep):
    kept.q_sb = keep.sb("q_sb", [P, NB, 4, 32])
    kept.q_dsa = keep.sb("q_dsa", [P, NB, 2, 64])
    kept.q_nsa = keep.sb("q_nsa", [P, NB, 2, 64])
    kept.q_idx = keep.sb("q_idx", [P, 2, NB, 32])
    kept.k_sb = keep.sb("k_sb", [P, 4, NS])
    kept.k_dsa = keep.sb("k_dsa", [P, 2, NS])
    kept.k_slc = keep.sb("k_slc", [P, 2, NS])
    kept.k_win = keep.sb("k_win", [P, 2, NS])
    kept.k_idx = keep.sb("k_idx", [64, NS])
    kept.w_idx = keep.sb("w_idx", [P, 2])
    kept.gates = keep.sb("gates", [P, 4, 3])
    with ExitStack() as ctx:
        s = Scope(nc, ctx, "prep")
        new = s.sb("new", [NS, DIN])
        tp = [s.ps(f"tp{i}", [P, 8, NS]) for i in range(4)]
        new_in, copies_out, cols_in = s.sem("new_in"), s.sem("copies_out"), s.sem("cols_in")
        zeroed, turned, copied, gated = s.sem("zeroed"), s.sem("turned"), s.sem("copied"), s.sem("gated")
        block = ctx.enter_context(nc.Block())

        items = [(SB_Q + h * DH, kept.q_sb[:, :, h, h * 8:h * 8 + 8], SCALE) for h in range(4)]
        for col, q in ((DSA_Q, kept.q_dsa), (NSA_Q, kept.q_nsa)):
            items += [(col + h * DH, q[:, :, h // 3, h * 8:h * 8 + 8], SCALE) for h in range(6)]
        for col, k, n in ((SB_K, kept.k_sb, 4), (DSA_K, kept.k_dsa, 2), (NSA_KS, kept.k_slc, 2), (NSA_KW, kept.k_win, 2)):
            items += [(col + h * DH, k[:, h, :], None) for h in range(n)]
        n_full = len(items)
        idx_cols = [IDX_Q, IDX_Q + DH, IDX_K]
        total = n_full + 3

        @block.sync
        def _(sp):
            sp.dma_start(new[:], io.proj[SEQ:TOK, :]).then_inc(new_in, 16)
            sp.wait_ge(zeroed, 5)
            with nc.allow_non_contiguous_dma(reason="a few numbers per row"):
                for b in range(NB):
                    rows = io.proj[SEQ + b * NT:SEQ + b * NT + NT, :]
                    sp.dma_start(kept.w_idx[b % 4 * 32:b % 4 * 32 + 32, b // 4:b // 4 + 1],
                                 rows[:, IDX_W:IDX_W + 4].rearrange("t h -> h t").unsqueeze(2)).then_inc(cols_in, 16)
                    for r in range(3):
                        sp.dma_start(kept.gates[b % 2 * 64:b % 2 * 64 + 48, b // 2, r:r + 1],
                                     rows[:, NSA_BG + 6 * r:NSA_BG + 6 * r + 6].rearrange("t h -> h t").unsqueeze(2)).then_inc(cols_in, 16)
            sp.wait_ge(cols_in, 64 * NB)

        @block.gpsimd
        def _(pool):
            for n, t in enumerate((kept.q_sb, kept.q_dsa, kept.q_nsa, kept.q_idx, kept.gates)):
                pool.memset(t[:], 0.0).then_inc(zeroed, 1)

        @block.scalar
        def _(act):
            n = 0
            for to_p, to_s, col, width in io.new_rows:
                act.dma_start(to_p, io.proj[0:SEQ, col:col + width]).then_inc(copies_out, 16)
                act.dma_start(to_s, io.proj[SEQ:TOK, col:col + width]).then_inc(copies_out, 16)
                n += 2
            act.dma_start(io.win_p, io.proj[0:SEQ, NSA_KW:NSA_KW + 512]).then_inc(copies_out, 16)
            act.dma_start(io.win_s[:, WIN - NT:WIN, :], io.proj[SEQ:TOK, NSA_KW:NSA_KW + 512].rearrange("(b t) n -> b t n", t=NT)).then_inc(copies_out, 16)
            act.dma_start(io.win_s[:, 0:WIN - NT, :], io.win_state[:, NT:WIN, :]).then_inc(copies_out, 16)
            first = DMAX - SEQ - (P - 1)
            act.dma_start(io.lines, io.line[:, first:first + XL].unsqueeze(0).to_broadcast([P, HB, XL])).then_inc(copies_out, 16)
            act.wait_ge(cols_in, 64 * NB)
            act.activation(kept.gates[:], kept.gates[:], ACT.Exp, scale=-1.0).then_inc(gated, 1)
            act.wait_ge(zeroed, 5)
            for i, (_, to, scale) in enumerate(items):
                act.wait_ge(turned, i // 8 + 1)
                src = tp[i // 8][:, i % 8, :]
                if scale:
                    act.activation(to, src.rearrange("p (b t) -> p b t", t=NT), ACT.Copy, scale=scale).then_inc(copied, 1)
                else:
                    act.copy(to, src).then_inc(copied, 1)
            act.wait_ge(turned, 4)
            for j in range(2):
                src = tp[3][:, n_full - 24 + j, :].rearrange("p (b t) -> p b t", t=NT)
                for i in range(2):
                    h = 2 * j + i
                    for half in range(2):
                        act.copy(kept.q_idx[64 * half:64 * half + 64, half, :, h * 8:h * 8 + 8], src[64 * i:64 * i + 64]).then_inc(copied, 1)
            act.copy(kept.k_idx[:], tp[3][0:64, n_full - 24 + 2, :]).then_inc(copied, 1)
            act.wait_ge(copies_out, 16 * (n + 4))

        @block.tensor
        def _(pe):
            pe.wait_ge(new_in, 16)
            cols = [c for c, _, _ in items] + idx_cols
            for i, c in enumerate(cols):
                last = pe.transpose(tp[i // 8][:, i % 8, :], new[:, c:c + DH], kept.ident[0:NS, 0:NS])
                if i % 8 == 7 or i == total - 1:
                    last.then_inc(turned, 1)

        @block.vector
        def _(dve):
            dve.wait_ge(gated, 1)
            dve.tensor_scalar(kept.gates[:], kept.gates[:], 1.0, None, ALU.add).then_inc(gated, 1)
            dve.wait_ge(gated, 2)
            dve.reciprocal(kept.gates[:], kept.gates[:]).then_inc(gated, 1)


def load_pages(nc, io, sp, kept, to, cache, first, col, width, sem):
    _, pages = nc.values_load_multi_w_load_instructions(kept.pages[0:1, bass.ds(first, PPC)], engines=(mybir.EngineType.SP,),
                                                        min_val=0, max_val=io.n_pool - 1)
    for p, page in enumerate(pages):
        src = cache[bass.ds(page, 1), :, col:col + width].rearrange("o p c -> (o p) c")
        sp.dma_start(to[:, p], src).then_inc(sem, 16)


def compress(nc, io, kept, keep):
    kept.cmp_k = keep.sb("cmp_k", [P, NB, 2, NC])
    kept.cmp_v = keep.sb("cmp_v", [P, NB, 2, DH])
    with ExitStack() as ctx:
        s = Scope(nc, ctx, "cmp")
        w1 = s.sb("w1", [P, 4, CMPB, DH])
        w2 = s.sb("w2", [P, 4, DH])
        pe_rows = s.sb("pe_rows", [CMPB, 4, DH])
        peT = s.sb("peT", [P, 4, CMPB])
        shift = s.sb("shift", [P, 2, 4])
        rows = [s.sb(f"rows{i}", [P, PPC, 4, DH]) for i in range(2)]
        xT = s.sb("xT", [P, 4, PAST])
        hid = s.sb("hid", [P, 3, 4, NC])
        tp = [s.ps(f"tp{i}", [P, CH]) for i in range(2)]
        hp = s.ps("hp", [P, 4, NC])
        kp = s.ps("kp", [P, 2, NC])
        vp = s.ps("vp", [P, 2, DH])
        cp = s.ps("cp", [P, 4])
        w_in, rows_in = s.sem("w_in"), [s.sem(f"rows_in{i}") for i in range(2)]
        turned, x_even, x_odd = s.sem("turned"), s.sem("x_even"), s.sem("x_odd")
        hid_summed, hid_exp, hid_done, out_summed, out_copied = (
            s.sem("hid_summed"), s.sem("hid_exp"), s.sem("hid_done"), s.sem("out_summed"), s.sem("out_copied"))
        pe_turned, pe_copied, shift_summed, shift_done, hid_step = (
            s.sem("pe_turned"), s.sem("pe_copied"), s.sem("shift_summed"), s.sem("shift_done"), s.sem("hid_step"))
        block = ctx.enter_context(nc.Block())

        @block.sync
        def _(sp):
            sp.dma_start(pe_rows[:], io.cmp_pe).then_inc(w_in, 16)
            sp.dma_start(w2[:], io.cmp_w2.rearrange("a e f -> e a f")).then_inc(w_in, 16)
            for a in range(4):
                sp.dma_start(w1[:, a], io.cmp_w1[a]).then_inc(w_in, 16)
            sp.dma_start(rows[1][:], io.proj[0:SEQ, NSA_KC:NSA_KC + 512].rearrange("(m p) n -> p m n", p=P)).then_inc(rows_in[1], 64)
            with sp.Fori(0, NB * NCH // 2) as i:
                for u in range(2):
                    sp.wait_ge(turned, i * 8 + 4 * u + 4)
                    load_pages(nc, io, sp, kept, rows[u][:], io.nsa_cache, i * 8 + 4 * u, 0, 512, rows_in[u])

        def turn(pe, unit, u, filled):
            pe.wait_ge(rows_in[u], filled)
            for a in range(4):
                pe.wait_ge((x_even, x_odd)[a % 2], unit * 2 + a // 2 + 1)
                for p in range(PPC):
                    last = pe.transpose(tp[a % 2][:, p * P:(p + 1) * P], rows[u][:, p, a, :], kept.ident)
                last.then_inc(turned, 1)

        def mlp(pe, n, blocks, units_copied):
            pe.wait_ge(x_even, units_copied * 2 + 1)
            pe.wait_ge(x_odd, units_copied * 2 + 1)
            for a in range(4):
                xv = xT[:, a, 0:blocks * CMPB].rearrange("p (c r) -> p r c", r=CMPB)
                for r in range(CMPB):
                    last = pe.matmul(hp[:, a, 0:blocks], w1[:, a, r, :], xv[:, r, :], start=(r == 0), stop=(r == CMPB - 1))
            last.then_inc(hid_summed, 1)
            pe.wait_ge(hid_done, n + 1)
            pe.wait_ge(out_copied, n * 2 + 2)
            for kv in range(2):
                pe.matmul(kp[:, kv, 0:blocks], w2[:, kv, :], hid[:, 2, kv, 0:blocks], start=True, stop=True)
            for kv in range(2):
                last = pe.matmul(vp[0:blocks, kv, :], hid[:, 2, 2 + kv, 0:blocks], w2[:, 2 + kv, :], start=True, stop=True)
            last.then_inc(out_summed, 1)

        @block.tensor
        def _(pe):
            pe.nop().then_inc(turned, 4)
            pe.wait_ge(w_in, 96)
            for a in range(4):
                last = pe.transpose(tp[0][:, a * CMPB:(a + 1) * CMPB], pe_rows[:, a, :], kept.ident[0:CMPB, 0:CMPB])
            last.then_inc(pe_turned, 1)
            pe.wait_ge(pe_copied, 1)
            for a in range(4):
                for r in range(CMPB):
                    last = pe.matmul(cp[:, a:a + 1], w1[:, a, r, :], peT[:, a, r:r + 1], start=(r == 0), stop=(r == CMPB - 1))
            last.then_inc(shift_summed, 1)
            turn(pe, 0, 1, 64)
            mlp(pe, 0, SEQ // CMPB, 1)
            with pe.Fori(0, NB) as b:
                with pe.Fori(0, NCH // 2) as c:
                    for u in range(2):
                        turn(pe, b * 8 + c * 2 + (u + 1), u, (b * 4 + c) * 64 + (64 if u == 0 else 128))
                mlp(pe, b + 1, NC, b * 8 + 9)

        def copy_part(eng, sem, a, unit, at, last_mlp):
            eng.wait_ge(turned, unit * 4 + a + 1 + 4)
            eng.wait_ge(hid_summed, last_mlp)
            copy = eng.copy if a % 2 else eng.tensor_copy
            copy(xT[:, a, at], tp[a % 2][:]).then_inc(sem, 1)

        @block.vector
        def _(dve):
            dve.nop().then_inc(x_even, 1)
            dve.nop().then_inc(hid_summed, 1)
            dve.wait_ge(pe_turned, 1)
            dve.tensor_copy(peT[:].rearrange("p a r -> p (a r)"), tp[0][:, 0:4 * CMPB]).then_inc(pe_copied, 1)
            dve.wait_ge(shift_summed, 1)
            dve.tensor_copy(shift[:, 0, :], cp[:]).then_inc(shift_done, 1)
            dve.wait_ge(shift_done, 1)
            dve.tensor_scalar(shift[:, 1, :], shift[:, 0, :], -1.0, None, ALU.mult).then_inc(shift_done, 1)

            def activate(n, blocks):
                dve.wait_ge(hid_exp, n + 1)
                dve.tensor_scalar(hid[:, 1, :, 0:blocks], hid[:, 0, :, 0:blocks], 1.0, None, ALU.add).then_inc(hid_step, 1)
                dve.wait_ge(hid_step, n * 2 + 1)
                dve.reciprocal(hid[:, 1, :, 0:blocks], hid[:, 1, :, 0:blocks]).then_inc(hid_step, 1)
                dve.wait_ge(hid_step, n * 2 + 2)
                dve.wait_ge(out_summed, n + 1)
                for a in range(4):
                    last = dve.scalar_tensor_tensor(hid[:, 2, a, 0:blocks], hp[:, a, 0:blocks], shift[:, 0, a:a + 1], hid[:, 1, a, 0:blocks], ALU.add, ALU.mult)
                last.then_inc(hid_done, 1)

            dve.nop().then_inc(out_summed, 1)
            for a in (0, 2):
                copy_part(dve, x_even, a, 0, slice(0, CH), 1)
            activate(0, SEQ // CMPB)
            with dve.Fori(0, NB) as b:
                with dve.Fori(0, NCH) as c:
                    for a in (0, 2):
                        copy_part(dve, x_even, a, b * 8 + c + 1, bass.ds(c * CH, CH), b + 2)
                activate(b + 1, NC)

        @block.scalar
        def _(act):
            act.preload_act_table_set("natural_log_exp_and_others")
            act.nop().then_inc(x_odd, 1)
            act.nop().then_inc(out_copied, 2)

            def exps(n, blocks):
                act.wait_ge(hid_summed, n + 2)
                act.wait_ge(hid_done, n) if not isinstance(n, int) else None
                for a in range(4):
                    last = act.activation(hid[:, 0, a, 0:blocks], hp[:, a, 0:blocks], ACT.Exp, bias=shift[:, 1, a:a + 1], scale=-1.0)
                last.then_inc(hid_exp, 1)

            def results(n, to_k, to_v, blocks):
                act.wait_ge(out_summed, n + 2)
                act.copy(to_k, kp[:, :, 0:blocks]).then_inc(out_copied, 1)
                act.copy(to_v, vp[0:blocks]).then_inc(out_copied, 1)

            for a in (1, 3):
                copy_part(act, x_odd, a, 0, slice(0, CH), 1)
            act.wait_ge(shift_done, 2)
            exps(0, SEQ // CMPB)
            results(0, kept.cmp_kp[:], kept.cmp_vp[:], SEQ // CMPB)
            with act.Fori(0, NB) as b:
                with act.Fori(0, NCH) as c:
                    for a in (1, 3):
                        copy_part(act, x_odd, a, b * 8 + c + 1, bass.ds(c * CH, CH), b + 2)
                exps(b + 1, NC)
                results(b + 1, kept.cmp_k[:, bass.ds(b, 1)].rearrange("p o k c -> p (o k) c"),
                        kept.cmp_v[:, bass.ds(b, 1)].rearrange("p o k c -> p (o k) c"), NC)


def index_scores(nc, io, kept, keep):
    kept.scores = keep.sb("scores", [NS, KEYS])
    kept.drop = keep.sb("drop", [NS, KEYS], BF16)
    with ExitStack() as ctx:
        s = Scope(nc, ctx, "idx")
        rows = s.sb("rows", [P, NB, PPC, 64])
        kT = [s.sb(f"kT{i}", [P, 2, P]) for i in range(2)]
        relu = [s.sb(f"relu{g}", [P, CH]) for g in range(2)]
        tp = [s.ps(f"tp{i}", [P, 2, P]) for i in range(2)]
        sp_ = [s.ps(f"sc{g}", [P, CH]) for g in range(2)]
        total = s.ps("total", [NS, CH])
        rows_in = [s.sem(f"rows_in{b}") for b in range(NB)]
        turned, even_copied, odd_copied, multiplied = s.sem("turned"), s.sem("even_copied"), s.sem("odd_copied"), s.sem("multiplied")
        weighted, summed, total_copied, masked = s.sem("weighted"), s.sem("summed"), s.sem("total_copied"), s.sem("masked")
        copied_by = (even_copied, odd_copied)
        block = ctx.enter_context(nc.Block())
        seli = [kept.consts[:, C_SELI + g * NS:C_SELI + (g + 1) * NS] for g in range(2)]

        @block.sync
        def _(sp):
            with sp.Fori(0, NCH) as c:
                for b in range(NB):
                    sp.wait_ge(turned, c * NB + b + 1)
                    load_pages(nc, io, sp, kept, rows[:, b], io.idx_cache, c * PPC + b * NPG, 0, 64, rows_in[b])

        @block.tensor
        def _(pe):
            pe.nop().then_inc(turned, NB)
            pe.nop().then_inc(multiplied, 2)

            def product(b, n):
                g, r = divmod(b, 4)
                pe.wait_ge(copied_by[b % 2], n + 2)
                for half in range(2):
                    to = sp_[g][32 * r:32 * r + 32, :].rearrange("p (q a k) -> p a q k", a=2, k=P)[:, half]
                    last = pe.matmul(to, kept.q_idx[:, half, b, :], kT[b % 2][:], start=(half == 0), stop=(half == 1),
                                     tile_position=(0, 32 * r), skip_group_check=True)
                last.then_inc(multiplied, 1)

            def add_up(g, c):
                pe.wait_ge(weighted, c * 2 + g + 3)
                pe.matmul(total[:], seli[g], relu[g][:], start=(g == 0), stop=(g == 1)).then_inc(summed, 1)

            with pe.Fori(0, NCH) as c:
                for b in range(NB):
                    pe.wait_ge(rows_in[b], c * 64 + 64)
                    pe.wait_ge(copied_by[b % 2], c * 4 + (b // 2 + 1))
                    for q in range(2):
                        last = pe.transpose(tp[b % 2][:, q, :], rows[:, b, 2 * q:2 * q + 2, :].rearrange("p a d -> p (a d)"), kept.ident)
                    last.then_inc(turned, 1)
                    if b == 1 or b == 5:
                        pe.wait_ge(weighted, c * 2 + b // 4 + 1)
                    if b:
                        product(b - 1, c * 4 + (b - 1) // 2)
                    if b == 6:
                        pe.wait_ge(total_copied, c + 1)
                        add_up(0, c)
                product(NB - 1, c * 4 + (NB - 1) // 2)
                add_up(1, c)
            n = NCH * NB
            for g in range(2):
                pe.wait_ge(weighted, NCH * 2 + g + 1)
                for r in range(4):
                    b = 4 * g + r
                    last = pe.matmul(sp_[g][32 * r:32 * r + 32, 0:NT], kept.q_idx[0:64, 0, b, :], kept.k_idx[:, b * NT:b * NT + NT],
                                     start=True, stop=True, tile_position=(0, 32 * r))
                last.then_inc(multiplied, 4)
            pe.wait_ge(total_copied, NCH + 1)
            for g in range(2):
                pe.wait_ge(weighted, NCH * 2 + g + 3)
                pe.matmul(total[:, 0:NT], seli[g], relu[g][:, 0:NT], start=(g == 0), stop=(g == 1)).then_inc(summed, 1)

        def copy_keys(eng, n, b):
            eng.wait_ge(turned, n + 1 + NB)
            eng.wait_ge(multiplied, n + 1)
            copy = eng.copy if b % 2 else eng.tensor_copy
            copy(kT[b % 2][:], tp[b % 2][:]).then_inc(copied_by[b % 2], 1)

        @block.vector
        def _(dve):
            dve.nop().then_inc(even_copied, 1)
            dve.nop().then_inc(weighted, 2)

            def weigh(g, c, width):
                dve.wait_ge(multiplied, c * NB + 4 * g + 4 + 2)
                dve.wait_ge(summed, c * 2 + g + 1)
                dve.tensor_scalar(relu[g][:, 0:width], sp_[g][:, 0:width], 0.0, kept.w_idx[:, g:g + 1], ALU.max, ALU.mult).then_inc(weighted, 1)

            with dve.Fori(0, NCH) as c:
                for b in range(NB):
                    if b % 2 == 0:
                        copy_keys(dve, c * NB + b, b)
                    if b == 5:
                        weigh(0, c, CH)
                weigh(1, c, CH)
            weigh(0, NCH, NT)
            weigh(1, NCH, NT)
            dve.wait_ge(summed, 2 * NCH + 2 + 2)
            dve.tensor_tensor(kept.scores[:, PAST:KEYS], total[:, 0:NT], kept.consts[0:NS, C_NM:C_NM + NT], ALU.add).then_inc(masked, 1)

        @block.scalar
        def _(act):
            act.nop().then_inc(odd_copied, 1)
            act.nop().then_inc(summed, 2)
            act.nop().then_inc(total_copied, 1)
            with act.Fori(0, NCH) as c:
                for b in range(1, NB, 2):
                    copy_keys(act, c * NB + b, b)
                act.wait_ge(summed, c * 2 + 4)
                act.copy(kept.scores[:, bass.ds(c * CH, CH)], total[:]).then_inc(total_copied, 1)


def stream(nc, io, kept, tag, *, cache, k_col, v_col, proj_v, heads, per, q, k_new, add_mask=None, bias_rows=None,
           bias_first=0, mask_last=None, head0, state=None, gate=None, add=False, stick=False):
    groups = NB // per
    stride = P // per
    nch = 1 if state is not None else NCH
    past = nch * CH
    width = heads * DH
    items = per * heads
    U = 2 if nch > 1 else 1
    with ExitStack() as ctx:
        s = Scope(nc, ctx, tag)
        k_rows = [s.sb(f"k_rows{b}", [P, PPC, width]) for b in range(per)]
        v_rows = [s.sb(f"v_rows{b}", [P, PPC, width]) for b in range(per)]
        v_new = s.sb("v_new", [NT, per, width])
        kT = [s.sb(f"kT{i}", [P, CH]) for i in range(2)]
        logits = [s.sb(f"logits{i}", [P, past + NT]) for i in range(2)]
        prob = [s.sb(f"prob{i}", [P, CH]) for i in range(2)]
        prob_new = s.sb("prob_new", [P, P])
        pT = [s.sb(f"pT{i}", [P, PPC, P]) for i in range(2)]
        pT_new = s.sb("pT_new", [NT, P])
        maxes = s.sb("maxes", [P, nch + 1])
        nmax = s.sb("nmax", [P, groups])
        sums = s.sb("sums", [P, groups, nch + 1])
        rcp = s.sb("rcp", [P, groups])
        if stick:
            soft = s.sb("soft", [P, KEYS])
            top8 = s.sb("top8", [NS, 8])
        else:
            bias = s.sb("bias", [P, past + NT])
            diag = s.sb("diag", [P, P])
            rcpT = s.sb("rcpT", [P, P])
            scaled = s.sb("scaled", [P, per, 48])
        tp = [s.ps(f"tp{i}", [P, CH]) for i in range(2)]
        sc = s.ps("sc", [P, CH])
        sc_new = s.ps("sc_new", [P, NT])
        qp = [s.ps(f"qp{i}", [P, PPC, P]) for i in range(2)]
        ov = [s.ps(f"ov{i}", [P, 3, P]) for i in range(2)]

        k_in, v_in = [s.sem(f"k_in{b}") for b in range(per)], [s.sem(f"v_in{b}") for b in range(per)]
        small_in, bias_in, zeroed = s.sem("small_in"), s.sem("bias_in"), s.sem("zeroed")
        k_turned, kT_copied, scored, logits_out, new_scored, new_out = (
            s.sem("k_turned"), s.sem("kT_copied"), s.sem("scored"), s.sem("logits_out"), s.sem("new_scored"), s.sem("new_out"))
        maxed, max_done, probs, probs_turned, pT_copied, v_used = (
            s.sem("maxed"), s.sem("max_done"), s.sem("probs"), s.sem("probs_turned"), s.sem("pT_copied"), s.sem("v_used"))
        new_prob, new_turned, new_copied, out_summed, rcp_done, rcp_spread, rcp_copied, out_done, step = (
            s.sem("new_prob"), s.sem("new_turned"), s.sem("new_copied"), s.sem("out_summed"), s.sem("rcp_done"),
            s.sem("rcp_spread"), s.sem("rcp_copied"), s.sem("out_done"), s.sem("step"))
        added = s.sem("added")
        if stick:
            top_step, dropped, soft_act, soft_dve, logits_act = (
                s.sem("top_step"), s.sem("dropped"), s.sem("soft_act"), s.sem("soft_dve"), s.sem("logits_act"))
        block = ctx.enter_context(nc.Block())
        order = [("k", 0)] + [x for g in range(1, groups) for x in (("k", g), ("v", g - 1))] + [("v", groups - 1)]

        def chunks(eng, step=1):
            return eng.Fori(0, nch // step)

        @block.sync
        def _(sp):
            if not stick:
                sp.wait_ge(zeroed, 2)
                for b in range(per):
                    for t in range(NT):
                        sp.dma_start(bias[b * stride + t:b * stride + t + 41:8, :],
                                     io.line[bias_rows:bias_rows + 6, bias_first + NT - 1 - t:bias_first + NT - 1 - t + past + NT]).then_inc(bias_in, 16)
            def load(to, sem, b, g, c, col):
                if state is None:
                    load_pages(nc, io, sp, kept, to[b], cache, c * PPC + (g * per + b) * NPG, col, width, sem[b])
                else:
                    sp.dma_start(to[b][:], state[g * per + b, :, col:col + width].rearrange("(m p) c -> p m c", p=P)).then_inc(sem[b], 64)

            for kind, g in order:
                if kind == "v":
                    if g:
                        sp.wait_ge(v_used, 2 * per + (g - 1) * nch * per + 1)
                    first = SEQ + g * per * NT
                    sp.dma_start(v_new[:], io.proj[first:first + per * NT, proj_v:proj_v + width].rearrange("(b t) c -> t b c", t=NT)).then_inc(small_in, 16)
                with chunks(sp) as c:
                    n = c + g * nch
                    for b in range(per):
                        if kind == "k":
                            sp.wait_ge(k_turned, n * items + (b + 1) * heads)
                            load(k_rows, k_in, b, g, c, k_col)
                        else:
                            sp.wait_ge(v_used, (n + 1) * per + b + 1)
                            load(v_rows, v_in, b, g, c, v_col)

        @block.gpsimd
        def _(pool):
            if not stick:
                pool.memset(bias[:], 0.0).then_inc(zeroed, 1)
            else:
                pool.nop().then_inc(zeroed, 1)
            pool.memset(prob_new[:], 0.0).then_inc(zeroed, 1)

        @block.tensor
        def _(pe):
            pe.nop().then_inc(k_turned, items)
            pe.nop().then_inc(scored, 2)
            pe.nop().then_inc(probs_turned, 2)
            pe.nop().then_inc(v_used, 2 * per)

            def turn(n, j):
                b, h = divmod(j, heads)
                if h == 0:
                    pe.wait_ge(k_in[b], n * 64 + 64)
                pe.wait_ge(kT_copied, n * items + j + 1)
                for p in range(PPC):
                    last = pe.transpose(tp[j % 2][:, p * P:(p + 1) * P], k_rows[b][:, p, h * DH:(h + 1) * DH], kept.ident)
                last.then_inc(k_turned, 1)

            def mask(g, to, at, w):
                if add_mask is not None:
                    lhs, rhs = add_mask(g, at, w)
                    pe.matmul(to, lhs, rhs, start=True, stop=False, skip_group_check=True)

            def score(g, n, c, j):
                b, h = divmod(j, heads)
                if j == 0:
                    pe.wait_ge(logits_out, n + 1)
                    mask(g, sc[:], c, CH)
                pe.wait_ge(kT_copied, n * items + j + 3)
                pe.matmul(sc[b * stride:(b + 1) * stride, :], q[:, g * per + b, h, :], kT[j % 2][:],
                          start=(add_mask is None and h == 0), stop=(h == heads - 1), skip_group_check=True,
                          tile_position=(0, b * stride)).then_inc(scored, 1)

            def keys(g):
                with chunks(pe) as c:
                    n = c + g * nch
                    for j in range(items + 1):
                        if j < items:
                            turn(n, j)
                        if j:
                            score(g, n, c, j - 1)
                pe.wait_ge(new_out, g + 1)
                mask(g, sc_new[:], None, NT)
                for j in range(items):
                    b, h = divmod(j, heads)
                    gb = g * per + b
                    last = pe.matmul(sc_new[b * stride:(b + 1) * stride, :], q[:, gb, h, :], k_new[:, h, gb * NT:(gb + 1) * NT],
                                     start=(add_mask is None and h == 0), stop=(h == heads - 1), skip_group_check=True,
                                     tile_position=(0, b * stride))
                last.then_inc(new_scored, 1)

            rows_per = stride // heads if stick else 24

            def values(g):
                out = ov[g % 2]

                def product(b, kv, v, probT, first, last):
                    r = b * stride + kv * rows_per
                    return pe.matmul(out[:, 0, r:r + rows_per], v, probT[:, r:r + rows_per], start=first, stop=last, skip_group_check=True)

                pe.wait_ge(new_prob, g + 1)
                pe.wait_ge(new_copied, g + 1)
                pe.wait_ge(small_in, 16 * (g + 1))
                pe.transpose(tp[0][:, 0:P], prob_new[:], kept.ident).then_inc(new_turned, 1)
                pe.wait_ge(new_copied, g + 2)
                if g >= 2:
                    pe.wait_ge(out_done, g - 1)
                for j in range(items):
                    b, kv = divmod(j, heads)
                    product(b, kv, v_new[:, b, kv * DH:(kv + 1) * DH], pT_new, j == 0, False)
                with chunks(pe, U) as i:
                    for u in range(U):
                        n = i * U + u + g * nch
                        pe.wait_ge(probs, n + 1)
                        pe.wait_ge(pT_copied, n + 3 - U)
                        for p in range(PPC):
                            last = pe.transpose(qp[u][:, p, :], prob[u][:, p * P:(p + 1) * P], kept.ident)
                        last.then_inc(probs_turned, 1)
                    for u in range(U):
                        n = i * U + u + g * nch
                        pe.wait_ge(pT_copied, n + 3)
                        for b in range(per):
                            pe.wait_ge(v_in[b], n * 64 + 64)
                            for p in range(PPC):
                                for kv in range(heads):
                                    last = product(b, kv, v_rows[b][:, p, kv * DH:(kv + 1) * DH], pT[u][:, p, :], False, False)
                            last.then_inc(v_used, 1)
                if not stick:
                    pe.wait_ge(rcp_done, g + 1)
                    pe.matmul(out[:, 1, :], kept.ones[:], diag[:], start=True, stop=True, skip_group_check=True).then_inc(rcp_spread, 1)

            for kind, g in order:
                (keys if kind == "k" else values)(g)

        @block.scalar
        def _(act):
            act.preload_act_table_set("natural_log_exp_and_others")
            act.nop().then_inc(kT_copied, 2)
            if stick:
                act.nop().then_inc(logits_out, 1)
                act.nop().then_inc(new_out, 1)

            def keys(g):
                with chunks(act) as c:
                    n = c + g * nch
                    for j in range(items):
                        act.wait_ge(k_turned, n * items + j + 1 + items)
                        act.wait_ge(scored, n * items + j + 1)
                        act.copy(kT[j % 2][:], tp[j % 2][:]).then_inc(kT_copied, 1)
                    if stick:
                        act.wait_ge(scored, (n + 1) * items + 2)
                        act.copy(logits[g % 2][:, bass.ds(c * CH, CH)], sc[:]).then_inc(logits_out, 1)
                if stick:
                    act.wait_ge(new_scored, g + 1)
                    act.copy(logits[g % 2][:, past:past + NT], sc_new[:]).then_inc(new_out, 1)
                    if g == 1:
                        for gg in range(groups):
                            if gg == 0:
                                act.wait_ge(logits_out, 1 + 2 * nch)
                                act.wait_ge(new_out, 1 + groups)
                            else:
                                act.wait_ge(soft_dve, 5)
                            z = logits[gg % 2][:]
                            act.activation(soft[:], z, ACT.Abs).then_inc(soft_act, 1)
                            act.wait_ge(soft_act, 3 * gg + 1)
                            act.activation(soft[:], soft[:], ACT.Exp, scale=-1.0).then_inc(soft_act, 1)
                            act.wait_ge(soft_act, 3 * gg + 2)
                            act.activation(soft[:], soft[:], ACT.Ln, bias=1.0).then_inc(soft_act, 1)

            def values(g):
                act.wait_ge(zeroed, 2)
                if not stick:
                    act.wait_ge(max_done, g + 1)
                else:
                    act.wait_ge(soft_dve, 5 * g + 5)
                if g:
                    act.wait_ge(new_turned, g)
                kw = {} if stick else dict(bias=nmax[:, g:g + 1])
                act.activation(prob_new[:, 0:NT], logits[g % 2][:, past:past + NT], ACT.Exp,
                               **(kw if stick else dict(kw, accum_out=sums[:, g, nch:nch + 1]))).then_inc(new_prob if not stick else step, 1)
                with chunks(act, U) as i:
                    for u in range(U):
                        c = i * U + u
                        n = c + g * nch
                        act.wait_ge(probs_turned, n + 3 - U)
                        if not stick:
                            kw["accum_out"] = sums[:, g, bass.ds(c, 1)] if nch > 1 else sums[:, g, 0:1]
                        act.activation(prob[u][:], logits[g % 2][:, bass.ds(c * CH, CH)], ACT.Exp, **kw).then_inc(probs, 1)
                if not stick:
                    act.wait_ge(rcp_spread, g + 1)
                    act.copy(rcpT[:], ov[g % 2][:, 1, :]).then_inc(rcp_copied, 1)

            for kind, g in order:
                (keys if kind == "k" else values)(g)

        @block.vector
        def _(dve):
            if not stick:
                dve.nop().then_inc(logits_out, 1)
                dve.nop().then_inc(new_out, 1)
            dve.nop().then_inc(pT_copied, 2)
            dve.nop().then_inc(new_copied, 1)

            if stick:
                for i in range(TOPK_S // 8):
                    dve.max(top8[:], kept.scores[:]).then_inc(top_step, 1)
                    dve.wait_ge(top_step, i * 2 + 1)
                    dve.match_replace(kept.scores[:], top8[:], kept.scores[:], GONE).then_inc(top_step, 1)
                    dve.wait_ge(top_step, i * 2 + 2)
                dve.tensor_scalar(kept.drop[:], kept.scores[:], GONE / 2, NEG, ALU.is_gt, ALU.mult).then_inc(dropped, 1)

            def keys(g):
                if stick:
                    return
                if g == 0:
                    dve.wait_ge(bias_in, 16 * per * NT)
                    if mask_last is not None:
                        lo, col = mask_last
                        dve.tensor_tensor(bias[:, lo:lo + NT], bias[:, lo:lo + NT], kept.consts[:, col:col + NT], ALU.add).then_inc(step, 1)
                        dve.wait_ge(step, 1)
                    dve.tensor_tensor(bias[:, past:], bias[:, past:], kept.consts[:, C_NM:C_NM + NT], ALU.add).then_inc(zeroed, 1)
                    dve.wait_ge(zeroed, 3)
                to = logits[g % 2]
                with chunks(dve) as c:
                    n = c + g * nch
                    at = bass.ds(c * CH, CH)
                    dve.wait_ge(scored, (n + 1) * items + 2)
                    dve.tensor_tensor(to[:, at], sc[:], bias[:, at], ALU.add).then_inc(logits_out, 1)
                    dve.wait_ge(logits_out, n + 2)
                    dve.tensor_reduce(maxes[:, bass.ds(c, 1)], to[:, at], AX.X, ALU.max).then_inc(maxed, 1)
                dve.wait_ge(new_scored, g + 1)
                dve.tensor_tensor(to[:, past:], sc_new[:], bias[:, past:], ALU.add).then_inc(new_out, 1)
                dve.wait_ge(new_out, g + 2)
                dve.tensor_reduce(maxes[:, nch:nch + 1], to[:, past:], AX.X, ALU.max).then_inc(maxed, 1)
                dve.wait_ge(maxed, (g + 1) * (nch + 1))
                dve.tensor_reduce(nmax[:, g:g + 1], maxes[:], AX.X, ALU.max, negate=True).then_inc(max_done, 1)
                dve.wait_ge(max_done, g + 1)

            def soften(g):
                z = logits[g % 2]
                strict = kept.consts[:, C_STRICT:C_STRICT + NT]
                dve.wait_ge(soft_act, 3 * g + 3)
                dve.scalar_tensor_tensor(soft[:], z[:], 0.0, soft[:], ALU.max, ALU.add).then_inc(soft_dve, 1)
                dve.wait_ge(soft_dve, 5 * g + 1)
                dve.tensor_tensor(soft[:, past:], soft[:, past:], strict, ALU.mult).then_inc(soft_dve, 1)
                dve.wait_ge(soft_dve, 5 * g + 2)
                dve.tensor_tensor_scan(soft[:, ::-1], soft[:, ::-1], soft[:, ::-1], 0.0, ALU.add, ALU.bypass).then_inc(soft_dve, 1)
                dve.wait_ge(soft_dve, 5 * g + 3)
                dve.tensor_tensor(z[:], z[:], soft[:], ALU.subtract).then_inc(soft_dve, 1)
                dve.wait_ge(soft_dve, 5 * g + 4)
                dve.nop().then_inc(soft_dve, 1)

            def values(g):
                if stick:
                    soften(g)
                    dve.wait_ge(step, g + 1)
                    dve.tensor_tensor(prob_new[:, 0:NT], prob_new[:, 0:NT], kept.consts[:, C_STRICT:C_STRICT + NT], ALU.mult).then_inc(new_prob, 1)
                dve.wait_ge(new_turned, g + 1)
                if g:
                    dve.wait_ge(v_used, 2 * per + g * nch * per)
                dve.tensor_copy(pT_new[:], tp[0][0:NT, 0:P]).then_inc(new_copied, 1)
                with chunks(dve, U) as i:
                    for u in range(U):
                        n = i * U + u + g * nch
                        dve.wait_ge(probs_turned, n + 3)
                        dve.wait_ge(v_used, (n + 3 - U) * per)
                        dve.tensor_copy(pT[u][:], qp[u][:]).then_inc(pT_copied, 1)
                if stick:
                    dve.wait_ge(v_used, 2 * per + (g + 1) * nch * per)
                    for b in range(per):
                        at = (g * per + b) * NT
                        ins = dve.tensor_copy(kept.oTs[:, head0:head0 + 4, at:at + NT],
                                              ov[g % 2][:, 0, b * 32:(b + 1) * 32].rearrange("p (h t) -> p h t", t=NT))
                    ins.then_inc(out_done, 1)
                    return
                dve.wait_ge(probs, (g + 1) * nch)
                dve.wait_ge(new_prob, g + 1)
                dve.tensor_reduce(rcp[:, g:g + 1], sums[:, g, :], AX.X, ALU.add).then_inc(step, 1)
                k = (1 if mask_last is not None else 0) + 4 * g
                dve.wait_ge(step, k + 1)
                dve.tensor_scalar(rcp[:, g:g + 1], rcp[:, g:g + 1], 1e-30, None, ALU.max).then_inc(step, 1)
                dve.wait_ge(step, k + 2)
                dve.reciprocal(rcp[:, g:g + 1], rcp[:, g:g + 1]).then_inc(step, 1)
                dve.wait_ge(step, k + 3)
                if gate is not None:
                    dve.tensor_tensor(rcp[:, g:g + 1], rcp[:, g:g + 1], kept.gates[:, g, gate:gate + 1], ALU.mult).then_inc(step, 1)
                else:
                    dve.nop().then_inc(step, 1)
                dve.wait_ge(step, k + 4)
                if g:
                    dve.wait_ge(rcp_spread, g)
                dve.tensor_scalar(diag[:], kept.ident, rcp[:, g:g + 1], None, ALU.mult).then_inc(rcp_done, 1)
                dve.wait_ge(rcp_copied, g + 1)
                dve.wait_ge(v_used, 2 * per + (g + 1) * nch * per)
                if add:
                    if g:
                        dve.wait_ge(out_done, g)
                    used = lambda x: x.rearrange("p (b r) -> p b r", b=per)[:, :, 0:48]
                    dve.tensor_tensor(scaled[:], used(ov[g % 2][:, 0, :]), used(rcpT[:]), ALU.mult).then_inc(added, 1)
                    dve.wait_ge(added, g + 1)
                for b in range(per):
                    at = (g * per + b) * NT
                    to = kept.oTs[:, head0:head0 + 6, at:at + NT]
                    r = slice(b * stride, b * stride + 48)
                    view = lambda x: x.rearrange("p (h t) -> p h t", t=NT)
                    if add:
                        ins = dve.tensor_tensor(to, to, view(scaled[:, b]), ALU.add)
                    else:
                        ins = dve.tensor_tensor(to, view(ov[g % 2][:, 0, r]), view(rcpT[:, r]), ALU.mult)
                ins.then_inc(out_done, 1)

            for kind, g in order:
                (keys if kind == "k" else values)(g)


def stick_breaking(nc, io, kept, keep):
    stream(nc, io, kept, "sb", cache=io.sb_cache, k_col=0, v_col=512, proj_v=SB_V, heads=4, per=4, q=kept.q_sb, k_new=kept.k_sb,
           head0=0, stick=True)


def dsa_sample(nc, io, kept, keep):
    def chosen(g, c, w):
        at = slice(PAST, KEYS) if c is None else bass.ds(c * CH, CH)
        return kept.sel_d[:, g * P:(g + 1) * P], kept.drop[:, at]

    stream(nc, io, kept, "dsa", cache=io.dsa_cache, k_col=0, v_col=256, proj_v=DSA_V, heads=2, per=2, q=kept.q_dsa, k_new=kept.k_dsa,
           add_mask=chosen, bias_rows=0, head0=4)


def cmp_sample(nc, io, kept, keep):
    kept.drop_blk = keep.sb("drop_blk", [P, NSB], BF16)
    with ExitStack() as ctx:
        s = Scope(nc, ctx, "ca")
        bias = s.sb("bias", [P, PAST])
        prob = s.sb("prob", [P, 4, NC])
        gated = s.sb("gated", [P, 4, NC])
        pT = s.sb("pT", [P, 4, P])
        nmax, sums, rcp = s.sb("nmax", [P, 4]), s.sb("sums", [P, 4]), s.sb("rcp", [P, 4])
        imp = s.sb("imp", [P, NSB])
        top8 = s.sb("top8", [P, 8])
        sc = s.ps("sc", [P, 4, NC])
        ip = s.ps("ip", [P, NC])
        tp = s.ps("tp", [P, 4, P])
        ov = s.ps("ov", [P, 4, P])
        zeroed, bias_in, scored, step, exped, normed, gate_done, imp_summed, turned, copied, out_summed, out_done = (
            s.sem(n) for n in ("zeroed", "bias_in", "scored", "step", "exped", "normed", "gate_done", "imp_summed", "turned",
                               "copied", "out_summed", "out_done"))
        block = ctx.enter_context(nc.Block())

        @block.gpsimd
        def _(pool):
            pool.memset(bias[:], 0.0).then_inc(zeroed, 1)

        @block.sync
        def _(sp):
            sp.wait_ge(zeroed, 1)
            for b in range(2):
                for t in range(NT):
                    sp.dma_start(bias[b * 64 + t:b * 64 + t + 41:8, :], io.line[6:12, NT - 1 - t:NT - 1 - t + PAST]).then_inc(bias_in, 16)

        @block.tensor
        def _(pe):
            for g in range(4):
                for j in range(4):
                    b, kv = divmod(j, 2)
                    last = pe.matmul(sc[b * 64:b * 64 + 64, g, :], kept.q_nsa[:, 2 * g + b, kv, :], kept.cmp_k[:, 2 * g + b, kv, :],
                                     start=(kv == 0), stop=(kv == 1), skip_group_check=True, tile_position=(0, b * 64))
            last.then_inc(scored, 1)
            pe.wait_ge(normed, 1)
            for g in range(4):
                last = pe.matmul(ip[:], kept.consts[:, C_SELG + g * P:C_SELG + (g + 1) * P], prob[:, g, :], start=(g == 0), stop=(g == 3))
            last.then_inc(imp_summed, 1)
            pe.wait_ge(gate_done, 1)
            for g in range(4):
                last = pe.transpose(tp[:, g, :], gated[:, g, :], kept.ident)
            last.then_inc(turned, 1)
            pe.wait_ge(copied, 1)
            for g in range(4):
                for j in range(4):
                    b, kv = divmod(j, 2)
                    r = b * 64 + kv * 24
                    last = pe.matmul(ov[:, g, r:r + 24], kept.cmp_v[:, 2 * g + b, kv, :], pT[:, g, r:r + 24], start=True, stop=True, skip_group_check=True)
            last.then_inc(out_summed, 1)

        @block.scalar
        def _(act):
            act.wait_ge(step, 2)
            for g in range(4):
                last = act.activation(prob[:, g, :], prob[:, g, :], ACT.Exp, bias=nmax[:, g:g + 1], accum_out=sums[:, g:g + 1])
            last.then_inc(exped, 1)
            act.wait_ge(turned, 1)
            act.copy(pT[:], tp[:]).then_inc(copied, 1)

        @block.vector
        def _(dve):
            dve.wait_ge(bias_in, 16 * 16)
            dve.wait_ge(scored, 1)
            ends = bias[:, CMPB - 1::CMPB].unsqueeze(1).to_broadcast([P, 4, NC])
            dve.tensor_tensor(prob[:], sc[:], ends, ALU.add).then_inc(step, 1)
            dve.wait_ge(step, 1)
            dve.tensor_reduce(nmax[:], prob[:], AX.X, ALU.max, negate=True).then_inc(step, 1)
            dve.wait_ge(exped, 1)
            dve.tensor_scalar(rcp[:], sums[:], 1e-30, None, ALU.max).then_inc(step, 1)
            dve.wait_ge(step, 3)
            dve.reciprocal(rcp[:], rcp[:]).then_inc(step, 1)
            dve.wait_ge(step, 4)
            dve.tensor_tensor(prob[:], prob[:], rcp[:].unsqueeze(2).to_broadcast([P, 4, NC]), ALU.mult).then_inc(normed, 1)
            dve.wait_ge(normed, 1)
            dve.tensor_tensor(gated[:], prob[:], kept.gates[:, :, 0:1].to_broadcast([P, 4, NC]), ALU.mult).then_inc(gate_done, 1)
            dve.memset(imp[:], 1e4).then_inc(step, 1)
            dve.wait_ge(imp_summed, 1)
            dve.wait_ge(step, 5)
            dve.tensor_reduce(imp[:, 1:NSB - 2], ip[:].rearrange("p (n a) -> p n a", a=2)[:, 1:NSB - 2, :], AX.X, ALU.add).then_inc(step, 1)
            for n in range(SLC_TOPN // 8):
                dve.wait_ge(step, 6 + 2 * n)
                dve.max(top8[:], imp[:]).then_inc(step, 1)
                dve.wait_ge(step, 7 + 2 * n)
                dve.match_replace(imp[:], top8[:], imp[:], GONE).then_inc(step, 1)
            dve.wait_ge(step, 10)
            dve.tensor_scalar(kept.drop_blk[:], imp[:], GONE / 2, NEG, ALU.is_gt, ALU.mult).then_inc(step, 1)
            dve.wait_ge(out_summed, 1)
            for b in range(NB):
                r = b % 2 * 64
                last = dve.tensor_copy(kept.oTs[:, 10:16, b * NT:(b + 1) * NT], ov[:, b // 2, r:r + 48].rearrange("p (h t) -> p h t", t=NT))
            last.then_inc(out_done, 1)


def slc_sample(nc, io, kept, keep):
    def chosen(g, c, w):
        blocks = kept.drop_blk[:, NSB - 1:NSB] if c is None else kept.drop_blk[:, bass.ds(c * 8, 8)]
        rhs = blocks.to_broadcast([P, NT]) if c is None else blocks.unsqueeze(2).to_broadcast([P, 8, SLCB])
        return kept.sel_e[:, g * P:(g + 1) * P], rhs

    stream(nc, io, kept, "slc", cache=io.nsa_cache, k_col=512, v_col=768, proj_v=NSA_VS, heads=2, per=2, q=kept.q_nsa, k_new=kept.k_slc,
           add_mask=chosen, bias_rows=6, head0=10, gate=1, add=True)


def win_sample(nc, io, kept, keep):
    stream(nc, io, kept, "win", cache=None, state=io.win_state, k_col=0, v_col=256, proj_v=NSA_VW, heads=2, per=2, q=kept.q_nsa,
           k_new=kept.k_win, bias_rows=6, bias_first=PAST - WIN, mask_last=(0, C_WM), head0=10, gate=2, add=True)


def prompt_prepare(nc, io, kept, keep):
    kept.qT = keep.sb("qT", [P, 16, SEQ])
    kept.kT = keep.sb("kT", [P, 10, SEQ])
    kept.v = keep.sb("v", [P, 4, 10 * DH])
    kept.bias = keep.sb("bias", [P, HB, XW])
    kept.dropp = keep.sb("dropp", [P, 4, SEQ], BF16)
    kept.pgates = keep.sb("pgates", [P, 4, 18])
    kept.pmask = keep.sb("pmask", [P, C_END - C_KEPT])
    with ExitStack() as ctx:
        s = Scope(nc, ctx, "pp")
        rows = [s.sb(f"rows{i}", [P, 4, 2 * DH]) for i in range(3)]
        iq = s.sb("iq", [64, 4, SEQ])
        ik = s.sb("ik", [64, SEQ])
        iw = s.sb("iw", [P, 4, 4])
        relu = [s.sb(f"relu{i}", [P, SEQ]) for i in range(2)]
        score = s.sb("score", [P, 4, SEQ])
        top8 = s.sb("top8", [P, 3, 8])
        tp = [s.ps(f"tp{i}", [P, SEQ]) for i in range(4)]
        sc = [s.ps(f"sc{i}", [P, SEQ]) for i in range(2)]
        pairs = [SB_Q, SB_Q + 256] + [DSA_Q + 256 * i for i in range(3)] + [NSA_Q + 256 * i for i in range(3)]
        n_q = len(pairs)
        pairs += [SB_K, SB_K + 256, DSA_K, NSA_KS, NSA_KW, IDX_Q, IDX_K]
        n_full = len(pairs) - 2
        rows_in = [s.sem(f"rows_in{i}") for i in range(3)]
        v_in, bias_in, small_in, mask_in = s.sem("v_in"), s.sem("bias_in"), s.sem("small_in"), s.sem("mask_in")
        turned, copied_a, copied_d, gated, biased = s.sem("turned"), s.sem("copied_a"), s.sem("copied_d"), s.sem("gated"), s.sem("biased")
        scored, rectified, weighted, top_step, dropped, idx_copied = (s.sem("scored"), s.sem("rectified"), s.sem("weighted"), s.sem("top_step"), s.sem("dropped"), s.sem("idx_copied"))
        block = ctx.enter_context(nc.Block())
        n_items = 2 * len(pairs) - 1
        idx_units = [(i, h) for i in range(1, 4) for h in range(4)]

        @block.sync
        def _(sp):
            for i, col in enumerate(pairs):
                if i >= 3:
                    sp.wait_ge(turned, 2 * (i - 2))
                width = 2 * DH if i < len(pairs) - 1 else DH
                sp.dma_start(rows[i % 3][:, :, 0:width], io.proj[0:SEQ, col:col + width].rearrange("(m p) n -> p m n", p=P)).then_inc(rows_in[i % 3], 16)
            sp.wait_ge(v_in, 16 * 4)
            sp.wait_ge(small_in, 32)

        @block.gpsimd
        def _(pool):
            with nc.allow_non_contiguous_dma(reason="a few numbers per row"):
                pool.dma_start(iw[:], io.proj[0:SEQ, IDX_W:IDX_W + 4].rearrange("(m p) n -> p m n", p=P)).then_inc(small_in, 16)
                pool.dma_start(kept.pgates[:], io.proj[0:SEQ, NSA_BG:NSA_BG + 18].rearrange("(m p) n -> p m n", p=P)).then_inc(small_in, 16)

        @block.scalar
        def _(act):
            act.preload_act_table_set("natural_log_exp_and_others")
            act.dma_start(kept.pmask[:], io.consts[:, C_KEPT:C_END]).then_inc(mask_in, 16)
            src = bass.AP(io.lines.tensor, P - 1, [[HB * XL - 1, P], [XL, HB], [1, XW]])
            act.dma_start(kept.bias[:], src).then_inc(bias_in, 16)
            for to, col, n in ((0, SB_V, 4), (4, DSA_V, 2), (6, NSA_VS, 2), (8, NSA_VW, 2)):
                act.dma_start(kept.v[:, :, to * DH:(to + n) * DH], io.proj[0:SEQ, col:col + n * DH].rearrange("(m p) n -> p m n", p=P)).then_inc(v_in, 16)
            for n in range(1, 2 * n_full, 2):
                act.wait_ge(turned, n + 1)
                if n // 2 < n_q:
                    act.activation(kept.qT[:, n, :], tp[n % 4][:], ACT.Copy, scale=SCALE).then_inc(copied_a, 1)
                else:
                    act.copy(kept.kT[:, n - 2 * n_q, :], tp[n % 4][:]).then_inc(copied_a, 1)
            act.wait_ge(small_in, 32)
            act.activation(kept.pgates[:], kept.pgates[:], ACT.Exp, scale=-1.0).then_inc(gated, 1)
            for u in range(len(idx_units)):
                i, h = idx_units[u]
                w = (i + 1) * P
                act.wait_ge(scored, u + 1)
                if u >= 2:
                    act.wait_ge(weighted, u - 1)
                act.activation(relu[u % 2][:, 0:w], sc[u % 2][:, 0:w], ACT.Relu).then_inc(rectified, 1)

        @block.tensor
        def _(pe):
            for n in range(n_items):
                i, j = divmod(n, 2)
                if j == 0:
                    pe.wait_ge(rows_in[i % 3], 16 * (i // 3 + 1))
                if n >= 4:
                    pe.wait_ge(copied_a if n % 2 else copied_d, (n - 4) // 2 + 1)
                for m in range(4):
                    last = pe.transpose(tp[n % 4][:, m * P:(m + 1) * P], rows[i % 3][:, m, j * DH:(j + 1) * DH], kept.ident)
                last.then_inc(turned, 1)
            pe.wait_ge(idx_copied, 5)
            for u, (i, h) in enumerate(idx_units):
                w = (i + 1) * P
                if u >= 2:
                    pe.wait_ge(rectified, u - 1)
                pe.matmul(sc[u % 2][:, 0:w], iq[:, h, i * P:(i + 1) * P], ik[:, 0:w], start=True, stop=True).then_inc(scored, 1)

        @block.vector
        def _(dve):
            for n in range(0, 2 * n_full, 2):
                dve.wait_ge(turned, n + 1)
                if n // 2 < n_q:
                    dve.tensor_scalar(kept.qT[:, n, :], tp[n % 4][:], SCALE, None, ALU.mult).then_inc(copied_d, 1)
                else:
                    dve.tensor_copy(kept.kT[:, n - 2 * n_q, :], tp[n % 4][:]).then_inc(copied_d, 1)
            for n in range(2 * n_full, n_items):
                j = n - 2 * n_full
                dve.wait_ge(turned, n + 1)
                for half in range(2 if j < 2 else 1):
                    to = iq[:, 2 * j + half, :] if j < 2 else ik[:]
                    dve.tensor_copy(to, tp[n % 4][64 * half:64 * half + 64, :]).then_inc(idx_copied, 1)
            dve.wait_ge(mask_in, 16)
            dve.wait_ge(small_in, 32)
            pm = kept.pmask[:, C_PM - C_KEPT:C_PM - C_KEPT + XW]
            for u, (i, h) in enumerate(idx_units):
                w = (i + 1) * P
                dve.wait_ge(rectified, u + 1)
                if h:
                    dve.wait_ge(weighted, u)
                before = score[:, i, 0:w] if h else pm[:, SEQ - i * P:SEQ - i * P + w]
                dve.scalar_tensor_tensor(score[:, i, 0:w], relu[u % 2][:, 0:w], iw[:, i, h:h + 1], before, ALU.mult, ALU.add).then_inc(weighted, 1)
            dve.wait_ge(gated, 1)
            dve.tensor_scalar(kept.pgates[:], kept.pgates[:], 1.0, None, ALU.add).then_inc(gated, 1)
            dve.wait_ge(gated, 2)
            dve.reciprocal(kept.pgates[:], kept.pgates[:]).then_inc(gated, 1)
            dve.wait_ge(bias_in, 16)
            dve.tensor_tensor(kept.bias[:], kept.bias[:], pm.unsqueeze(1).to_broadcast([P, HB, XW]), ALU.add).then_inc(biased, 1)
            dve.wait_ge(weighted, len(idx_units))
            for r in range(TOPK_P // 8):
                for i in range(1, 4):
                    dve.max(top8[:, i - 1, :], score[:, i, 0:(i + 1) * P]).then_inc(top_step, 1)
                for i in range(1, 4):
                    dve.wait_ge(top_step, r * 6 + i)
                    dve.match_replace(score[:, i, 0:(i + 1) * P], top8[:, i - 1, :], score[:, i, 0:(i + 1) * P], GONE).then_inc(top_step, 1)
                dve.wait_ge(top_step, r * 6 + 6)
            for i in range(1, 4):
                last = dve.tensor_scalar(kept.dropp[:, i, 0:(i + 1) * P], score[:, i, 0:(i + 1) * P], GONE / 2, NEG, ALU.is_gt, ALU.mult)
            last.then_inc(dropped, 1)


class Unit:

    def __init__(self, kind, out, tile, q, k, v, bias, gate, first, last):
        self.kind, self.out, self.tile, self.q, self.k, self.v = kind, out, tile, q, k, v
        self.bias, self.gate, self.first, self.last = bias, gate, first, last
        self.off = SEQ - tile * P
        self.w = (tile + 1) * P
        self.blocks = self.w // CMPB
        self.u = None


class Links:

    def __init__(self, sem):
        self.sem, self.n = sem, 0

    def step(self, ins):
        self.n += 1
        ins.then_inc(self.sem, 1)
        return self.n


def prompt_attention(nc, io, kept, keep):
    units = []
    for h in range(4):
        for i in range(4):
            units.append(Unit("stick", h, i, h, h, h, None, None, True, True))
    n_stick = len(units)
    for h in range(6):
        for i in range(4):
            units.append(Unit("dsa", 4 + h, i, 4 + h, 4 + h // 3, 4 + h // 3, h, None, True, True))
    for h in range(6):
        for i in range(4):
            units.append(Unit("slc", 10 + h, i, 10 + h, 6 + h // 3, 6 + h // 3, 6 + h, 6 + h, True, False))
            units.append(Unit("win", 10 + h, i, 10 + h, 8 + h // 3, 8 + h // 3, 6 + h, 12 + h, False, False))
            units.append(Unit("cmp", 10 + h, i, 10 + h, h // 3, h // 3, 6 + h, h, False, True))
    N = len(units)
    for u, x in enumerate(units):
        x.u = u
    outs = [x.u for x in units if x.last and x.tile == 3]

    with ExitStack() as ctx:
        s = Scope(nc, ctx, "pa")
        L = [s.sb(f"logits{i}", [P, XW]) for i in range(4)]
        soft = s.sb("soft", [P, SEQ])
        pT = [s.sb(f"pT{i}", [P, 4, P]) for i in range(2)]
        nmax, sums, rcp = s.sb("nmax", [P, N]), s.sb("sums", [P, N]), s.sb("rcp", [P, N])
        sc = [s.ps(f"sc{i}", [P, SEQ]) for i in range(2)]
        tp = [s.ps(f"tp{i}", [P, 4, P]) for i in range(2)]
        ov = [s.ps(f"ov{i}", [P, 4, P]) for i in range(2)]
        cleared, scored, added, padded, maxed, exped, rcp_ready, ready_stick, ready = (
            s.sem(n) for n in ("cleared", "scored", "added", "padded", "maxed", "exped", "rcp_ready", "ready_stick", "ready"))
        turned, copied, multiplied, out_done = s.sem("turned"), [s.sem("copied_even"), s.sem("copied_odd")], s.sem("multiplied"), s.sem("out_done")
        soft_act, soft_dve, small = s.sem("soft_act"), s.sem("soft_dve"), s.sem("small")
        block = ctx.enter_context(nc.Block())
        wins = [x.u for x in units if x.kind == "win"]

        def view(x):
            if x.kind == "cmp":
                return L[x.u % 4][:, 0:x.blocks]
            return L[x.u % 4][:, x.off:x.off + x.w]

        def all_of(x):
            return L[x.u % 4][:, 0:XW] if x.kind == "win" else view(x)

        @block.tensor
        def _(pe):
            def score(x):
                if x.u >= 2:
                    pe.wait_ge(added, x.u - 1)
                q = kept.qT[:, x.q, x.tile * P:(x.tile + 1) * P]
                if x.kind == "cmp":
                    pe.matmul(sc[x.u % 2][:, 0:x.blocks], q, kept.cmp_kp[:, x.k, 0:x.blocks], start=True, stop=True).then_inc(scored, 1)
                    return
                dropping = x.kind == "dsa" and x.tile > 0
                if dropping:
                    pe.matmul(sc[x.u % 2][:, 0:x.w], kept.ident_b[:], kept.dropp[:, x.tile, 0:x.w], start=True, stop=False)
                pe.matmul(sc[x.u % 2][:, 0:x.w], q, kept.kT[:, x.k, 0:x.w], start=not dropping, stop=True).then_inc(scored, 1)

            def turn(x):
                if x.kind == "stick":
                    pe.wait_ge(ready_stick, x.u + 1)
                else:
                    pe.wait_ge(ready, x.u - n_stick + 1)
                if x.u >= 2:
                    pe.wait_ge(copied[x.u % 2], x.u // 2)
                if x.kind == "cmp":
                    last = pe.transpose(tp[x.u % 2][:, 0, :], L[x.u % 4][:, 0:P], kept.ident)
                else:
                    for j in range(x.tile + 1):
                        last = pe.transpose(tp[x.u % 2][:, j, :], view(x)[:, j * P:(j + 1) * P], kept.ident)
                last.then_inc(turned, 1)

            def product(x):
                pe.wait_ge(copied[x.u % 2], x.u // 2 + 1)
                if x.tile == 0 and x.first and x.out >= 2:
                    pe.wait_ge(out_done, x.out - 1)
                to = ov[x.out % 2][:, x.tile, :]
                if x.kind == "cmp":
                    last = pe.matmul(to, kept.cmp_vp[0:x.blocks, x.v, :], pT[x.u % 2][0:x.blocks, 0, :], start=False, stop=True, skip_group_check=True)
                else:
                    for j in range(x.tile + 1):
                        last = pe.matmul(to, kept.v[:, j, x.v * DH:(x.v + 1) * DH], pT[x.u % 2][:, j, :],
                                         start=(x.first and j == 0), stop=(x.last and j == x.tile), skip_group_check=True)
                last.then_inc(multiplied, 1)

            pe.wait_ge(cleared, 4)
            for u in range(N + 3):
                if u < N:
                    score(units[u])
                if 2 <= u < N + 2:
                    turn(units[u - 2])
                if u >= 3:
                    product(units[u - 3])

        def copy(eng, x):
            eng.wait_ge(turned, x.u + 1)
            if x.u >= 2:
                eng.wait_ge(multiplied, x.u - 1)
            do = eng.copy if x.u % 2 else eng.tensor_copy
            n = 1 if x.kind == "cmp" else x.tile + 1
            rows = x.blocks if x.kind == "cmp" else P
            do(pT[x.u % 2][0:rows, 0:n, :], tp[x.u % 2][0:rows, 0:n, :]).then_inc(copied[x.u % 2], 1)

        @block.gpsimd
        def _(pool):
            for i in range(4):
                pool.memset(L[i][:], 0.0).then_inc(cleared, 1)
            pool.wait_ge(cleared, 4)

            def normalise(x):
                if x.kind == "stick":
                    return
                pool.wait_ge(rcp_ready, x.u - n_stick + 1)
                v = view(x)
                pool.tensor_scalar(v, v, rcp[:, x.u:x.u + 1], 1.0, ALU.mult, ALU.mult).then_inc(ready, 1)

            for u in range(N + 1):
                if u < N and units[u].kind == "win":
                    pool.wait_ge(turned, u - 3)
                    x = units[u]
                    if x.off:
                        pool.tensor_copy(L[u % 4][:, 0:x.off], kept.bias[:, x.bias, 0:x.off]).then_inc(padded, 1)
                if u:
                    normalise(units[u - 1])

        @block.scalar
        def _(act):
            act.preload_act_table_set("natural_log_exp_and_others")
            chain = Links(soft_act)

            def exp(x):
                if x.kind == "stick":
                    act.wait_ge(scored, x.u + 1)
                    if x.u:
                        act.wait_ge(soft_dve, 4 * x.u)
                    t = soft[:, 0:x.w]
                    act.wait_ge(soft_act, chain.step(act.activation(t, sc[x.u % 2][:, 0:x.w], ACT.Abs)))
                    act.wait_ge(soft_act, chain.step(act.activation(t, t, ACT.Exp, scale=-1.0)))
                    chain.step(act.activation(t, t, ACT.Ln, bias=1.0))
                    return
                act.wait_ge(maxed, x.u - n_stick + 1)
                act.activation(all_of(x), all_of(x), ACT.Exp, bias=nmax[:, x.u:x.u + 1], accum_out=sums[:, x.u:x.u + 1]).then_inc(exped, 1)

            def exp_stick(x):
                act.wait_ge(soft_dve, 4 * x.u + 4)
                act.activation(view(x), view(x), ACT.Exp).then_inc(exped, 1)

            for u in range(N + 3):
                if 1 <= u <= n_stick:
                    exp_stick(units[u - 1])
                if u < N:
                    exp(units[u])
                if 2 <= u < N + 2 and u % 2:
                    copy(act, units[u - 2])

        @block.vector
        def _(dve):
            chain = Links(small)
            tri = kept.pmask[:, C_TRI - C_KEPT:C_TRI - C_KEPT + P]
            dve.wait_ge(cleared, 4)

            def add(x):
                if x.u >= 4:
                    dve.wait_ge(turned, x.u - 3)
                v = view(x)
                if x.kind == "stick":
                    t = soft[:, 0:x.w]
                    z = sc[x.u % 2][:, 0:x.w]
                    dve.wait_ge(soft_act, 3 * x.u + 3)
                    dve.scalar_tensor_tensor(t, z, 0.0, t, ALU.max, ALU.add).then_inc(soft_dve, 1)
                    dve.wait_ge(soft_dve, 4 * x.u + 1)
                    d = soft[:, x.w - P:x.w]
                    dve.tensor_tensor(d, d, tri, ALU.mult).then_inc(soft_dve, 1)
                    dve.wait_ge(soft_dve, 4 * x.u + 2)
                    dve.tensor_tensor_scan(t[:, ::-1], t[:, ::-1], t[:, ::-1], 0.0, ALU.add, ALU.bypass).then_inc(soft_dve, 1)
                    dve.wait_ge(soft_dve, 4 * x.u + 3)
                    dve.tensor_tensor(v, z, t, ALU.subtract).then_inc(soft_dve, 1)
                    dve.wait_ge(soft_dve, 4 * x.u + 4)
                    dve.nop().then_inc(added, 1)
                    return
                dve.wait_ge(scored, x.u + 1)
                if x.kind == "cmp":
                    b = kept.bias[:, x.bias, x.off + CMPB - 1:x.off + x.w:CMPB]
                    dve.tensor_tensor(v, sc[x.u % 2][:, 0:x.blocks], b, ALU.add).then_inc(added, 1)
                else:
                    dve.tensor_tensor(v, sc[x.u % 2][:, 0:x.w], kept.bias[:, x.bias, x.off:x.off + x.w], ALU.add).then_inc(added, 1)
                dve.wait_ge(added, x.u + 1)
                if x.kind == "win":
                    dve.wait_ge(padded, wins.index(x.u) + 1)
                dve.tensor_reduce(nmax[:, x.u:x.u + 1], all_of(x), AX.X, ALU.max, negate=True).then_inc(maxed, 1)

            def invert(x):
                dve.wait_ge(exped, x.u + 1)
                if x.kind == "stick":
                    d = view(x)[:, x.w - P:x.w]
                    dve.tensor_tensor(d, d, tri, ALU.mult).then_inc(ready_stick, 1)
                    return
                r = rcp[:, x.u:x.u + 1]
                if x.kind == "cmp" and x.tile == 0:
                    v = view(x)
                    cm = kept.pmask[:, C_CM - C_KEPT:C_CM - C_KEPT + x.blocks]
                    dve.wait_ge(small, chain.step(dve.scalar_tensor_tensor(v, v, 1.0, cm, ALU.mult, ALU.mult, accum_out=sums[:, x.u:x.u + 1])))
                dve.wait_ge(small, chain.step(dve.tensor_scalar(r, sums[:, x.u:x.u + 1], 1e-30, None, ALU.max)))
                if x.gate is None:
                    dve.reciprocal(r, r).then_inc(rcp_ready, 1)
                else:
                    dve.wait_ge(small, chain.step(dve.reciprocal(r, r)))
                    dve.tensor_tensor(r, r, kept.pgates[:, x.tile, x.gate:x.gate + 1], ALU.mult).then_inc(rcp_ready, 1)

            for u in range(N + 4):
                if u < N:
                    add(units[u])
                if 1 <= u <= N:
                    invert(units[u - 1])
                if 2 <= u < N + 2 and u % 2 == 0:
                    copy(dve, units[u - 2])
                if u - 4 in outs:
                    dve.wait_ge(multiplied, u - 3)
                    h = units[u - 4].out
                    dve.tensor_copy(kept.oT[:, h, :].rearrange("p (m t) -> p m t", m=4), ov[h % 2][:]).then_inc(out_done, 1)


def finish(nc, io, kept, keep):
    with ExitStack() as ctx:
        s = Scope(nc, ctx, "fin")
        w = s.sb("w", [P, 16, D])
        gate = s.sb("gate", [P, D])
        sig = s.sb("sig", [P, D])
        gain = s.sb("gain", [P, D])
        x, y = gate, sig
        sq = s.sb("sq", [P, CH])
        ss, rstd = s.sb("ss", [P, 5, 4]), s.sb("rstd", [P, 5])
        tp = [s.ps(f"tp{i}", [P, 4, P]) for i in range(2)]
        yp = [s.ps(f"yp{i}", [P, CH]) for i in range(4)]
        w_in, gain_in, gate_in, x_in = s.sem("w_in"), s.sem("gain_in"), s.sem("gate_in"), s.sem("x_in")
        sig_exp, sig_step, gate_ready, turned, gated = s.sem("sig_exp"), s.sem("sig_step"), s.sem("gate_ready"), s.sem("turned"), s.sem("gated")
        projected, squared, moved, var, rooted, scaled, summed, stored = (
            s.sem(n) for n in ("projected", "squared", "moved", "var", "rooted", "scaled", "summed", "stored"))
        block = ctx.enter_context(nc.Block())
        rows = [P, P, P, P, NS]
        first_rows = [0, P, 2 * P, 3 * P, SEQ]

        def heads_at(m, h, n):
            return kept.oT[:, h:h + n, m * P:(m + 1) * P] if m < 4 else kept.oTs[:, h:h + n, :]

        @block.sync
        def _(sp):
            for m in range(5):
                if m:
                    sp.wait_ge(turned, 4 * m)
                r = slice(first_rows[m], first_rows[m] + rows[m])
                sp.dma_start(gate[0:rows[m], 0:512], io.proj[r, SB_G:SB_G + 512]).then_inc(gate_in, 16)
                sp.dma_start(gate[0:rows[m], 512:1280], io.proj[r, DSA_G:DSA_G + 768]).then_inc(gate_in, 16)
                sp.dma_start(gate[0:rows[m], 1280:2048], io.proj[r, NSA_G:NSA_G + 768]).then_inc(gate_in, 16)
            sp.wait_ge(turned, 20)
            for m in range(5):
                if m:
                    sp.wait_ge(summed, m)
                sp.dma_start(x[0:rows[m], :], io.xp[m * P:(m + 1) * P, :] if m < 4 else io.xs).then_inc(x_in, 16)

        @block.gpsimd
        def _(pool):
            for m in range(5):
                pool.wait_ge(summed, m + 1)
                pool.dma_start(io.y_p[m * P:(m + 1) * P, :] if m < 4 else io.y_s, y[0:rows[m], :]).then_inc(stored, 16)
            pool.wait_ge(stored, 80)

        @block.scalar
        def _(act):
            act.preload_act_table_set("natural_log_exp_and_others")
            src = io.w_out.rearrange("(h p) n -> p h n", p=P)
            for c in range(4):
                act.dma_start(w[:, 4 * c:4 * c + 4, :], src[:, 4 * c:4 * c + 4, :]).then_inc(w_in, 16)
            act.dma_start(gain[:], io.norm_post.to_broadcast([P, D])).then_inc(gain_in, 16)
            for m in range(5):
                act.wait_ge(gate_in, 48 * (m + 1))
                if m:
                    act.wait_ge(gate_ready, m)
                act.activation(sig[0:rows[m], :], gate[0:rows[m], :], ACT.Exp, scale=-1.0).then_inc(sig_exp, 1)
            for m in range(5):
                for c in range(4):
                    k = 4 * m + c
                    act.wait_ge(moved, k + 1)
                    if k:
                        act.wait_ge(squared, k)
                    act.activation(sq[0:rows[m], :], y[0:rows[m], c * CH:(c + 1) * CH], ACT.Square, accum_out=ss[0:rows[m], m, c:c + 1]).then_inc(squared, 1)
                act.wait_ge(var, 2 * m + 2)
                r = rstd[0:rows[m], m:m + 1]
                act.activation(r, r, ACT.Ln).then_inc(rooted, 1)
                act.wait_ge(rooted, 2 * m + 1)
                act.activation(r, r, ACT.Exp, scale=-0.5).then_inc(rooted, 1)

        @block.tensor
        def _(pe):
            for m in range(5):
                pe.wait_ge(gate_ready, m + 1)
                for q in range(4):
                    n = 4 * m + q
                    if n >= 2:
                        pe.wait_ge(gated, n - 1)
                    for k in range(4):
                        last = pe.transpose(tp[n % 2][:, k, 0:rows[m]], gate[0:rows[m], (4 * q + k) * P:(4 * q + k + 1) * P], kept.ident[0:rows[m], 0:rows[m]])
                    last.then_inc(turned, 1)
            pe.wait_ge(w_in, 64)
            pe.wait_ge(gated, 20)
            for m in range(5):
                for c in range(4):
                    k = 4 * m + c
                    if k >= 4:
                        pe.wait_ge(moved, k - 3)
                    for h in range(16):
                        last = pe.matmul(yp[k % 4][0:rows[m], :], heads_at(m, h, 1)[:, 0, :], w[:, h, c * CH:(c + 1) * CH], start=(h == 0), stop=(h == 15))
                    last.then_inc(projected, 1)

        @block.vector
        def _(dve):
            for m in range(5):
                r = rows[m]
                dve.wait_ge(sig_exp, m + 1)
                dve.tensor_scalar(sig[0:r, :], sig[0:r, :], 1.0, None, ALU.add).then_inc(sig_step, 1)
                dve.wait_ge(sig_step, 2 * m + 1)
                dve.reciprocal(sig[0:r, :], sig[0:r, :]).then_inc(sig_step, 1)
                dve.wait_ge(sig_step, 2 * m + 2)
                dve.tensor_tensor(gate[0:r, :], gate[0:r, :], sig[0:r, :], ALU.mult).then_inc(gate_ready, 1)
                for q in range(4):
                    n = 4 * m + q
                    dve.wait_ge(turned, n + 1)
                    o = heads_at(m, 4 * q, 4)
                    dve.tensor_tensor(o, o, tp[n % 2][:, :, 0:r], ALU.mult).then_inc(gated, 1)
            dve.wait_ge(gain_in, 16)
            for m in range(5):
                r = rows[m]
                for c in range(4):
                    k = 4 * m + c
                    dve.wait_ge(projected, k + 1)
                    if m:
                        dve.wait_ge(stored, 16 * m)
                    dve.tensor_copy(y[0:r, c * CH:(c + 1) * CH], yp[k % 4][0:r, :]).then_inc(moved, 1)
                dve.wait_ge(squared, 4 * m + 4)
                dve.tensor_reduce(rstd[0:r, m:m + 1], ss[0:r, m, :], AX.X, ALU.add).then_inc(var, 1)
                dve.wait_ge(var, 2 * m + 1)
                dve.tensor_scalar(rstd[0:r, m:m + 1], rstd[0:r, m:m + 1], 1.0 / D, EPS, ALU.mult, ALU.add).then_inc(var, 1)
                dve.wait_ge(rooted, 2 * m + 2)
                dve.wait_ge(moved, 4 * m + 4)
                dve.scalar_tensor_tensor(y[0:r, :], y[0:r, :], rstd[0:r, m:m + 1], gain[0:r, :], ALU.mult, ALU.mult).then_inc(scaled, 1)
                dve.wait_ge(scaled, m + 1)
                dve.wait_ge(x_in, 16 * (m + 1))
                dve.tensor_tensor(y[0:r, :], y[0:r, :], x[0:r, :], ALU.add).then_inc(summed, 1)


def program(nc, io, stages=99):
    with ExitStack() as ctx:
        s = Scope(nc, ctx, "kept")
        kept = Kept()
        kept.consts = s.sb("consts", [P, C_KEPT])
        kept.ident = kept.consts[:, C_ID:C_ID + P]
        kept.sel_e = s.sb("sel_e", [P, 4 * P], BF16)
        kept.sel_d = s.sb("sel_d", [NS, 4 * P], BF16)
        kept.ident_b = s.sb("ident_b", [P, P], BF16)
        kept.ones = s.sb("ones", [P, P])
        kept.pages = s.sb("pages", [1, NB * NPG], I32)
        with nc.sbuf_tensor("hT", [P, KT_IN, TOK], F32) as hT:
            setup_and_norm(nc, io, kept, hT)
            project_in(nc, io, hT)
        kept.cmp_kp = s.sb("cmp_kp", [P, 2, 16])
        kept.cmp_vp = s.sb("cmp_vp", [16, 2, DH])
        kept.oTs = s.sb("oTs", [P, 16, NS])
        with ExitStack() as sample_ctx:
            sample = Scope(nc, sample_ctx, "kept")
            for stage in (prepare, compress, index_scores, stick_breaking, dsa_sample, cmp_sample, slc_sample, win_sample)[:stages]:
                stage(nc, io, kept, sample)
        if stages < 9:
            return
        kept.oT = s.sb("oT", [P, 16, SEQ])
        with ExitStack() as prompt_ctx:
            prompt = Scope(nc, prompt_ctx, "kept")
            prompt_prepare(nc, io, kept, prompt)
            prompt_attention(nc, io, kept, prompt)
        finish(nc, io, kept, s)


_INS = ['x_prompt', 'x_sample', 'cache_sb_kv', 'cache_dsa_kv', 'cache_dsa_idx', 'cache_nsa_kv', 'state_nsa_win', 'page_table',
        'w_in', 'w_out', 'norm_pre', 'norm_post', 'cmp_pe', 'cmp_w1', 'cmp_w2', 'rel_bias']
_OUTS = [(1, SEQ, D), (NB, NT, D), (1, 1, SEQ, 2, 4, DH), (1, NB, NT, 2, 4, DH), (1, 1, SEQ, 2, 2, DH), (1, NB, NT, 2, 2, DH),
         (1, 1, SEQ, 64), (1, NB, NT, 64), (1, 1, SEQ, 4, 2, DH), (1, NB, NT, 4, 2, DH),
         (1, 1, WIN, 2, 2, DH), (1, NB, WIN, 2, 2, DH)]


def describe(nc, shapes):
    def inp(name, shape, dt=F32):
        return nc.dram_tensor(f"in_{name}_dram", shape, dt, kind="ExternalInput").ap()

    a = {n: inp(n, *shapes[n]) for n in _INS}
    io = Io()
    io.consts = inp("constants", [P, C_END])
    io.onehot = inp("onehot", [NBUCK, LINE])
    io.xp = a['x_prompt'].rearrange("a s d -> (a s) d")
    io.xs = a['x_sample'].rearrange("b t d -> (b t) d")
    io.sb_cache = a['cache_sb_kv'].rearrange("l n p a h d -> (l n) p (a h d)")
    io.dsa_cache = a['cache_dsa_kv'].rearrange("l n p a h d -> (l n) p (a h d)")
    io.idx_cache = a['cache_dsa_idx'].rearrange("l n p d -> (l n) p d")
    io.nsa_cache = a['cache_nsa_kv'].rearrange("l n p a h d -> (l n) p (a h d)")
    io.win_state = a['state_nsa_win'].rearrange("l b w a h d -> (l b) w (a h d)")
    io.page_table = a['page_table']
    io.w_in = a['w_in'].rearrange("l k n -> (l k) n")
    io.w_out = a['w_out'].rearrange("l k n -> (l k) n")
    io.norm_pre = a['norm_pre'].rearrange("l d -> (l d)")
    io.norm_post = a['norm_post']
    io.cmp_pe = a['cmp_pe'].rearrange("l r p k d -> (l r) (p k d)")
    io.cmp_w1 = a['cmp_w1'].rearrange("l p k (r d) e -> (l p k) d r e", d=DH)
    io.cmp_w2 = a['cmp_w2'].rearrange("l p k e f -> (l p k) e f")
    io.rel_bias = a['rel_bias']
    io.line = nc.dram_tensor("bias_line", [HB, LINE], F32).ap()
    io.lines = nc.dram_tensor("bias_lines", [P, HB, XL], F32).ap()
    io.proj = nc.dram_tensor("proj", [TOK, DIN], F32).ap()
    outs = [nc.dram_tensor(f"out_{i}_dram", shape, F32, kind="ExternalOutput").ap() for i, shape in enumerate(_OUTS)]
    io.y_p = outs[0].rearrange("a s d -> (a s) d")
    io.y_s = outs[1].rearrange("b t d -> (b t) d")
    io.new_rows = []
    for n, (col, width) in enumerate(((SB_K, 1024), (DSA_K, 512), (IDX_K, 64), (NSA_KC, 1024))):
        flat = "l b s d -> (l b s) d" if width == 64 else "l b s a h d -> (l b s) (a h d)"
        io.new_rows.append((outs[2 + 2 * n].rearrange(flat), outs[3 + 2 * n].rearrange(flat), col, width))
    io.win_p = outs[10].rearrange("l b s a h d -> (l b s) (a h d)")
    io.win_s = outs[11].rearrange("l b s a h d -> (l b) s (a h d)")
    io.n_pool = shapes['cache_sb_kv'][0][1]
    return io


def kernel(**inputs):
    import concourse.bacc as _bacc
    from concourse.bass_utils import run_bass_kernel_spmd as _run

    nc = _bacc.Bacc("TRN2", target_bir_lowering=False, num_devices=1)
    arrays, shapes = {}, {}
    for name in _INS:
        a = np.ascontiguousarray(inputs[name])
        arrays[f"in_{name}_dram"] = a
        shapes[name] = (a.shape, mybir.dt.from_np(a.dtype))
    arrays["in_constants_dram"], arrays["in_onehot_dram"] = constants()
    program(nc, describe(nc, shapes))
    r = _run(nc, [arrays], core_ids=[0])
    return tuple(r.results[0][f"out_{i}_dram"] for i in range(len(_OUTS)))
```

```python
import math
from contextlib import ExitStack

import numpy as np
import concourse.bass as bass
from concourse import mybir

F32 = mybir.dt.float32
BF16 = mybir.dt.bfloat16
I32 = mybir.dt.int32
ALU = mybir.AluOpType
ACT = mybir.ActivationFunctionType
AX = mybir.AxisListType

P = 128
D = 2048
SEQ = 512
NB, NT = 8, 8
NS = NB * NT
PAST = 4096
NPG = PAST // P
KEYS = PAST + NT
DH = 128
NBUCK = 32
HB = 12
WIN = 512
CMPB, SLCB = 32, 64
NC = PAST // CMPB
NSB = 65
TOPK_S, TOPK_P = 256, 128
SLC_TOPN = 16
EPS = 1e-6
NEG = -1e30
GONE = -3e38
SCALE = DH ** -0.5
DIN = 7510
KT_IN = D // P
TOK = SEQ + NS
CH = 512
NCH = PAST // CH
PPC = CH // P

SB_Q, SB_K, SB_V, SB_G = 0, 512, 1024, 1536
DSA_Q, DSA_K, DSA_V, DSA_G = 2048, 2816, 3072, 3328
IDX_Q, IDX_K, IDX_W = 4096, 4352, 4416
NSA_Q, NSA_KC, NSA_KS, NSA_VS, NSA_KW, NSA_VW, NSA_G, NSA_BG = 4420, 5188, 5700, 5956, 6212, 6468, 6724, 7492

DMAX = PAST + NT - 1
LINE = DMAX + P
XW = SEQ + P
XL = XW + P - 1

C_ID = 0
C_NM = C_ID + P
C_STRICT = C_NM + NT
C_WM = C_STRICT + NT
C_SELI = C_WM + NT
C_SELG = C_SELI + 2 * NS
C_KEPT = C_SELG + 4 * P
C_SELE = C_KEPT
C_SELD = C_SELE + 4 * P
C_PM = C_SELD + 4 * P
C_CM = C_PM + XW
C_TRI = C_CM + 4 * 16
C_END = C_TRI + P


def bucket(dist):
    n = np.maximum(dist, 0)
    nf = np.maximum(n, 1).astype(np.float32)
    large = 16 + (np.log(nf / np.float32(16)) / np.float32(math.log(64)) * np.float32(16)).astype(np.int32)
    return np.where(n < 16, n, np.minimum(large, NBUCK - 1))


def constants():
    c = np.zeros((P, C_END), np.float32)
    p = np.arange(P)[:, None]
    c[:, C_ID:C_ID + P] = np.eye(P)
    x = np.arange(XW)[None]
    c[:, C_PM:C_PM + XW] = np.where((p - x + SEQ >= 0) & (p - x + SEQ < WIN), 0, NEG)
    t, j = p % NT, np.arange(NT)[None]
    c[:, C_NM:C_NM + NT] = np.where(j > t, NEG, 0)
    c[:, C_STRICT:C_STRICT + NT] = j < t
    c[:, C_WM:C_WM + NT] = np.where(j <= t, NEG, 0)
    for g in range(2):
        for r in range(P):
            b, _, tt = g * 4 + r // 32, r % 32 // 8, r % 8
            c[r, C_SELI + g * NS + b * NT + tt] = 1
    for g in range(4):
        for r in range(P):
            b2, q = divmod(r, 64)
            if q < 48:
                kv, tt = q // 24, q % 8
                b = 2 * g + b2
                c[r, C_SELG + g * P + b * 16 + kv * 8 + tt] = 1
                c[b * 16 + kv * 8 + tt, C_SELE + g * P + r] = 1
                c[b * NT + tt, C_SELD + g * P + r] = 1
    for i in range(4):
        e = np.arange(16)[None] * CMPB + CMPB - 1
        c[:, C_CM + i * 16:C_CM + i * 16 + 16] = e <= i * P + p
    c[:, C_TRI:C_TRI + P] = np.arange(P)[None] < p
    onehot = np.zeros((NBUCK, LINE), np.float32)
    y = np.arange(LINE)
    onehot[bucket(DMAX - y), y] = 1
    return c, onehot


class Kept:
    pass


class Io:
    pass


class Scope:

    def __init__(self, nc, ctx, tag):
        self.nc, self.ctx, self.tag, self.sems = nc, ctx, tag, []
        ctx.callback(self.clear)

    def sb(self, name, shape, dt=F32):
        return self.ctx.enter_context(self.nc.sbuf_tensor(f"{self.tag}_{name}", shape, dt))

    def ps(self, name, shape, dt=F32):
        return self.ctx.enter_context(self.nc.psum_tensor(f"{self.tag}_{name}", shape, dt))

    def sem(self, name):
        self.sems.append(self.nc.alloc_semaphore(f"{self.tag}_{name}"))
        return self.sems[-1]

    def clear(self):
        if self.sems:
            self.nc.clear_and_free_semaphores(self.sems)
            self.nc.all_engine_barrier()


def setup_and_norm(nc, io, kept, hT):
    with ExitStack() as ctx:
        s = Scope(nc, ctx, "norm")
        x = s.sb("x", [P, 2, D])
        sq = s.sb("sq", [P, D])
        ss = s.sb("ss", [P, 5])
        rstd = s.sb("rstd", [P, 5])
        gcol = s.sb("gcol", [P, KT_IN])
        table = s.sb("table", [NBUCK, HB])
        choices = s.sb("choices", [P, 2, 4 * P])
        onehot = s.sb("onehot", [NBUCK, LINE])
        line = s.sb("line", [HB, LINE])
        tp = [s.ps(f"tp{i}", [P, 4, P]) for i in range(2)]
        lp = [s.ps(f"lp{i}", [HB, CH]) for i in range(2)]
        consts_in, gain_in, table_in, onehot_in = s.sem("consts_in"), s.sem("gain_in"), s.sem("table_in"), s.sem("onehot_in")
        x_in = [s.sem(f"x_in{i}") for i in range(2)]
        squared, rooted, scaled, normed = s.sem("squared"), s.sem("rooted"), s.sem("scaled"), s.sem("normed")
        turned, hT_written = s.sem("turned"), s.sem("hT_written")
        line_done, line_copied, line_out = s.sem("line_done"), s.sem("line_copied"), s.sem("line_out")
        choices_in = s.sem("choices_in")
        bf_ready, pt_in = s.sem("bf_ready"), s.sem("pt_in")
        block = ctx.enter_context(nc.Block())
        rows = [P, P, P, P, NS]
        pieces = [(c, min(CH, LINE - c)) for c in range(0, LINE, CH)]

        @block.sync
        def _(sp):
            sp.dma_start(kept.consts[:], io.consts[:, 0:C_KEPT]).then_inc(consts_in, 16)
            sp.dma_start(choices[:].rearrange("p a n -> p (a n)"), io.consts[:, C_SELE:C_PM]).then_inc(choices_in, 16)
            for m in range(5):
                if m >= 2:
                    sp.wait_ge(turned, 4 * (m - 1))
                src = io.xp[m * P:(m + 1) * P, :] if m < 4 else io.xs
                sp.dma_start(x[0:rows[m], m % 2, :], src).then_inc(x_in[m % 2], 16)
                if m == 1:
                    sp.dma_start(table[:], io.rel_bias).then_inc(table_in, 16)
                    sp.dma_start(onehot[:], io.onehot).then_inc(onehot_in, 16)
                    sp.dma_start(kept.pages[:], io.page_table.rearrange("b n -> (b n)").rearrange("(a n) -> a n", a=1)).then_inc(pt_in, 16)
                    for b in range(NB):
                        to = kept.paired[:].rearrange("o (g c b q) -> o g b c q", g=NB // 2, b=2, q=PPC)[:, b // 2, b % 2]
                        sp.dma_start(to, io.page_table[b:b + 1, :].rearrange("o (c q) -> o c q", q=PPC)).then_inc(pt_in, 16)
            sp.wait_ge(line_copied, len(pieces))
            sp.dma_start(io.line, line[:]).then_inc(line_out, 16)
            sp.wait_ge(line_out, 16)
            sp.wait_ge(pt_in, 16 * (1 + NB))

        @block.gpsimd
        def _(pool):
            with nc.allow_non_contiguous_dma(reason="a small column"):
                pool.dma_start(gcol[:], io.norm_pre.rearrange("(k p) -> p k", p=P)).then_inc(gain_in, 16)
            pool.wait_ge(gain_in, 16)

        @block.scalar
        def _(act):
            act.preload_act_table_set("natural_log_exp_and_others")
            for m in range(5):
                act.wait_ge(x_in[m % 2], 16 * (m // 2 + 1))
                if m:
                    act.wait_ge(squared, m)
                act.activation(sq[0:rows[m], :], x[0:rows[m], m % 2, :], ACT.Square,
                               accum_out=ss[0:rows[m], m:m + 1]).then_inc(squared, 1)
                act.wait_ge(scaled, m + 1)
                act.activation(rstd[0:rows[m], m:m + 1], rstd[0:rows[m], m:m + 1], ACT.Ln).then_inc(rooted, 1)
                act.wait_ge(rooted, 2 * m + 1)
                act.activation(rstd[0:rows[m], m:m + 1], rstd[0:rows[m], m:m + 1], ACT.Exp, scale=-0.5).then_inc(rooted, 1)
            for n, (c, w) in enumerate(pieces):
                act.wait_ge(line_done, n + 1)
                act.copy(line[:, c:c + w], lp[n % 2][:, 0:w]).then_inc(line_copied, 1)

        @block.tensor
        def _(pe):
            pe.wait_ge(consts_in, 16)
            for m in range(5):
                pe.wait_ge(normed, m + 1)
                for q in range(4):
                    n = 4 * m + q
                    if n >= 2:
                        pe.wait_ge(hT_written, n - 1)
                    for k in range(4):
                        last = pe.transpose(tp[n % 2][:, k, 0:rows[m]], x[0:rows[m], m % 2, (4 * q + k) * P:(4 * q + k + 1) * P],
                                            kept.ident[0:rows[m], 0:rows[m]])
                    last.then_inc(turned, 1)
            pe.wait_ge(table_in, 16)
            pe.wait_ge(onehot_in, 16)
            for n, (c, w) in enumerate(pieces):
                if n >= 2:
                    pe.wait_ge(line_copied, n - 1)
                pe.matmul(lp[n % 2][:, 0:w], table[:], onehot[:, c:c + w], start=True, stop=True).then_inc(line_done, 1)

        @block.vector
        def _(dve):
            dve.wait_ge(consts_in, 16)
            dve.wait_ge(choices_in, 16)
            dve.tensor_copy(kept.sel_e[:], choices[:, 0]).then_inc(bf_ready, 1)
            dve.tensor_copy(kept.sel_d[:], choices[0:NS, 1]).then_inc(bf_ready, 1)
            dve.tensor_copy(kept.ident_b[:], kept.ident).then_inc(bf_ready, 1)

            def norm(m):
                r = rows[m]
                dve.wait_ge(squared, m + 1)
                dve.tensor_scalar(rstd[0:r, m:m + 1], ss[0:r, m:m + 1], 1.0 / D, EPS, ALU.mult, ALU.add).then_inc(scaled, 1)
                dve.wait_ge(rooted, 2 * m + 2)
                dve.tensor_scalar(x[0:r, m % 2, :], x[0:r, m % 2, :], rstd[0:r, m:m + 1], None, ALU.mult).then_inc(normed, 1)

            norm(0)
            dve.wait_ge(gain_in, 16)
            for m in range(5):
                if m < 4:
                    norm(m + 1)
                r = rows[m]
                for q in range(4):
                    n = 4 * m + q
                    dve.wait_ge(turned, n + 1)
                    dve.tensor_tensor(hT[:, 4 * q:4 * q + 4, m * P:m * P + r], tp[n % 2][:, :, 0:r],
                                      gcol[:, 4 * q:4 * q + 4].unsqueeze(2).to_broadcast([P, 4, r]), ALU.mult).then_inc(hT_written, 1)


def project_in(nc, io, hT):
    with ExitStack() as ctx:
        s = Scope(nc, ctx, "proj")
        w = [s.sb(f"w{i}", [P, KT_IN, CH]) for i in range(2)]
        out = [s.sb(f"out{i}", [P, 5, CH]) for i in range(2)]
        acc = [s.ps(f"acc{m}", [P, CH]) for m in range(5)]
        w_in = [s.sem(f"w_in{i}") for i in range(2)]
        w_used, summed, copied = s.sem("w_used"), s.sem("summed"), s.sem("copied")
        out_stored = [s.sem(f"out_stored{i}") for i in range(2)]
        block = ctx.enter_context(nc.Block())
        rows = [P, P, P, P, NS]
        CREDIT = 5 + 1
        whole = DIN // CH
        tail = DIN - whole * CH
        assert whole % 2 == 0

        def load_w(sp, u, col, width):
            src = io.w_in.rearrange("(k p) n -> p k n", p=P)
            for q in range(4):
                sp.dma_start(w[u][:, 4 * q:4 * q + 4, 0:width], src[:, 4 * q:4 * q + 4, col]).then_inc(w_in[u], 16)

        @block.sync
        def _(sp):
            with sp.Fori(0, whole // 2) as i:
                for u in range(2):
                    sp.wait_ge(summed, i * 10 + 5 * u + 1)
                    load_w(sp, u, bass.ds((i * 2 + u) * CH, CH), CH)
            sp.wait_ge(summed, 5 * whole + 1)
            load_w(sp, 0, slice(whole * CH, DIN), tail)

        @block.tensor
        def _(pe):
            pe.nop().then_inc(summed, CREDIT)

            def chunk(u, fills, n_waits, width):
                pe.wait_ge(w_in[u], fills)
                for m in range(5):
                    pe.wait_ge(copied, n_waits + m)
                    for k in range(KT_IN):
                        last = pe.matmul(acc[m][0:rows[m], 0:width], hT[:, k, m * P:m * P + rows[m]], w[u][:, k, 0:width],
                                         start=(k == 0), stop=(k == KT_IN - 1))
                    last.then_inc(summed, 1)

            with pe.Fori(0, whole // 2) as i:
                for u in range(2):
                    chunk(u, i * 64 + 64, i * 10 + 5 * u + 2, CH)
            chunk(0, 64 * (whole // 2 + 1), 5 * whole + 2, tail)

        def evacuate(eng, m, u, summed_by, stored_by, width):
            eng.wait_ge(summed, summed_by)
            eng.wait_ge(out_stored[u], stored_by)
            copy = eng.copy if eng is nc.scalar else eng.tensor_copy
            copy(out[u][0:rows[m], m, 0:width], acc[m][0:rows[m], 0:width]).then_inc(copied, 1)

        @block.vector
        def _(dve):
            dve.nop().then_inc(copied, CREDIT)
            with dve.Fori(0, whole // 2) as i:
                for u in range(2):
                    for m in range(5):
                        evacuate(dve, m, u, i * 10 + 5 * u + m + 1 + CREDIT, i * 32 + 16, CH)
            for m in range(5):
                evacuate(dve, m, 0, 5 * whole + m + 1 + CREDIT, 32 * (whole // 2) + 16, tail)

        @block.scalar
        def _(act):
            for u in range(2):
                act.nop().then_inc(out_stored[u], 16)

            def store(u, col, width, copied_by):
                act.wait_ge(copied, copied_by)
                act.dma_start(io.proj[0:SEQ, col].rearrange("(m p) n -> p m n", p=P), out[u][:, 0:4, 0:width]).then_inc(out_stored[u], 16)
                act.dma_start(io.proj[SEQ:TOK, col], out[u][0:NS, 4, 0:width]).then_inc(out_stored[u], 16)

            with act.Fori(0, whole // 2) as i:
                for u in range(2):
                    store(u, bass.ds((i * 2 + u) * CH, CH), CH, i * 10 + 5 * u + 5 + CREDIT)
            store(0, slice(whole * CH, DIN), tail, 5 * whole + 5 + CREDIT)
            act.wait_ge(out_stored[0], 32 * (whole // 2 + 1) + 16)
            act.wait_ge(out_stored[1], 32 * (whole // 2) + 16)


def place_queries(kept, keep):
    kept.q_sb = keep.sb("q_sb", [P, NB, 4, 32])
    kept.q_dsa = keep.sb("q_dsa", [P, NB, 2, 64])
    kept.q_nsa = keep.sb("q_nsa", [P, NB, 2, 64])
    kept.q_idx = keep.sb("q_idx", [P, 2, NB, 32])
    kept.k_sb = keep.sb("k_sb", [P, 4, NS])
    kept.k_dsa = keep.sb("k_dsa", [P, 2, NS])
    kept.k_slc = keep.sb("k_slc", [P, 2, NS])
    kept.k_win = keep.sb("k_win", [P, 2, NS])
    kept.k_idx = keep.sb("k_idx", [64, NS])
    kept.w_idx = keep.sb("w_idx", [P, 2])
    kept.gates = keep.sb("gates", [P, 4, 3])


def prepare(nc, io, kept):
    with ExitStack() as ctx:
        s = Scope(nc, ctx, "prep")
        new = s.sb("new", [NS, DIN])
        tp = [s.ps(f"tp{i}", [P, 8, NS]) for i in range(4)]
        new_in, copies_out, cols_in = s.sem("new_in"), s.sem("copies_out"), s.sem("cols_in")
        zeroed, turned, copied, gated = s.sem("zeroed"), s.sem("turned"), s.sem("copied"), s.sem("gated")
        block = ctx.enter_context(nc.Block())

        items = [(SB_Q + h * DH, kept.q_sb[:, :, h, h * 8:h * 8 + 8], SCALE) for h in range(4)]
        for col, q in ((DSA_Q, kept.q_dsa), (NSA_Q, kept.q_nsa)):
            items += [(col + h * DH, q[:, :, h // 3, h * 8:h * 8 + 8], SCALE) for h in range(6)]
        for col, k, n in ((SB_K, kept.k_sb, 4), (DSA_K, kept.k_dsa, 2), (NSA_KS, kept.k_slc, 2), (NSA_KW, kept.k_win, 2)):
            items += [(col + h * DH, k[:, h, :], None) for h in range(n)]
        n_full = len(items)
        idx_cols = [IDX_Q, IDX_Q + DH, IDX_K]
        total = n_full + 3

        @block.sync
        def _(sp):
            sp.dma_start(new[:], io.proj[SEQ:TOK, :]).then_inc(new_in, 16)
            sp.wait_ge(zeroed, 5)
            with nc.allow_non_contiguous_dma(reason="a few numbers per row"):
                for b in range(NB):
                    rows = io.proj[SEQ + b * NT:SEQ + b * NT + NT, :]
                    sp.dma_start(kept.w_idx[b % 4 * 32:b % 4 * 32 + 32, b // 4:b // 4 + 1],
                                 rows[:, IDX_W:IDX_W + 4].rearrange("t h -> h t").unsqueeze(2)).then_inc(cols_in, 16)
                    for r in range(3):
                        sp.dma_start(kept.gates[b % 2 * 64:b % 2 * 64 + 48, b // 2, r:r + 1],
                                     rows[:, NSA_BG + 6 * r:NSA_BG + 6 * r + 6].rearrange("t h -> h t").unsqueeze(2)).then_inc(cols_in, 16)
            sp.wait_ge(cols_in, 64 * NB)

        @block.gpsimd
        def _(pool):
            for n, t in enumerate((kept.q_sb, kept.q_dsa, kept.q_nsa, kept.q_idx, kept.gates)):
                pool.memset(t[:], 0.0).then_inc(zeroed, 1)

        @block.scalar
        def _(act):
            n = 0
            for to_p, to_s, col, width in io.new_rows:
                act.dma_start(to_p, io.proj[0:SEQ, col:col + width]).then_inc(copies_out, 16)
                act.dma_start(to_s, io.proj[SEQ:TOK, col:col + width]).then_inc(copies_out, 16)
                n += 2
            act.dma_start(io.win_p, io.proj[0:SEQ, NSA_KW:NSA_KW + 512]).then_inc(copies_out, 16)
            act.dma_start(io.win_s[:, WIN - NT:WIN, :], io.proj[SEQ:TOK, NSA_KW:NSA_KW + 512].rearrange("(b t) n -> b t n", t=NT)).then_inc(copies_out, 16)
            act.dma_start(io.win_s[:, 0:WIN - NT, :], io.win_state[:, NT:WIN, :]).then_inc(copies_out, 16)
            first = DMAX - SEQ - (P - 1)
            act.dma_start(io.lines, io.line[:, first:first + XL].unsqueeze(0).to_broadcast([P, HB, XL])).then_inc(copies_out, 16)
            act.wait_ge(cols_in, 64 * NB)
            act.activation(kept.gates[:], kept.gates[:], ACT.Exp, scale=-1.0).then_inc(gated, 1)
            act.wait_ge(zeroed, 5)
            for i, (_, to, scale) in enumerate(items):
                act.wait_ge(turned, i // 8 + 1)
                src = tp[i // 8][:, i % 8, :]
                if scale:
                    act.activation(to, src.rearrange("p (b t) -> p b t", t=NT), ACT.Copy, scale=scale).then_inc(copied, 1)
                else:
                    act.copy(to, src).then_inc(copied, 1)
            act.wait_ge(turned, 4)
            for j in range(2):
                src = tp[3][:, n_full - 24 + j, :].rearrange("p (b t) -> p b t", t=NT)
                for i in range(2):
                    h = 2 * j + i
                    for half in range(2):
                        act.copy(kept.q_idx[64 * half:64 * half + 64, half, :, h * 8:h * 8 + 8], src[64 * i:64 * i + 64]).then_inc(copied, 1)
            act.copy(kept.k_idx[:], tp[3][0:64, n_full - 24 + 2, :]).then_inc(copied, 1)
            act.wait_ge(copies_out, 16 * (n + 4))

        @block.tensor
        def _(pe):
            pe.wait_ge(new_in, 16)
            cols = [c for c, _, _ in items] + idx_cols
            for i, c in enumerate(cols):
                last = pe.transpose(tp[i // 8][:, i % 8, :], new[:, c:c + DH], kept.ident[0:NS, 0:NS])
                if i % 8 == 7 or i == total - 1:
                    last.then_inc(turned, 1)

        @block.vector
        def _(dve):
            dve.wait_ge(gated, 1)
            dve.tensor_scalar(kept.gates[:], kept.gates[:], 1.0, None, ALU.add).then_inc(gated, 1)
            dve.wait_ge(gated, 2)
            dve.reciprocal(kept.gates[:], kept.gates[:]).then_inc(gated, 1)


def page_numbers(nc, io, table, first, count):
    _, pages = nc.values_load_multi_w_load_instructions(table[0:1, bass.ds(first, count)], engines=(mybir.EngineType.SP,),
                                                        min_val=0, max_val=io.n_pool - 1)
    return pages


def pair_pages(nc, io, kept, pair, c):
    return page_numbers(nc, io, kept.paired, pair * (2 * NPG) + c * (2 * PPC), 2 * PPC)


def load_pages(sp, pages, to, cache, col, width, sem):
    for p, page in enumerate(pages):
        src = cache[bass.ds(page, 1), :, col:col + width].rearrange("o p c -> (o p) c")
        sp.dma_start(to[:, p], src).then_inc(sem, 16)


def compress(nc, io, kept):
    with ExitStack() as ctx:
        s = Scope(nc, ctx, "cmp")
        SLOTS = 4
        CREDIT = 4 * (SLOTS - 1)
        w1 = s.sb("w1", [P, 4, CMPB, DH])
        w2 = kept.q_sb[:].rearrange("p b h r -> p (b h r)")[:, 0:4 * DH].rearrange("p (a f) -> p a f", f=DH)
        pe_rows = kept.q_dsa[0:CMPB].rearrange("p b h r -> p (b h r)")[:, 0:4 * DH].rearrange("p (a f) -> p a f", f=DH)
        half = lambda x, i: x[:, i * 4 * NC:(i + 1) * 4 * NC].rearrange("p (a c) -> p a c", c=NC)
        spare_a, spare_b = kept.oTs[:].rearrange("p h t -> p (h t)"), kept.q_nsa[:].rearrange("p b h r -> p (b h r)")
        hid_e, hid_r, hid = half(spare_a, 0), half(spare_a, 1), half(spare_b, 0)
        shift = s.sb("shift", [P, 2, 4])
        rows = [s.sb(f"rows{i}", [P, PPC, 4, DH]) for i in range(SLOTS)]
        xT = s.sb("xT", [P, 4, PAST])
        tp = [s.ps(f"tp{i}", [P, CH]) for i in range(2)]
        hp = s.ps("hp", [P, 4, NC])
        kp = s.ps("kp", [P, 2, NC])
        vp = s.ps("vp", [P, 2, DH])
        pe_in, w_in, rows_in = s.sem("pe_in"), s.sem("w_in"), [s.sem(f"rows_in{i}") for i in range(SLOTS)]
        turned, x_even, x_odd = s.sem("turned"), s.sem("x_even"), s.sem("x_odd")
        hid_summed, hid_exp, hid_done, out_summed, out_copied = (
            s.sem("hid_summed"), s.sem("hid_exp"), s.sem("hid_done"), s.sem("out_summed"), s.sem("out_copied"))
        pe_turned, pe_copied, shift_done, hid_step = (
            s.sem("pe_turned"), s.sem("pe_copied"), s.sem("shift_done"), s.sem("hid_step"))
        block = ctx.enter_context(nc.Block())

        @block.sync
        def _(sp):
            sp.dma_start(pe_rows, io.cmp_pe).then_inc(pe_in, 16)
            sp.dma_start(w2, io.cmp_w2.rearrange("a e f -> e a f")).then_inc(w_in, 16)
            sp.dma_start(rows[0][:], io.proj[0:SEQ, NSA_KC:NSA_KC + 512].rearrange("(m p) n -> p m n", p=P)).then_inc(rows_in[0], 64)
            for a in range(4):
                sp.dma_start(w1[:, a], io.cmp_w1[a]).then_inc(w_in, 16)
            with sp.Fori(0, NB * NCH // SLOTS) as i:
                for u in range(SLOTS):
                    if u % 2 == 0:
                        pages = page_numbers(nc, io, kept.pages, i * (SLOTS * PPC) + PPC * u, 2 * PPC)
                    sp.wait_ge(turned, i * 16 + 4 * u + 4)
                    v = (u + 1) % SLOTS
                    load_pages(sp, pages[u % 2 * PPC:(u % 2 + 1) * PPC], rows[v][:], io.nsa_cache, 0, 512, rows_in[v])

        def turn(pe, unit, u, filled):
            pe.wait_ge(rows_in[u], filled)
            for a in range(4):
                pe.wait_ge((x_even, x_odd)[a % 2], unit * 2 + a // 2 + 1)
                for p in range(PPC):
                    last = pe.transpose(tp[a % 2][:, p * P:(p + 1) * P], rows[u][:, p, a, :], kept.ident)
                last.then_inc(turned, 1)

        def mlp(pe, n, blocks, units_copied):
            pe.wait_ge(x_even, units_copied * 2 + 1)
            pe.wait_ge(x_odd, units_copied * 2 + 1)
            for a in range(4):
                more = blocks if blocks == NC else blocks + 1
                xv = xT[:, a, 0:more * CMPB].rearrange("p (c r) -> p r c", r=CMPB)
                for r in range(CMPB):
                    last = pe.matmul(hp[:, a, 0:more], w1[:, a, r, :], xv[:, r, :], start=(r == 0), stop=(r == CMPB - 1))
            last.then_inc(hid_summed, 1)
            pe.wait_ge(hid_done, n + 1)
            pe.wait_ge(out_copied, n * 2 + 2)
            for kv in range(2):
                pe.matmul(kp[:, kv, 0:blocks], w2[:, kv, :], hid[:, kv, 0:blocks], start=True, stop=True)
            for kv in range(2):
                last = pe.matmul(vp[0:blocks, kv, :], hid[:, 2 + kv, 0:blocks], w2[:, 2 + kv, :], start=True, stop=True)
            last.then_inc(out_summed, 1)

        @block.tensor
        def _(pe):
            pe.nop().then_inc(turned, CREDIT)
            pe.wait_ge(pe_in, 16)
            for a in range(4):
                last = pe.transpose(tp[0][:, a * CMPB:(a + 1) * CMPB], pe_rows[:, a, :], kept.ident[0:CMPB, 0:CMPB])
            last.then_inc(pe_turned, 1)
            pe.wait_ge(pe_copied, 1)
            turn(pe, 0, 0, 64)
            pe.wait_ge(w_in, 80)
            mlp(pe, 0, SEQ // CMPB, 1)
            with pe.Fori(0, NB) as b:
                with pe.Fori(0, NCH // SLOTS) as c:
                    for u in range(SLOTS):
                        turn(pe, b * 8 + c * 4 + (u + 1), (u + 1) % SLOTS, (b * 2 + c) * 64 + 64 * (1 + (u + 1) // SLOTS))
                mlp(pe, b + 1, NC, b * 8 + 9)

        def copy_part(eng, sem, a, unit, at, last_mlp):
            eng.wait_ge(turned, unit * 4 + a + 1 + CREDIT)
            eng.wait_ge(hid_summed, last_mlp)
            copy = eng.copy if a % 2 else eng.tensor_copy
            copy(xT[:, a, at], tp[a % 2][:]).then_inc(sem, 1)

        @block.vector
        def _(dve):
            dve.nop().then_inc(x_even, 1)
            dve.nop().then_inc(hid_summed, 1)
            dve.wait_ge(pe_turned, 1)
            dve.tensor_copy(xT[:, :, SEQ:SEQ + CMPB], tp[0][:, 0:4 * CMPB].rearrange("p (a r) -> p a r", r=CMPB)).then_inc(pe_copied, 1)

            def activate(n, blocks):
                dve.wait_ge(hid_exp, n + 1)
                dve.tensor_scalar(hid_r[:, :, 0:blocks], hid_e[:, :, 0:blocks], 1.0, None, ALU.add).then_inc(hid_step, 1)
                dve.wait_ge(hid_step, n * 2 + 1)
                dve.reciprocal(hid_r[:, :, 0:blocks], hid_r[:, :, 0:blocks]).then_inc(hid_step, 1)
                dve.wait_ge(hid_step, n * 2 + 2)
                dve.wait_ge(out_summed, n + 1)
                for a in range(4):
                    last = dve.scalar_tensor_tensor(hid[:, a, 0:blocks], hp[:, a, 0:blocks], shift[:, 0, a:a + 1], hid_r[:, a, 0:blocks], ALU.add, ALU.mult)
                last.then_inc(hid_done, 1)

            dve.nop().then_inc(out_summed, 1)
            for a in (0, 2):
                copy_part(dve, x_even, a, 0, slice(0, CH), 1)
            dve.wait_ge(hid_summed, 2)
            dve.tensor_copy(shift[:, 0, :], hp[:, :, SEQ // CMPB]).then_inc(shift_done, 1)
            dve.wait_ge(shift_done, 1)
            dve.tensor_scalar(shift[:, 1, :], shift[:, 0, :], -1.0, None, ALU.mult).then_inc(shift_done, 1)
            activate(0, SEQ // CMPB)
            with dve.Fori(0, NB) as b:
                with dve.Fori(0, NCH) as c:
                    for a in (0, 2):
                        copy_part(dve, x_even, a, b * 8 + c + 1, bass.ds(c * CH, CH), b + 2)
                activate(b + 1, NC)

        @block.scalar
        def _(act):
            act.preload_act_table_set("natural_log_exp_and_others")
            act.nop().then_inc(x_odd, 1)
            act.nop().then_inc(out_copied, 2)

            def exps(n, blocks):
                act.wait_ge(hid_summed, n + 2)
                act.wait_ge(hid_done, n) if not isinstance(n, int) else None
                for a in range(4):
                    last = act.activation(hid_e[:, a, 0:blocks], hp[:, a, 0:blocks], ACT.Exp, bias=shift[:, 1, a:a + 1], scale=-1.0)
                last.then_inc(hid_exp, 1)

            def results(n, to_k, to_v, blocks):
                act.wait_ge(out_summed, n + 2)
                act.copy(to_k, kp[:, :, 0:blocks]).then_inc(out_copied, 1)
                act.copy(to_v, vp[0:blocks]).then_inc(out_copied, 1)

            for a in (1, 3):
                copy_part(act, x_odd, a, 0, slice(0, CH), 1)
            act.wait_ge(shift_done, 2)
            exps(0, SEQ // CMPB)
            results(0, kept.cmp_kp[:], kept.cmp_vp[:], SEQ // CMPB)
            with act.Fori(0, NB) as b:
                with act.Fori(0, NCH) as c:
                    for a in (1, 3):
                        copy_part(act, x_odd, a, b * 8 + c + 1, bass.ds(c * CH, CH), b + 2)
                exps(b + 1, NC)
                results(b + 1, kept.cmp_k[:, bass.ds(b, 1)].rearrange("p o k c -> p (o k) c"),
                        kept.cmp_v[:, bass.ds(b, 1)].rearrange("p o k c -> p (o k) c"), NC)


def index_scores(nc, io, kept):
    with ExitStack() as ctx:
        s = Scope(nc, ctx, "idx")
        rows = s.sb("rows", [P, NB, PPC, 64])
        kT = [s.sb(f"kT{i}", [P, 2, P]) for i in range(2)]
        relu = [s.sb(f"relu{g}", [P, CH]) for g in range(2)]
        tp = [s.ps(f"tp{i}", [P, 2, P]) for i in range(2)]
        sp_ = [s.ps(f"sc{g}", [P, CH]) for g in range(2)]
        total = s.ps("total", [NS, CH])
        rows_in = [s.sem(f"rows_in{b}") for b in range(NB)]
        turned, even_copied, odd_copied, multiplied = s.sem("turned"), s.sem("even_copied"), s.sem("odd_copied"), s.sem("multiplied")
        weighted, summed, total_copied, masked = s.sem("weighted"), s.sem("summed"), s.sem("total_copied"), s.sem("masked")
        copied_by = (even_copied, odd_copied)
        block = ctx.enter_context(nc.Block())
        seli = [kept.consts[:, C_SELI + g * NS:C_SELI + (g + 1) * NS] for g in range(2)]

        @block.sync
        def _(sp):
            with sp.Fori(0, NCH) as c:
                for b in range(NB):
                    if b % 2 == 0:
                        pages = pair_pages(nc, io, kept, b // 2, c)
                    sp.wait_ge(turned, c * NB + b + 1)
                    load_pages(sp, pages[b % 2 * PPC:(b % 2 + 1) * PPC], rows[:, b], io.idx_cache, 0, 64, rows_in[b])

        @block.tensor
        def _(pe):
            pe.nop().then_inc(turned, NB)
            pe.nop().then_inc(multiplied, 2)

            def product(b, n):
                g, r = divmod(b, 4)
                pe.wait_ge(copied_by[b % 2], n + 2)
                for half in range(2):
                    to = sp_[g][32 * r:32 * r + 32, :].rearrange("p (q a k) -> p a q k", a=2, k=P)[:, half]
                    last = pe.matmul(to, kept.q_idx[:, half, b, :], kT[b % 2][:], start=(half == 0), stop=(half == 1),
                                     tile_position=(0, 32 * r), skip_group_check=True)
                last.then_inc(multiplied, 1)

            def add_up(g, c):
                pe.wait_ge(weighted, c * 2 + g + 3)
                pe.matmul(total[:], seli[g], relu[g][:], start=(g == 0), stop=(g == 1)).then_inc(summed, 1)

            with pe.Fori(0, NCH) as c:
                for b in range(NB):
                    pe.wait_ge(rows_in[b], c * 64 + 64)
                    pe.wait_ge(copied_by[b % 2], c * 4 + (b // 2 + 1))
                    for q in range(2):
                        last = pe.transpose(tp[b % 2][:, q, :], rows[:, b, 2 * q:2 * q + 2, :].rearrange("p a d -> p (a d)"), kept.ident)
                    last.then_inc(turned, 1)
                    if b == 1 or b == 5:
                        pe.wait_ge(weighted, c * 2 + b // 4 + 1)
                    if b:
                        product(b - 1, c * 4 + (b - 1) // 2)
                    if b == 6:
                        pe.wait_ge(total_copied, c + 1)
                        add_up(0, c)
                product(NB - 1, c * 4 + (NB - 1) // 2)
                add_up(1, c)
            n = NCH * NB
            for g in range(2):
                pe.wait_ge(weighted, NCH * 2 + g + 1)
                for r in range(4):
                    b = 4 * g + r
                    last = pe.matmul(sp_[g][32 * r:32 * r + 32, 0:NT], kept.q_idx[0:64, 0, b, :], kept.k_idx[:, b * NT:b * NT + NT],
                                     start=True, stop=True, tile_position=(0, 32 * r))
                last.then_inc(multiplied, 4)
            pe.wait_ge(total_copied, NCH + 1)
            for g in range(2):
                pe.wait_ge(weighted, NCH * 2 + g + 3)
                pe.matmul(total[:, 0:NT], seli[g], relu[g][:, 0:NT], start=(g == 0), stop=(g == 1)).then_inc(summed, 1)

        def copy_keys(eng, n, b):
            eng.wait_ge(turned, n + 1 + NB)
            eng.wait_ge(multiplied, n + 1)
            copy = eng.copy if b % 2 else eng.tensor_copy
            copy(kT[b % 2][:], tp[b % 2][:]).then_inc(copied_by[b % 2], 1)

        @block.vector
        def _(dve):
            dve.nop().then_inc(even_copied, 1)
            dve.nop().then_inc(weighted, 2)

            def weigh(g, c, width):
                dve.wait_ge(multiplied, c * NB + 4 * g + 4 + 2)
                dve.wait_ge(summed, c * 2 + g + 1)
                dve.tensor_scalar(relu[g][:, 0:width], sp_[g][:, 0:width], 0.0, kept.w_idx[:, g:g + 1], ALU.max, ALU.mult).then_inc(weighted, 1)

            with dve.Fori(0, NCH) as c:
                for b in range(NB):
                    if b % 2 == 0:
                        copy_keys(dve, c * NB + b, b)
                    if b == 5:
                        weigh(0, c, CH)
                weigh(1, c, CH)
            weigh(0, NCH, NT)
            weigh(1, NCH, NT)
            dve.wait_ge(summed, 2 * NCH + 2 + 2)
            dve.tensor_tensor(kept.scores[:, PAST:KEYS], total[:, 0:NT], kept.consts[0:NS, C_NM:C_NM + NT], ALU.add).then_inc(masked, 1)

        @block.scalar
        def _(act):
            act.nop().then_inc(odd_copied, 1)
            act.nop().then_inc(summed, 2)
            act.nop().then_inc(total_copied, 1)
            with act.Fori(0, NCH) as c:
                for b in range(1, NB, 2):
                    copy_keys(act, c * NB + b, b)
                act.wait_ge(summed, c * 2 + 4)
                act.copy(kept.scores[:, bass.ds(c * CH, CH)], total[:]).then_inc(total_copied, 1)


def stream(nc, io, kept, tag, *, cache, col, proj_v, heads, per, q, k_new, select=None, dropped_keys=None, bias_rows=None,
           bias_first=0, mask_last=None, head0, state=None, gate=None, add=False, stick=False):
    groups = NB // per
    stride = P // per
    nch = 1 if state is not None else NCH
    past = nch * CH
    width = heads * DH
    items = per * heads
    SLOTS = 2 if stick or nch == 1 else 4
    per_bank = CH // width
    with ExitStack() as ctx:
        s = Scope(nc, ctx, tag)
        if stick:
            k_rows = [s.sb(f"k_rows{i}", [P, per, PPC, width]) for i in range(SLOTS)]
            v_rows = [s.sb(f"v_rows{i}", [P, per, PPC, width]) for i in range(SLOTS)]
        else:
            rows = [s.sb(f"rows{i}", [P, per, PPC, 2 * width]) for i in range(SLOTS)]
            k_rows = [r[:, :, :, 0:width] for r in rows]
            v_rows = [r[:, :, :, width:] for r in rows]
        q_now = s.sb("q_now", [P, per, heads, stride])
        v_new = (v_rows if stick else rows)[SLOTS - 1][0:NT].rearrange("p b m c -> p (b m c)")[:, 0:NB * width].rearrange("p (b c) -> p b c", b=NB)
        kT = [s.sb(f"kT{i}", [P, CH]) for i in range(2)]
        prob = [s.sb(f"prob{i}", [P, CH]) for i in range(2)]
        pT = [s.sb(f"pT{i}", [P, PPC, P]) for i in range(2)]
        log_new = s.sb("log_new", [P, groups, NT])
        prob_new = s.sb("prob_new", [P, groups, P])
        pT_new = s.sb("pT_new", [NT, groups, P])
        acc = s.sb("acc", [P, groups, width])
        if stick:
            soft = [s.sb(f"soft{i}", [P, CH]) for i in range(2)]
            soft_new = s.sb("soft_new", [P, groups, NT])
            top8 = s.sb("top8", [NS, 8])
        else:
            bias = s.sb("bias", [P, past + NT])
            nstep = s.sb("nstep", [P, groups, nch + 1])
            nmax = s.sb("nmax", [P, groups, nch + 1])
            shrink = s.sb("shrink", [P, groups, nch + 1])
            share = s.sb("share", [P, groups, nch + 1])
            sums = s.sb("sums", [P, groups, nch + 1])
            rcp = s.sb("rcp", [P, groups])
        if select is not None:
            sel_now = s.sb("sel_now", [select.shape[0], P], BF16)
        tp = [s.ps(f"tp{i}", [P, CH]) for i in range(2)]
        sc = [s.ps(f"sc{i}", [P, CH]) for i in range(2)]
        sc_new = s.ps("sc_new", [P, groups, NT])
        qp = s.ps("qp", [P, PPC, P])
        pv = [s.ps(f"pv{i}", [P, CH]) for i in range(2)]

        k_in = [[s.sem(f"k_in{i}_{b}") for b in range(per)] for i in range(SLOTS)]
        v_in = [[s.sem(f"v_in{i}_{b}") for b in range(per)] for i in range(SLOTS)] if stick else k_in
        small_in, bias_in, zeroed, staged = s.sem("small_in"), s.sem("bias_in"), s.sem("zeroed"), s.sem("staged")
        k_turned, kT_copied, scored, sc_read = s.sem("k_turned"), s.sem("kT_copied"), s.sem("scored"), s.sem("sc_read")
        maxed, probs, probs_turned, pT_copied, v_used, acc_done = (
            s.sem("maxed"), s.sem("probs"), s.sem("probs_turned"), s.sem("pT_copied"), s.sem("v_used"), s.sem("acc_done"))
        new_scored, new_prob, new_turned, new_copied, new_summed, new_acc = (
            s.sem("new_scored"), s.sem("new_prob"), s.sem("new_turned"), s.sem("new_copied"), s.sem("new_summed"), s.sem("new_acc"))
        step_dve, step_act, acc_ready, acc_turned, out_done, shrunk = (
            s.sem("step_dve"), s.sem("step_act"), s.sem("acc_ready"), s.sem("acc_turned"), s.sem("out_done"), s.sem("shrunk"))
        if stick:
            soft_step, soft_done, top_step = s.sem("soft_step"), s.sem("soft_done"), s.sem("top_step")
        block = ctx.enter_context(nc.Block())

        def each_group(eng, body, unroll=False):
            if nch == 1 or unroll:
                for g in range(groups):
                    body(g)
            else:
                with eng.Fori(0, groups) as g:
                    body(g)

        def slot(g, c):
            return (c % SLOTS, g * (nch // SLOTS) + c // SLOTS + 1) if nch > 1 else (g % SLOTS, g // SLOTS + 1)

        def parity(g, c):
            return c % 2 if nch > 1 else g % 2

        def data(c):
            return nch - 1 - c if stick else c

        @block.sync
        def _(sp):
            sp.dma_start(v_new, io.proj[SEQ:TOK, proj_v:proj_v + width].rearrange("(b t) c -> t b c", t=NT)).then_inc(small_in, 16)

            def rows_of(g):
                for c in range(nch):
                    n = c + g * nch
                    i, _ = slot(g, c)
                    if i == SLOTS - 1:
                        sp.wait_ge(new_summed, 1)
                    for b in range(per):
                        if state is not None:
                            sp.wait_ge(v_used, n * per + b + 1)
                            sp.dma_start(rows[i][:, b], state[g * per + b].rearrange("(m p) c -> p m c", p=P)).then_inc(k_in[i][b], 64)
                            continue
                        if b % 2 == 0:
                            pages = pair_pages(nc, io, kept, g * (per // 2) + b // 2, data(c))
                        mine = pages[b % 2 * PPC:(b % 2 + 1) * PPC]
                        if stick:
                            sp.wait_ge(k_turned, n * items + (b + 1) * heads)
                            load_pages(sp, mine, k_rows[i][:, b], cache, col, width, k_in[i][b])
                        sp.wait_ge(v_used, n * per + b + 1)
                        if stick:
                            load_pages(sp, mine, v_rows[i][:, b], cache, col + width, width, v_in[i][b])
                        else:
                            load_pages(sp, mine, rows[i][:, b], cache, col, 2 * width, k_in[i][b])

            each_group(sp, rows_of)

        @block.gpsimd
        def _(pool):
            if not stick:
                pool.memset(bias[:], 0.0).then_inc(zeroed, 1)
            pool.memset(prob_new[:], 0.0).then_inc(zeroed, 1)

            def stage(g):
                pool.wait_ge(scored, g * nch * items + 2)
                pool.tensor_copy(q_now[:], q[:, bass.ds(g * per, per)]).then_inc(staged, 1)
                if select is not None:
                    pool.tensor_copy(sel_now[:], select[:, bass.ds(g * P, P)]).then_inc(staged, 1)

            each_group(pool, stage)

        @block.tensor
        def _(pe):
            pe.nop().then_inc(k_turned, SLOTS * items)
            pe.nop().then_inc(scored, 2)
            pe.nop().then_inc(probs_turned, 2)
            pe.nop().then_inc(v_used, SLOTS * per)

            def turn(g, c, j):
                n = c + g * nch
                i, filled = slot(g, c)
                b, h = divmod(j, heads)
                if h == 0:
                    pe.wait_ge(k_in[i][b], filled * 64)
                pe.wait_ge(kT_copied, n * items + j + 1)
                for p in range(PPC):
                    last = pe.transpose(tp[j % 2][:, p * P:(p + 1) * P], k_rows[i][:, b, p, h * DH:(h + 1) * DH], kept.ident)
                last.then_inc(k_turned, 1)

            def score(g, c, j):
                n = c + g * nch
                b, h = divmod(j, heads)
                to = sc[parity(g, c)]
                if j == 0:
                    pe.wait_ge(sc_read, n + 1)
                    if c == 0:
                        pe.wait_ge(staged, (1 if select is None else 2) * (g + 1))
                    if select is not None:
                        pe.matmul(to[:], sel_now[:], dropped_keys(data(c)), start=True, stop=False, skip_group_check=True)
                pe.wait_ge(kT_copied, n * items + j + 3)
                pe.matmul(to[b * stride:(b + 1) * stride, :], q_now[:, b, h, :], kT[j % 2][:],
                          start=(select is None and h == 0), stop=(h == heads - 1), skip_group_check=True,
                          tile_position=(0, b * stride)).then_inc(scored, 1)

            def turn_probs(g, c):
                n = c + g * nch
                pe.wait_ge(probs, n + 3)
                pe.wait_ge(pT_copied, n + 1)
                for p in range(PPC):
                    last = pe.transpose(qp[:, p, :], prob[parity(g, c)][:, p * P:(p + 1) * P], kept.ident)
                last.then_inc(probs_turned, 1)

            def values(g, c):
                n = c + g * nch
                i, filled = slot(g, c)
                at = parity(g, c)
                pe.wait_ge(pT_copied, n + 2)
                if c == 0:
                    pe.wait_ge(new_acc, 2)
                pe.wait_ge(acc_done, n + 1)
                for b in range(per):
                    if stick:
                        pe.wait_ge(v_in[i][b], filled * 64)
                    for p in range(PPC):
                        last = pe.matmul(pv[at][b * stride:(b + 1) * stride, 0:width], pT[at][:, p, b * stride:(b + 1) * stride],
                                         v_rows[i][:, b, p, :], start=(p == 0), stop=(p == PPC - 1), skip_group_check=True,
                                         tile_position=(0, b * stride))
                    last.then_inc(v_used, 1)

            for g in range(groups):
                if select is not None:
                    pe.matmul(sc_new[:, g, :], select[:, g * P:(g + 1) * P], dropped_keys(None), start=True, stop=False, skip_group_check=True)
                for j in range(items):
                    b, h = divmod(j, heads)
                    gb = g * per + b
                    last = pe.matmul(sc_new[b * stride:(b + 1) * stride, g, :], q[:, gb, h, :], k_new[:, h, gb * NT:(gb + 1) * NT],
                                     start=(select is None and h == 0), stop=(h == heads - 1), skip_group_check=True,
                                     tile_position=(0, b * stride))
            last.then_inc(new_scored, 1)
            pe.wait_ge(new_prob, groups if not stick else 1)
            for g in range(groups):
                last = pe.transpose(qp[:, g, :], prob_new[:, g, :], kept.ident)
            last.then_inc(new_turned, 1)
            pe.wait_ge(new_copied, 1)
            pe.wait_ge(small_in, 16)
            for g in range(groups):
                at = g % per_bank * width
                for b in range(per):
                    last = pe.matmul(pv[g // per_bank][b * stride:(b + 1) * stride, at:at + width], pT_new[:, g, b * stride:(b + 1) * stride],
                                     v_new[:, g * per + b, :], start=True, stop=True, skip_group_check=True, tile_position=(0, b * stride))
            last.then_inc(new_summed, 1)

            late = items - max(1, items // 4)

            def group(g):
                for c in range(nch):
                    for j in range(items + 1):
                        if j < items:
                            turn(g, c, j)
                        if j:
                            score(g, c, j - 1)
                        if c and j == late:
                            turn_probs(g, c - 1)
                    if c:
                        values(g, c - 1)
                turn_probs(g, nch - 1)
                values(g, nch - 1)

            each_group(pe, group)
            pe.wait_ge(acc_ready, 1)
            for g in range(groups):
                for h in range(heads):
                    i = g * heads + h
                    last = pe.transpose(tp[i // 4][:, i % 4 * P:(i % 4 + 1) * P], acc[:, g, h * DH:(h + 1) * DH], kept.ident)
            last.then_inc(acc_turned, 1)

        @block.scalar
        def _(act):
            act.preload_act_table_set("natural_log_exp_and_others")
            act.nop().then_inc(kT_copied, 2)
            act.nop().then_inc(probs, 2)
            if not stick:
                act.wait_ge(zeroed, 2)
                for b in range(per):
                    for t in range(NT):
                        act.dma_start(bias[b * stride + t:b * stride + t + 41:8, :],
                                      io.line[bias_rows:bias_rows + 6, bias_first + NT - 1 - t:bias_first + NT - 1 - t + past + NT]).then_inc(bias_in, 16)
                act.wait_ge(maxed, 1)
                for g in range(groups):
                    act.activation(prob_new[:, g, 0:NT], log_new[:, g, :], ACT.Exp, bias=nmax[:, g, 0:1],
                                   accum_out=sums[:, g, 0:1]).then_inc(new_prob, 1)
            else:
                act.wait_ge(new_scored, 1)
                act.activation(soft_new[:], sc_new[:], ACT.Abs).then_inc(step_act, 1)
                act.wait_ge(step_act, 1)
                act.activation(soft_new[:], soft_new[:], ACT.Exp, scale=-1.0).then_inc(step_act, 1)
                act.wait_ge(step_act, 2)
                act.activation(soft_new[:], soft_new[:], ACT.Ln, bias=1.0).then_inc(step_act, 1)
                act.wait_ge(step_dve, 2 + groups + 1)
                act.wait_ge(zeroed, 1)
                act.activation(prob_new[:, :, 0:NT], log_new[:], ACT.Exp).then_inc(step_act, 1)

            def copy_key(g, c, j):
                n = c + g * nch
                act.wait_ge(k_turned, n * items + j + 1 + SLOTS * items)
                act.wait_ge(scored, n * items + j + 1)
                act.copy(kT[j % 2][:], tp[j % 2][:]).then_inc(kT_copied, 1)

            def exps(g, c):
                n = c + g * nch
                act.wait_ge(maxed, n + 2)
                at = parity(g, c)
                one = lambda x, k: x[:, bass.ds(g, 1), k:k + 1].rearrange("p o k -> p (o k)")
                act.activation(prob[at][:], prob[at][:], ACT.Exp, bias=one(nmax, c + 1), accum_out=one(sums, c + 1)).then_inc(probs, 1)
                act.activation(one(shrink, c + 1), one(nmax, c), ACT.Exp, bias=one(nmax, c + 1), scale=-1.0).then_inc(shrunk, 1)

            def soften(g, c, part):
                n = c + g * nch
                at = parity(g, c)
                if part == 0:
                    act.wait_ge(scored, (n + 1) * items + 2)
                    act.wait_ge(soft_done, n + 1)
                    act.activation(soft[at][:], sc[at][:], ACT.Abs).then_inc(soft_step, 1)
                elif part == 1:
                    act.wait_ge(soft_step, n * 3 + 1)
                    act.activation(soft[at][:], soft[at][:], ACT.Exp, scale=-1.0).then_inc(soft_step, 1)
                elif part == 2:
                    act.wait_ge(soft_step, n * 3 + 2)
                    act.activation(soft[at][:], soft[at][:], ACT.Ln, bias=1.0).then_inc(soft_step, 1)
                else:
                    act.wait_ge(soft_done, n + 2)
                    act.activation(prob[at][:], prob[at][:], ACT.Exp).then_inc(probs, 1)

            when = {0: 0, 1: 1, 2: 2, 3: 8} if stick else {0: 1}

            def group(g):
                for c in range(nch):
                    for j in range(items):
                        copy_key(g, c, j)
                        for part, after in when.items():
                            if c and after == j:
                                soften(g, c - 1, part) if stick else exps(g, c - 1)
                for part in when:
                    soften(g, nch - 1, part) if stick else exps(g, nch - 1)

            each_group(act, group)
            if not stick:
                for g in range(groups):
                    act.activation(share[:, g, :], nmax[:, g, :], ACT.Exp, bias=nmax[:, g, nch:nch + 1], scale=-1.0).then_inc(step_act, 1)

        @block.vector
        def _(dve):
            dve.nop().then_inc(pT_copied, 1)
            dve.nop().then_inc(acc_done, 2)
            dve.nop().then_inc(sc_read, 2)
            strict = kept.consts[:, C_STRICT:C_STRICT + NT]
            if stick:
                dve.nop().then_inc(soft_done, 1)
                dve.wait_ge(step_act, 3)
                dve.scalar_tensor_tensor(soft_new[:], sc_new[:], 0.0, soft_new[:], ALU.max, ALU.add).then_inc(step_dve, 1)
                dve.wait_ge(step_dve, 1)
                dve.tensor_tensor(soft_new[:], soft_new[:], strict.unsqueeze(1).to_broadcast([P, groups, NT]), ALU.mult).then_inc(step_dve, 1)
                dve.wait_ge(step_dve, 2)
                for g in range(groups):
                    back = soft_new[:, g, ::-1]
                    dve.tensor_tensor_scan(back, back, back, 0.0, ALU.add, ALU.bypass).then_inc(step_dve, 1)
                dve.wait_ge(step_dve, 2 + groups)
                dve.tensor_tensor(log_new[:], sc_new[:], soft_new[:], ALU.subtract).then_inc(step_dve, 1)
                dve.wait_ge(step_act, 4)
                dve.tensor_tensor(prob_new[:, :, 0:NT], prob_new[:, :, 0:NT], strict.unsqueeze(1).to_broadcast([P, groups, NT]), ALU.mult).then_inc(new_prob, 1)
            else:
                dve.wait_ge(bias_in, 16 * per * NT)
                if mask_last is not None:
                    lo, mcol = mask_last
                    dve.tensor_tensor(bias[:, lo:lo + NT], bias[:, lo:lo + NT], kept.consts[:, mcol:mcol + NT], ALU.add).then_inc(step_dve, 1)
                else:
                    dve.nop().then_inc(step_dve, 1)
                dve.tensor_tensor(bias[:, past:], bias[:, past:], kept.consts[:, C_NM:C_NM + NT], ALU.add).then_inc(step_dve, 1)
                dve.wait_ge(step_dve, 2)
                dve.wait_ge(new_scored, 1)
                dve.tensor_tensor(log_new[:], sc_new[:], bias[:, past:].unsqueeze(1).to_broadcast([P, groups, NT]), ALU.add).then_inc(step_dve, 1)
                dve.wait_ge(step_dve, 3)
                dve.tensor_reduce(nmax[:, :, 0], log_new[:], AX.X, ALU.max, negate=True).then_inc(maxed, 1)
            dve.wait_ge(new_turned, 1)
            dve.tensor_copy(pT_new[:], qp[0:NT, 0:groups, :]).then_inc(new_copied, 1)
            dve.wait_ge(new_summed, 1)
            half = groups // 2
            for i in range(2):
                dve.tensor_copy(acc[:, i * half:(i + 1) * half, :], pv[i][:].rearrange("p (g c) -> p g c", c=width)).then_inc(new_acc, 1)
            dve.wait_ge(new_acc, 2)

            def limit(g, c):
                n = c + g * nch
                at = parity(g, c)
                here = slice(data(c) * CH, (data(c) + 1) * CH)
                one = lambda x, k: x[:, bass.ds(g, 1), k:k + 1].rearrange("p o k -> p (o k)")
                dve.wait_ge(scored, (n + 1) * items + 2)
                dve.wait_ge(probs_turned, n + 1)
                dve.tensor_tensor(prob[at][:], sc[at][:], bias[:, here], ALU.add).then_inc(sc_read, 1)
                dve.wait_ge(sc_read, n + 3)
                dve.tensor_reduce(one(nstep, c + 1), prob[at][:], AX.X, ALU.max, negate=True).then_inc(step_dve, 1)
                dve.wait_ge(step_dve, n + 4)
                dve.wait_ge(maxed, n + 1)
                dve.tensor_tensor(one(nmax, c + 1), one(nstep, c + 1), one(nmax, c), ALU.min).then_inc(maxed, 1)

            def sum_back(g, c):
                n = c + g * nch
                at = parity(g, c)
                carried = soft[1 - at][:, 0:1] if c else soft_new[:, g, 0:1]
                dve.wait_ge(soft_step, n * 3 + 3)
                k = n * 2 + 2 + groups + 1
                dve.scalar_tensor_tensor(soft[at][:], sc[at][:], 0.0, soft[at][:], ALU.max, ALU.add).then_inc(step_dve, 1)
                dve.wait_ge(step_dve, k + 1)
                dve.tensor_tensor_scan(soft[at][:, ::-1], soft[at][:, ::-1], soft[at][:, ::-1], carried, ALU.add, ALU.bypass).then_inc(step_dve, 1)
                dve.wait_ge(step_dve, k + 2)
                dve.wait_ge(probs_turned, n + 1)
                dve.tensor_tensor(prob[at][:], sc[at][:], soft[at][:], ALU.subtract).then_inc(sc_read, 1)
                dve.wait_ge(sc_read, n + 3)
                dve.nop().then_inc(soft_done, 1)

            def copy_probs(g, c):
                n = c + g * nch
                dve.wait_ge(probs_turned, n + 3)
                dve.wait_ge(v_used, (n - 1 + SLOTS) * per)
                dve.tensor_copy(pT[parity(g, c)][:], qp[:]).then_inc(pT_copied, 1)

            def add_up(g, c):
                n = c + g * nch
                dve.wait_ge(v_used, (n + 1 + SLOTS) * per)
                to = acc[:, bass.ds(g, 1), :].rearrange("p o c -> p (o c)")
                new = pv[parity(g, c)][:, 0:width]
                dve.wait_ge(acc_done, n + 2)
                if stick:
                    dve.tensor_tensor(to, to, new, ALU.add).then_inc(acc_done, 1)
                else:
                    dve.wait_ge(shrunk, n + 1)
                    by = shrink[:, bass.ds(g, 1), c + 1:c + 2].rearrange("p o k -> p (o k)")
                    dve.scalar_tensor_tensor(to, to, by, new, ALU.mult, ALU.add).then_inc(acc_done, 1)

            def best(rounds):
                for i in rounds:
                    if i:
                        dve.wait_ge(top_step, i * 2)
                    dve.max(top8[:], kept.scores[:]).then_inc(top_step, 1)
                    dve.wait_ge(top_step, i * 2 + 1)
                    dve.match_replace(kept.scores[:], top8[:], kept.scores[:], GONE).then_inc(top_step, 1)

            def group(g):
                for c in range(nch):
                    if not stick:
                        if c:
                            copy_probs(g, c - 1)
                        limit(g, c)
                        if c:
                            add_up(g, c - 1)
                    else:
                        first = (g * nch + c) * 2
                        if c:
                            sum_back(g, c - 1)
                        best([first])
                        if c:
                            copy_probs(g, c - 1)
                        best([first + 1])
                        if c:
                            add_up(g, c - 1)
                if stick:
                    sum_back(g, nch - 1)
                copy_probs(g, nch - 1)
                add_up(g, nch - 1)

            each_group(dve, group, unroll=stick)
            if stick:
                dve.wait_ge(top_step, TOPK_S // 4)
                dve.tensor_scalar(kept.drop[:], kept.scores[:], GONE / 2, NEG, ALU.is_gt, ALU.mult)
                dve.wait_ge(acc_done, groups * nch + 2)
                dve.nop().then_inc(acc_ready, 1)
            else:
                k = groups * nch + 3
                dve.wait_ge(step_act, groups)
                dve.wait_ge(probs, groups * nch + 2)
                dve.wait_ge(new_prob, groups)
                dve.tensor_tensor(sums[:], sums[:], share[:], ALU.mult).then_inc(step_dve, 1)
                dve.wait_ge(step_dve, k + 1)
                dve.tensor_reduce(rcp[:], sums[:], AX.X, ALU.add).then_inc(step_dve, 1)
                dve.wait_ge(step_dve, k + 2)
                dve.tensor_scalar(rcp[:], rcp[:], 1e-30, None, ALU.max).then_inc(step_dve, 1)
                dve.wait_ge(step_dve, k + 3)
                dve.reciprocal(rcp[:], rcp[:]).then_inc(step_dve, 1)
                dve.wait_ge(step_dve, k + 4)
                if gate is not None:
                    dve.tensor_tensor(rcp[:], rcp[:], kept.gates[:, :, gate], ALU.mult).then_inc(step_dve, 1)
                    dve.wait_ge(step_dve, k + 5)
                dve.wait_ge(acc_done, groups * nch + 2)
                dve.tensor_tensor(acc[:], acc[:], rcp[:].unsqueeze(2).to_broadcast([P, groups, width]), ALU.mult).then_inc(acc_ready, 1)
            dve.wait_ge(acc_turned, 1)
            each = (stride // heads) // NT if stick else 3
            for g in range(groups):
                for h in range(heads):
                    i = g * heads + h
                    n = each * NT
                    got = tp[i // 4][:, i % 4 * P:(i % 4 + 1) * P].rearrange("p (b r) -> p b r", b=per)[:, :, h * n:(h + 1) * n]
                    got = got.rearrange("p b (j t) -> p b j t", t=NT)
                    to = kept.oTs[:, head0 + h * each:head0 + (h + 1) * each, g * per * NT:(g + 1) * per * NT].rearrange("p j (b t) -> p b j t", t=NT)
                    if add:
                        last = dve.tensor_tensor(to, to, got, ALU.add)
                    else:
                        last = dve.tensor_copy(to, got)
            last.then_inc(out_done, 1)


def stick_breaking(nc, io, kept):
    stream(nc, io, kept, "sb", cache=io.sb_cache, col=0, proj_v=SB_V, heads=4, per=4, q=kept.q_sb, k_new=kept.k_sb,
           head0=0, stick=True)


def dsa_sample(nc, io, kept):
    def keys(c):
        return kept.drop[:, PAST:KEYS] if c is None else kept.drop[:, c * CH:(c + 1) * CH]

    stream(nc, io, kept, "dsa", cache=io.dsa_cache, col=0, proj_v=DSA_V, heads=2, per=2, q=kept.q_dsa, k_new=kept.k_dsa,
           select=kept.sel_d, dropped_keys=keys, bias_rows=0, head0=4)


def cmp_sample(nc, io, kept):
    with ExitStack() as ctx:
        s = Scope(nc, ctx, "ca")
        bias = s.sb("bias", [P, PAST])
        prob = s.sb("prob", [P, 4, NC])
        gated = s.sb("gated", [P, 4, NC])
        pT = s.sb("pT", [P, 4, P])
        nmax, sums, rcp = s.sb("nmax", [P, 4]), s.sb("sums", [P, 4]), s.sb("rcp", [P, 4])
        imp = s.sb("imp", [P, NSB])
        top8 = s.sb("top8", [P, 8])
        sc = s.ps("sc", [P, 4, NC])
        ip = s.ps("ip", [P, NC])
        tp = s.ps("tp", [P, 4, P])
        ov = s.ps("ov", [P, 4, P])
        zeroed, bias_in, scored, step, exped, normed, gate_done, imp_summed, turned, copied, out_summed, out_done = (
            s.sem(n) for n in ("zeroed", "bias_in", "scored", "step", "exped", "normed", "gate_done", "imp_summed", "turned",
                               "copied", "out_summed", "out_done"))
        block = ctx.enter_context(nc.Block())

        @block.gpsimd
        def _(pool):
            pool.memset(bias[:], 0.0).then_inc(zeroed, 1)

        @block.sync
        def _(sp):
            sp.wait_ge(zeroed, 1)
            for b in range(2):
                for t in range(NT):
                    sp.dma_start(bias[b * 64 + t:b * 64 + t + 41:8, :], io.line[6:12, NT - 1 - t:NT - 1 - t + PAST]).then_inc(bias_in, 16)

        @block.tensor
        def _(pe):
            for g in range(4):
                for j in range(4):
                    b, kv = divmod(j, 2)
                    last = pe.matmul(sc[b * 64:b * 64 + 64, g, :], kept.q_nsa[:, 2 * g + b, kv, :], kept.cmp_k[:, 2 * g + b, kv, :],
                                     start=(kv == 0), stop=(kv == 1), skip_group_check=True, tile_position=(0, b * 64))
            last.then_inc(scored, 1)
            pe.wait_ge(normed, 1)
            for g in range(4):
                last = pe.matmul(ip[:], kept.consts[:, C_SELG + g * P:C_SELG + (g + 1) * P], prob[:, g, :], start=(g == 0), stop=(g == 3))
            last.then_inc(imp_summed, 1)
            pe.wait_ge(gate_done, 1)
            for g in range(4):
                last = pe.transpose(tp[:, g, :], gated[:, g, :], kept.ident)
            last.then_inc(turned, 1)
            pe.wait_ge(copied, 1)
            for g in range(4):
                for j in range(4):
                    b, kv = divmod(j, 2)
                    r = b * 64 + kv * 24
                    last = pe.matmul(ov[:, g, r:r + 24], kept.cmp_v[:, 2 * g + b, kv, :], pT[:, g, r:r + 24], start=True, stop=True, skip_group_check=True)
            last.then_inc(out_summed, 1)

        @block.scalar
        def _(act):
            act.wait_ge(step, 2)
            for g in range(4):
                last = act.activation(prob[:, g, :], prob[:, g, :], ACT.Exp, bias=nmax[:, g:g + 1], accum_out=sums[:, g:g + 1])
            last.then_inc(exped, 1)
            act.wait_ge(turned, 1)
            act.copy(pT[:], tp[:]).then_inc(copied, 1)

        @block.vector
        def _(dve):
            dve.wait_ge(bias_in, 16 * 16)
            dve.wait_ge(scored, 1)
            ends = bias[:, CMPB - 1::CMPB].unsqueeze(1).to_broadcast([P, 4, NC])
            dve.tensor_tensor(prob[:], sc[:], ends, ALU.add).then_inc(step, 1)
            dve.wait_ge(step, 1)
            dve.tensor_reduce(nmax[:], prob[:], AX.X, ALU.max, negate=True).then_inc(step, 1)
            dve.wait_ge(exped, 1)
            dve.tensor_scalar(rcp[:], sums[:], 1e-30, None, ALU.max).then_inc(step, 1)
            dve.wait_ge(step, 3)
            dve.reciprocal(rcp[:], rcp[:]).then_inc(step, 1)
            dve.wait_ge(step, 4)
            dve.tensor_tensor(prob[:], prob[:], rcp[:].unsqueeze(2).to_broadcast([P, 4, NC]), ALU.mult).then_inc(normed, 1)
            dve.wait_ge(normed, 1)
            dve.tensor_tensor(gated[:], prob[:], kept.gates[:, :, 0:1].to_broadcast([P, 4, NC]), ALU.mult).then_inc(gate_done, 1)
            dve.memset(imp[:], 1e4).then_inc(step, 1)
            dve.wait_ge(imp_summed, 1)
            dve.wait_ge(step, 5)
            dve.tensor_reduce(imp[:, 1:NSB - 2], ip[:].rearrange("p (n a) -> p n a", a=2)[:, 1:NSB - 2, :], AX.X, ALU.add).then_inc(step, 1)
            for n in range(SLC_TOPN // 8):
                dve.wait_ge(step, 6 + 2 * n)
                dve.max(top8[:], imp[:]).then_inc(step, 1)
                dve.wait_ge(step, 7 + 2 * n)
                dve.match_replace(imp[:], top8[:], imp[:], GONE).then_inc(step, 1)
            dve.wait_ge(step, 10)
            dve.tensor_scalar(kept.drop_blk[:], imp[:], GONE / 2, NEG, ALU.is_gt, ALU.mult).then_inc(step, 1)
            dve.wait_ge(out_summed, 1)
            for b in range(NB):
                r = b % 2 * 64
                last = dve.tensor_copy(kept.oTs[:, 10:16, b * NT:(b + 1) * NT], ov[:, b // 2, r:r + 48].rearrange("p (h t) -> p h t", t=NT))
            last.then_inc(out_done, 1)


def slc_sample(nc, io, kept):
    def keys(c):
        if c is None:
            return kept.drop_blk[:, NSB - 1:NSB].to_broadcast([P, NT])
        return kept.drop_blk[:, c * 8:(c + 1) * 8].unsqueeze(2).to_broadcast([P, 8, SLCB])

    stream(nc, io, kept, "slc", cache=io.nsa_cache, col=512, proj_v=NSA_VS, heads=2, per=2, q=kept.q_nsa, k_new=kept.k_slc,
           select=kept.sel_e, dropped_keys=keys, bias_rows=6, head0=10, gate=1, add=True)


def win_sample(nc, io, kept):
    stream(nc, io, kept, "win", cache=None, state=io.win_state, col=0, proj_v=NSA_VW, heads=2, per=2, q=kept.q_nsa,
           k_new=kept.k_win, bias_rows=6, bias_first=PAST - WIN, mask_last=(0, C_WM), head0=10, gate=2, add=True)


def prompt_prepare(nc, io, kept, keep):
    kept.qT = keep.sb("qT", [P, 16, SEQ])
    kept.kT = keep.sb("kT", [P, 10, SEQ])
    kept.v = keep.sb("v", [P, 4, 10 * DH])
    kept.bias = keep.sb("bias", [P, HB, XW])
    kept.dropp = keep.sb("dropp", [P, 4, SEQ], BF16)
    kept.pgates = keep.sb("pgates", [P, 4, 18])
    kept.pmask = keep.sb("pmask", [P, C_END - C_PM])
    with ExitStack() as ctx:
        s = Scope(nc, ctx, "pp")
        rows = [s.sb(f"rows{i}", [P, 4, 2 * DH]) for i in range(3)]
        iq = s.sb("iq", [64, 4, SEQ])
        ik = s.sb("ik", [64, SEQ])
        iw = s.sb("iw", [P, 4, 4])
        relu = [s.sb(f"relu{i}", [P, SEQ]) for i in range(2)]
        score = s.sb("score", [P, 4, SEQ])
        top8 = s.sb("top8", [P, 3, 8])
        tp = [s.ps(f"tp{i}", [P, SEQ]) for i in range(4)]
        sc = [s.ps(f"sc{i}", [P, SEQ]) for i in range(2)]
        pairs = [SB_Q, SB_Q + 256] + [DSA_Q + 256 * i for i in range(3)] + [NSA_Q + 256 * i for i in range(3)]
        n_q = len(pairs)
        pairs += [SB_K, SB_K + 256, DSA_K, NSA_KS, NSA_KW, IDX_Q, IDX_K]
        n_full = len(pairs) - 2
        rows_in = [s.sem(f"rows_in{i}") for i in range(3)]
        v_in, bias_in, small_in, mask_in = s.sem("v_in"), s.sem("bias_in"), s.sem("small_in"), s.sem("mask_in")
        turned, copied_a, copied_d, gated, biased = s.sem("turned"), s.sem("copied_a"), s.sem("copied_d"), s.sem("gated"), s.sem("biased")
        scored, rectified, weighted, top_step, dropped, idx_copied = (s.sem("scored"), s.sem("rectified"), s.sem("weighted"), s.sem("top_step"), s.sem("dropped"), s.sem("idx_copied"))
        block = ctx.enter_context(nc.Block())
        n_items = 2 * len(pairs) - 1
        idx_units = [(i, h) for i in range(1, 4) for h in range(4)]

        @block.sync
        def _(sp):
            for i, col in enumerate(pairs):
                if i >= 3:
                    sp.wait_ge(turned, 2 * (i - 2))
                width = 2 * DH if i < len(pairs) - 1 else DH
                sp.dma_start(rows[i % 3][:, :, 0:width], io.proj[0:SEQ, col:col + width].rearrange("(m p) n -> p m n", p=P)).then_inc(rows_in[i % 3], 16)
            sp.wait_ge(v_in, 16 * 4)
            sp.wait_ge(small_in, 32)

        @block.gpsimd
        def _(pool):
            with nc.allow_non_contiguous_dma(reason="a few numbers per row"):
                pool.dma_start(iw[:], io.proj[0:SEQ, IDX_W:IDX_W + 4].rearrange("(m p) n -> p m n", p=P)).then_inc(small_in, 16)
                pool.dma_start(kept.pgates[:], io.proj[0:SEQ, NSA_BG:NSA_BG + 18].rearrange("(m p) n -> p m n", p=P)).then_inc(small_in, 16)

        @block.scalar
        def _(act):
            act.preload_act_table_set("natural_log_exp_and_others")
            act.dma_start(kept.pmask[:], io.consts[:, C_PM:C_END]).then_inc(mask_in, 16)
            src = bass.AP(io.lines.tensor, P - 1, [[HB * XL - 1, P], [XL, HB], [1, XW]])
            act.dma_start(kept.bias[:], src).then_inc(bias_in, 16)
            for to, col, n in ((0, SB_V, 4), (4, DSA_V, 2), (6, NSA_VS, 2), (8, NSA_VW, 2)):
                act.dma_start(kept.v[:, :, to * DH:(to + n) * DH], io.proj[0:SEQ, col:col + n * DH].rearrange("(m p) n -> p m n", p=P)).then_inc(v_in, 16)
            for n in range(1, 2 * n_full, 2):
                act.wait_ge(turned, n + 1)
                if n // 2 < n_q:
                    act.activation(kept.qT[:, n, :], tp[n % 4][:], ACT.Copy, scale=SCALE).then_inc(copied_a, 1)
                else:
                    act.copy(kept.kT[:, n - 2 * n_q, :], tp[n % 4][:]).then_inc(copied_a, 1)
            act.wait_ge(small_in, 32)
            act.activation(kept.pgates[:], kept.pgates[:], ACT.Exp, scale=-1.0).then_inc(gated, 1)
            for u in range(len(idx_units)):
                i, h = idx_units[u]
                w = (i + 1) * P
                act.wait_ge(scored, u + 1)
                if u >= 2:
                    act.wait_ge(weighted, u - 1)
                act.activation(relu[u % 2][:, 0:w], sc[u % 2][:, 0:w], ACT.Relu).then_inc(rectified, 1)

        @block.tensor
        def _(pe):
            for n in range(n_items):
                i, j = divmod(n, 2)
                if j == 0:
                    pe.wait_ge(rows_in[i % 3], 16 * (i // 3 + 1))
                if n >= 4:
                    pe.wait_ge(copied_a if n % 2 else copied_d, (n - 4) // 2 + 1)
                for m in range(4):
                    last = pe.transpose(tp[n % 4][:, m * P:(m + 1) * P], rows[i % 3][:, m, j * DH:(j + 1) * DH], kept.ident)
                last.then_inc(turned, 1)
            pe.wait_ge(idx_copied, 5)
            for u, (i, h) in enumerate(idx_units):
                w = (i + 1) * P
                if u >= 2:
                    pe.wait_ge(rectified, u - 1)
                pe.matmul(sc[u % 2][:, 0:w], iq[:, h, i * P:(i + 1) * P], ik[:, 0:w], start=True, stop=True).then_inc(scored, 1)

        @block.vector
        def _(dve):
            for n in range(0, 2 * n_full, 2):
                dve.wait_ge(turned, n + 1)
                if n // 2 < n_q:
                    dve.tensor_scalar(kept.qT[:, n, :], tp[n % 4][:], SCALE, None, ALU.mult).then_inc(copied_d, 1)
                else:
                    dve.tensor_copy(kept.kT[:, n - 2 * n_q, :], tp[n % 4][:]).then_inc(copied_d, 1)
            for n in range(2 * n_full, n_items):
                j = n - 2 * n_full
                dve.wait_ge(turned, n + 1)
                for half in range(2 if j < 2 else 1):
                    to = iq[:, 2 * j + half, :] if j < 2 else ik[:]
                    dve.tensor_copy(to, tp[n % 4][64 * half:64 * half + 64, :]).then_inc(idx_copied, 1)
            dve.wait_ge(mask_in, 16)
            dve.wait_ge(small_in, 32)
            pm = kept.pmask[:, 0:XW]
            for u, (i, h) in enumerate(idx_units):
                w = (i + 1) * P
                dve.wait_ge(rectified, u + 1)
                if h:
                    dve.wait_ge(weighted, u)
                before = score[:, i, 0:w] if h else pm[:, SEQ - i * P:SEQ - i * P + w]
                dve.scalar_tensor_tensor(score[:, i, 0:w], relu[u % 2][:, 0:w], iw[:, i, h:h + 1], before, ALU.mult, ALU.add).then_inc(weighted, 1)
            dve.wait_ge(gated, 1)
            dve.tensor_scalar(kept.pgates[:], kept.pgates[:], 1.0, None, ALU.add).then_inc(gated, 1)
            dve.wait_ge(gated, 2)
            dve.reciprocal(kept.pgates[:], kept.pgates[:]).then_inc(gated, 1)
            dve.wait_ge(bias_in, 16)
            dve.tensor_tensor(kept.bias[:], kept.bias[:], pm.unsqueeze(1).to_broadcast([P, HB, XW]), ALU.add).then_inc(biased, 1)
            dve.wait_ge(weighted, len(idx_units))
            for r in range(TOPK_P // 8):
                for i in range(1, 4):
                    dve.max(top8[:, i - 1, :], score[:, i, 0:(i + 1) * P]).then_inc(top_step, 1)
                for i in range(1, 4):
                    dve.wait_ge(top_step, r * 6 + i)
                    dve.match_replace(score[:, i, 0:(i + 1) * P], top8[:, i - 1, :], score[:, i, 0:(i + 1) * P], GONE).then_inc(top_step, 1)
                dve.wait_ge(top_step, r * 6 + 6)
            for i in range(1, 4):
                last = dve.tensor_scalar(kept.dropp[:, i, 0:(i + 1) * P], score[:, i, 0:(i + 1) * P], GONE / 2, NEG, ALU.is_gt, ALU.mult)
            last.then_inc(dropped, 1)


class Unit:

    def __init__(self, kind, out, tile, q, k, v, bias, gate, first, last):
        self.kind, self.out, self.tile, self.q, self.k, self.v = kind, out, tile, q, k, v
        self.bias, self.gate, self.first, self.last = bias, gate, first, last
        self.off = SEQ - tile * P
        self.w = (tile + 1) * P
        self.blocks = self.w // CMPB
        self.u = None


class Links:

    def __init__(self, sem):
        self.sem, self.n = sem, 0

    def step(self, ins):
        self.n += 1
        ins.then_inc(self.sem, 1)
        return self.n


def prompt_attention(nc, io, kept, keep):
    units = []
    for h in range(4):
        for i in range(4):
            units.append(Unit("stick", h, i, h, h, h, None, None, True, True))
    n_stick = len(units)
    for h in range(6):
        for i in range(4):
            units.append(Unit("dsa", 4 + h, i, 4 + h, 4 + h // 3, 4 + h // 3, h, None, True, True))
    for h in range(6):
        for i in range(4):
            units.append(Unit("slc", 10 + h, i, 10 + h, 6 + h // 3, 6 + h // 3, 6 + h, 6 + h, True, False))
            units.append(Unit("win", 10 + h, i, 10 + h, 8 + h // 3, 8 + h // 3, 6 + h, 12 + h, False, False))
            units.append(Unit("cmp", 10 + h, i, 10 + h, h // 3, h // 3, 6 + h, h, False, True))
    N = len(units)
    for u, x in enumerate(units):
        x.u = u
    outs = [x.u for x in units if x.last and x.tile == 3]

    with ExitStack() as ctx:
        s = Scope(nc, ctx, "pa")
        L = [s.sb(f"logits{i}", [P, XW]) for i in range(4)]
        soft = s.sb("soft", [P, SEQ])
        pT = [s.sb(f"pT{i}", [P, 4, P]) for i in range(2)]
        nmax, sums, rcp = s.sb("nmax", [P, N]), s.sb("sums", [P, N]), s.sb("rcp", [P, N])
        sc = [s.ps(f"sc{i}", [P, SEQ]) for i in range(2)]
        tp = [s.ps(f"tp{i}", [P, 4, P]) for i in range(2)]
        ov = [s.ps(f"ov{i}", [P, 4, P]) for i in range(2)]
        cleared, scored, added, padded, maxed, exped, rcp_ready, ready_stick, ready = (
            s.sem(n) for n in ("cleared", "scored", "added", "padded", "maxed", "exped", "rcp_ready", "ready_stick", "ready"))
        turned, copied, multiplied, out_done = s.sem("turned"), [s.sem("copied_even"), s.sem("copied_odd")], s.sem("multiplied"), s.sem("out_done")
        soft_act, soft_dve, small = s.sem("soft_act"), s.sem("soft_dve"), s.sem("small")
        block = ctx.enter_context(nc.Block())
        wins = [x.u for x in units if x.kind == "win"]

        def view(x):
            if x.kind == "cmp":
                return L[x.u % 4][:, 0:x.blocks]
            return L[x.u % 4][:, x.off:x.off + x.w]

        def all_of(x):
            return L[x.u % 4][:, 0:XW] if x.kind == "win" else view(x)

        @block.tensor
        def _(pe):
            def score(x):
                if x.u >= 2:
                    pe.wait_ge(added, x.u - 1)
                q = kept.qT[:, x.q, x.tile * P:(x.tile + 1) * P]
                if x.kind == "cmp":
                    pe.matmul(sc[x.u % 2][:, 0:x.blocks], q, kept.cmp_kp[:, x.k, 0:x.blocks], start=True, stop=True).then_inc(scored, 1)
                    return
                dropping = x.kind == "dsa" and x.tile > 0
                if dropping:
                    pe.matmul(sc[x.u % 2][:, 0:x.w], kept.ident_b[:], kept.dropp[:, x.tile, 0:x.w], start=True, stop=False)
                pe.matmul(sc[x.u % 2][:, 0:x.w], q, kept.kT[:, x.k, 0:x.w], start=not dropping, stop=True).then_inc(scored, 1)

            def turn(x):
                if x.kind == "stick":
                    pe.wait_ge(ready_stick, x.u + 1)
                else:
                    pe.wait_ge(ready, x.u - n_stick + 1)
                if x.u >= 2:
                    pe.wait_ge(copied[x.u % 2], x.u // 2)
                if x.kind == "cmp":
                    last = pe.transpose(tp[x.u % 2][:, 0, :], L[x.u % 4][:, 0:P], kept.ident)
                else:
                    for j in range(x.tile + 1):
                        last = pe.transpose(tp[x.u % 2][:, j, :], view(x)[:, j * P:(j + 1) * P], kept.ident)
                last.then_inc(turned, 1)

            def product(x):
                pe.wait_ge(copied[x.u % 2], x.u // 2 + 1)
                if x.tile == 0 and x.first and x.out >= 2:
                    pe.wait_ge(out_done, x.out - 1)
                to = ov[x.out % 2][:, x.tile, :]
                if x.kind == "cmp":
                    last = pe.matmul(to, kept.cmp_vp[0:x.blocks, x.v, :], pT[x.u % 2][0:x.blocks, 0, :], start=False, stop=True, skip_group_check=True)
                else:
                    for j in range(x.tile + 1):
                        last = pe.matmul(to, kept.v[:, j, x.v * DH:(x.v + 1) * DH], pT[x.u % 2][:, j, :],
                                         start=(x.first and j == 0), stop=(x.last and j == x.tile), skip_group_check=True)
                last.then_inc(multiplied, 1)

            pe.wait_ge(cleared, 4)
            for u in range(N + 3):
                if u < N:
                    score(units[u])
                if 2 <= u < N + 2:
                    turn(units[u - 2])
                if u >= 3:
                    product(units[u - 3])

        def copy(eng, x):
            eng.wait_ge(turned, x.u + 1)
            if x.u >= 2:
                eng.wait_ge(multiplied, x.u - 1)
            do = eng.copy if x.u % 2 else eng.tensor_copy
            n = 1 if x.kind == "cmp" else x.tile + 1
            rows = x.blocks if x.kind == "cmp" else P
            do(pT[x.u % 2][0:rows, 0:n, :], tp[x.u % 2][0:rows, 0:n, :]).then_inc(copied[x.u % 2], 1)

        @block.gpsimd
        def _(pool):
            for i in range(4):
                pool.memset(L[i][:], 0.0).then_inc(cleared, 1)
            pool.wait_ge(cleared, 4)

            def normalise(x):
                if x.kind == "stick":
                    return
                pool.wait_ge(rcp_ready, x.u - n_stick + 1)
                v = view(x)
                pool.tensor_scalar(v, v, rcp[:, x.u:x.u + 1], 1.0, ALU.mult, ALU.mult).then_inc(ready, 1)

            for u in range(N + 1):
                if u < N and units[u].kind == "win":
                    pool.wait_ge(turned, u - 3)
                    x = units[u]
                    if x.off:
                        pool.tensor_copy(L[u % 4][:, 0:x.off], kept.bias[:, x.bias, 0:x.off]).then_inc(padded, 1)
                if u:
                    normalise(units[u - 1])

        @block.scalar
        def _(act):
            act.preload_act_table_set("natural_log_exp_and_others")
            chain = Links(soft_act)

            def exp(x):
                if x.kind == "stick":
                    act.wait_ge(scored, x.u + 1)
                    if x.u:
                        act.wait_ge(soft_dve, 4 * x.u)
                    t = soft[:, 0:x.w]
                    act.wait_ge(soft_act, chain.step(act.activation(t, sc[x.u % 2][:, 0:x.w], ACT.Abs)))
                    act.wait_ge(soft_act, chain.step(act.activation(t, t, ACT.Exp, scale=-1.0)))
                    chain.step(act.activation(t, t, ACT.Ln, bias=1.0))
                    return
                act.wait_ge(maxed, x.u - n_stick + 1)
                act.activation(all_of(x), all_of(x), ACT.Exp, bias=nmax[:, x.u:x.u + 1], accum_out=sums[:, x.u:x.u + 1]).then_inc(exped, 1)

            def exp_stick(x):
                act.wait_ge(soft_dve, 4 * x.u + 4)
                act.activation(view(x), view(x), ACT.Exp).then_inc(exped, 1)

            for u in range(N + 3):
                if 1 <= u <= n_stick:
                    exp_stick(units[u - 1])
                if u < N:
                    exp(units[u])
                if 2 <= u < N + 2 and u % 2:
                    copy(act, units[u - 2])

        @block.vector
        def _(dve):
            chain = Links(small)
            tri = kept.pmask[:, C_TRI - C_PM:C_TRI - C_PM + P]
            dve.wait_ge(cleared, 4)

            def add(x):
                if x.u >= 4:
                    dve.wait_ge(turned, x.u - 3)
                v = view(x)
                if x.kind == "stick":
                    t = soft[:, 0:x.w]
                    z = sc[x.u % 2][:, 0:x.w]
                    dve.wait_ge(soft_act, 3 * x.u + 3)
                    dve.scalar_tensor_tensor(t, z, 0.0, t, ALU.max, ALU.add).then_inc(soft_dve, 1)
                    dve.wait_ge(soft_dve, 4 * x.u + 1)
                    d = soft[:, x.w - P:x.w]
                    dve.tensor_tensor(d, d, tri, ALU.mult).then_inc(soft_dve, 1)
                    dve.wait_ge(soft_dve, 4 * x.u + 2)
                    dve.tensor_tensor_scan(t[:, ::-1], t[:, ::-1], t[:, ::-1], 0.0, ALU.add, ALU.bypass).then_inc(soft_dve, 1)
                    dve.wait_ge(soft_dve, 4 * x.u + 3)
                    dve.tensor_tensor(v, z, t, ALU.subtract).then_inc(soft_dve, 1)
                    dve.wait_ge(soft_dve, 4 * x.u + 4)
                    dve.nop().then_inc(added, 1)
                    return
                dve.wait_ge(scored, x.u + 1)
                if x.kind == "cmp":
                    b = kept.bias[:, x.bias, x.off + CMPB - 1:x.off + x.w:CMPB]
                    dve.tensor_tensor(v, sc[x.u % 2][:, 0:x.blocks], b, ALU.add).then_inc(added, 1)
                else:
                    dve.tensor_tensor(v, sc[x.u % 2][:, 0:x.w], kept.bias[:, x.bias, x.off:x.off + x.w], ALU.add).then_inc(added, 1)
                dve.wait_ge(added, x.u + 1)
                if x.kind == "win":
                    dve.wait_ge(padded, wins.index(x.u) + 1)
                dve.tensor_reduce(nmax[:, x.u:x.u + 1], all_of(x), AX.X, ALU.max, negate=True).then_inc(maxed, 1)

            def invert(x):
                dve.wait_ge(exped, x.u + 1)
                if x.kind == "stick":
                    d = view(x)[:, x.w - P:x.w]
                    dve.tensor_tensor(d, d, tri, ALU.mult).then_inc(ready_stick, 1)
                    return
                r = rcp[:, x.u:x.u + 1]
                if x.kind == "cmp" and x.tile == 0:
                    v = view(x)
                    cm = kept.pmask[:, C_CM - C_PM:C_CM - C_PM + x.blocks]
                    dve.wait_ge(small, chain.step(dve.scalar_tensor_tensor(v, v, 1.0, cm, ALU.mult, ALU.mult, accum_out=sums[:, x.u:x.u + 1])))
                dve.wait_ge(small, chain.step(dve.tensor_scalar(r, sums[:, x.u:x.u + 1], 1e-30, None, ALU.max)))
                if x.gate is None:
                    dve.reciprocal(r, r).then_inc(rcp_ready, 1)
                else:
                    dve.wait_ge(small, chain.step(dve.reciprocal(r, r)))
                    dve.tensor_tensor(r, r, kept.pgates[:, x.tile, x.gate:x.gate + 1], ALU.mult).then_inc(rcp_ready, 1)

            for u in range(N + 4):
                if u < N:
                    add(units[u])
                if 1 <= u <= N:
                    invert(units[u - 1])
                if 2 <= u < N + 2 and u % 2 == 0:
                    copy(dve, units[u - 2])
                if u - 4 in outs:
                    dve.wait_ge(multiplied, u - 3)
                    h = units[u - 4].out
                    dve.tensor_copy(kept.oT[:, h, :].rearrange("p (m t) -> p m t", m=4), ov[h % 2][:]).then_inc(out_done, 1)


def finish(nc, io, kept, keep):
    with ExitStack() as ctx:
        s = Scope(nc, ctx, "fin")
        w = s.sb("w", [P, 16, D])
        gate = s.sb("gate", [P, D])
        sig = s.sb("sig", [P, D])
        gain = s.sb("gain", [P, D])
        x, y = gate, sig
        sq = s.sb("sq", [P, CH])
        ss, rstd = s.sb("ss", [P, 5, 4]), s.sb("rstd", [P, 5])
        tp = [s.ps(f"tp{i}", [P, 4, P]) for i in range(2)]
        yp = [s.ps(f"yp{i}", [P, CH]) for i in range(4)]
        w_in, gain_in, gate_in, x_in = s.sem("w_in"), s.sem("gain_in"), s.sem("gate_in"), s.sem("x_in")
        sig_exp, sig_step, gate_ready, turned, gated = s.sem("sig_exp"), s.sem("sig_step"), s.sem("gate_ready"), s.sem("turned"), s.sem("gated")
        projected, squared, moved, var, rooted, scaled, summed, stored = (
            s.sem(n) for n in ("projected", "squared", "moved", "var", "rooted", "scaled", "summed", "stored"))
        block = ctx.enter_context(nc.Block())
        rows = [P, P, P, P, NS]
        first_rows = [0, P, 2 * P, 3 * P, SEQ]

        def heads_at(m, h, n):
            return kept.oT[:, h:h + n, m * P:(m + 1) * P] if m < 4 else kept.oTs[:, h:h + n, :]

        @block.sync
        def _(sp):
            for m in range(5):
                if m:
                    sp.wait_ge(turned, 4 * m)
                r = slice(first_rows[m], first_rows[m] + rows[m])
                sp.dma_start(gate[0:rows[m], 0:512], io.proj[r, SB_G:SB_G + 512]).then_inc(gate_in, 16)
                sp.dma_start(gate[0:rows[m], 512:1280], io.proj[r, DSA_G:DSA_G + 768]).then_inc(gate_in, 16)
                sp.dma_start(gate[0:rows[m], 1280:2048], io.proj[r, NSA_G:NSA_G + 768]).then_inc(gate_in, 16)
            sp.wait_ge(turned, 20)
            for m in range(5):
                if m:
                    sp.wait_ge(summed, m)
                sp.dma_start(x[0:rows[m], :], io.xp[m * P:(m + 1) * P, :] if m < 4 else io.xs).then_inc(x_in, 16)

        @block.gpsimd
        def _(pool):
            for m in range(5):
                pool.wait_ge(summed, m + 1)
                pool.dma_start(io.y_p[m * P:(m + 1) * P, :] if m < 4 else io.y_s, y[0:rows[m], :]).then_inc(stored, 16)
            pool.wait_ge(stored, 80)

        @block.scalar
        def _(act):
            act.preload_act_table_set("natural_log_exp_and_others")
            src = io.w_out.rearrange("(h p) n -> p h n", p=P)
            for c in range(4):
                act.dma_start(w[:, 4 * c:4 * c + 4, :], src[:, 4 * c:4 * c + 4, :]).then_inc(w_in, 16)
            act.dma_start(gain[:], io.norm_post.to_broadcast([P, D])).then_inc(gain_in, 16)
            for m in range(5):
                act.wait_ge(gate_in, 48 * (m + 1))
                if m:
                    act.wait_ge(gate_ready, m)
                act.activation(sig[0:rows[m], :], gate[0:rows[m], :], ACT.Exp, scale=-1.0).then_inc(sig_exp, 1)
            for m in range(5):
                for c in range(4):
                    k = 4 * m + c
                    act.wait_ge(moved, k + 1)
                    if k:
                        act.wait_ge(squared, k)
                    act.activation(sq[0:rows[m], :], y[0:rows[m], c * CH:(c + 1) * CH], ACT.Square, accum_out=ss[0:rows[m], m, c:c + 1]).then_inc(squared, 1)
                act.wait_ge(var, 2 * m + 2)
                r = rstd[0:rows[m], m:m + 1]
                act.activation(r, r, ACT.Ln).then_inc(rooted, 1)
                act.wait_ge(rooted, 2 * m + 1)
                act.activation(r, r, ACT.Exp, scale=-0.5).then_inc(rooted, 1)

        @block.tensor
        def _(pe):
            for m in range(5):
                pe.wait_ge(gate_ready, m + 1)
                for q in range(4):
                    n = 4 * m + q
                    if n >= 2:
                        pe.wait_ge(gated, n - 1)
                    for k in range(4):
                        last = pe.transpose(tp[n % 2][:, k, 0:rows[m]], gate[0:rows[m], (4 * q + k) * P:(4 * q + k + 1) * P], kept.ident[0:rows[m], 0:rows[m]])
                    last.then_inc(turned, 1)
            pe.wait_ge(w_in, 64)
            pe.wait_ge(gated, 20)
            for m in range(5):
                for c in range(4):
                    k = 4 * m + c
                    if k >= 4:
                        pe.wait_ge(moved, k - 3)
                    for h in range(16):
                        last = pe.matmul(yp[k % 4][0:rows[m], :], heads_at(m, h, 1)[:, 0, :], w[:, h, c * CH:(c + 1) * CH], start=(h == 0), stop=(h == 15))
                    last.then_inc(projected, 1)

        @block.vector
        def _(dve):
            for m in range(5):
                r = rows[m]
                dve.wait_ge(sig_exp, m + 1)
                dve.tensor_scalar(sig[0:r, :], sig[0:r, :], 1.0, None, ALU.add).then_inc(sig_step, 1)
                dve.wait_ge(sig_step, 2 * m + 1)
                dve.reciprocal(sig[0:r, :], sig[0:r, :]).then_inc(sig_step, 1)
                dve.wait_ge(sig_step, 2 * m + 2)
                dve.tensor_tensor(gate[0:r, :], gate[0:r, :], sig[0:r, :], ALU.mult).then_inc(gate_ready, 1)
                for q in range(4):
                    n = 4 * m + q
                    dve.wait_ge(turned, n + 1)
                    o = heads_at(m, 4 * q, 4)
                    dve.tensor_tensor(o, o, tp[n % 2][:, :, 0:r], ALU.mult).then_inc(gated, 1)
            dve.wait_ge(gain_in, 16)
            for m in range(5):
                r = rows[m]
                for c in range(4):
                    k = 4 * m + c
                    dve.wait_ge(projected, k + 1)
                    if m:
                        dve.wait_ge(stored, 16 * m)
                    dve.tensor_copy(y[0:r, c * CH:(c + 1) * CH], yp[k % 4][0:r, :]).then_inc(moved, 1)
                dve.wait_ge(squared, 4 * m + 4)
                dve.tensor_reduce(rstd[0:r, m:m + 1], ss[0:r, m, :], AX.X, ALU.add).then_inc(var, 1)
                dve.wait_ge(var, 2 * m + 1)
                dve.tensor_scalar(rstd[0:r, m:m + 1], rstd[0:r, m:m + 1], 1.0 / D, EPS, ALU.mult, ALU.add).then_inc(var, 1)
                dve.wait_ge(rooted, 2 * m + 2)
                dve.wait_ge(moved, 4 * m + 4)
                dve.scalar_tensor_tensor(y[0:r, :], y[0:r, :], rstd[0:r, m:m + 1], gain[0:r, :], ALU.mult, ALU.mult).then_inc(scaled, 1)
                dve.wait_ge(scaled, m + 1)
                dve.wait_ge(x_in, 16 * (m + 1))
                dve.tensor_tensor(y[0:r, :], y[0:r, :], x[0:r, :], ALU.add).then_inc(summed, 1)


def program(nc, io):
    with ExitStack() as ctx:
        s = Scope(nc, ctx, "kept")
        kept = Kept()
        kept.consts = s.sb("consts", [P, C_KEPT])
        kept.ident = kept.consts[:, C_ID:C_ID + P]
        kept.sel_e = s.sb("sel_e", [P, 4 * P], BF16)
        kept.sel_d = s.sb("sel_d", [NS, 4 * P], BF16)
        kept.ident_b = s.sb("ident_b", [P, P], BF16)
        kept.pages = s.sb("pages", [1, NB * NPG], I32)
        kept.paired = s.sb("paired", [1, NB * NPG], I32)
        with nc.sbuf_tensor("hT", [P, KT_IN, TOK], F32) as hT:
            setup_and_norm(nc, io, kept, hT)
            project_in(nc, io, hT)
        kept.cmp_kp = s.sb("cmp_kp", [P, 2, 16])
        kept.cmp_vp = s.sb("cmp_vp", [16, 2, DH])
        kept.oTs = s.sb("oTs", [P, 16, NS])
        with ExitStack() as sample_ctx:
            sample = Scope(nc, sample_ctx, "kept")
            place_queries(kept, sample)
            kept.drop_blk = sample.sb("drop_blk", [P, NSB], BF16)
            with nc.sbuf_tensor("cmp_k", [P, NB, 2, NC], F32) as kept.cmp_k, nc.sbuf_tensor("cmp_v", [P, NB, 2, DH], F32) as kept.cmp_v:
                compress(nc, io, kept)
                prepare(nc, io, kept)
                cmp_sample(nc, io, kept)
            kept.drop = sample.sb("drop", [NS, KEYS], BF16)
            with nc.sbuf_tensor("scores", [NS, KEYS], F32) as kept.scores:
                index_scores(nc, io, kept)
                stick_breaking(nc, io, kept)
            dsa_sample(nc, io, kept)
            slc_sample(nc, io, kept)
            win_sample(nc, io, kept)
        kept.oT = s.sb("oT", [P, 16, SEQ])
        with ExitStack() as prompt_ctx:
            prompt = Scope(nc, prompt_ctx, "kept")
            prompt_prepare(nc, io, kept, prompt)
            prompt_attention(nc, io, kept, prompt)
        finish(nc, io, kept, s)


_INS = ['x_prompt', 'x_sample', 'cache_sb_kv', 'cache_dsa_kv', 'cache_dsa_idx', 'cache_nsa_kv', 'state_nsa_win', 'page_table',
        'w_in', 'w_out', 'norm_pre', 'norm_post', 'cmp_pe', 'cmp_w1', 'cmp_w2', 'rel_bias']
_OUTS = [(1, SEQ, D), (NB, NT, D), (1, 1, SEQ, 2, 4, DH), (1, NB, NT, 2, 4, DH), (1, 1, SEQ, 2, 2, DH), (1, NB, NT, 2, 2, DH),
         (1, 1, SEQ, 64), (1, NB, NT, 64), (1, 1, SEQ, 4, 2, DH), (1, NB, NT, 4, 2, DH),
         (1, 1, WIN, 2, 2, DH), (1, NB, WIN, 2, 2, DH)]


def describe(nc, shapes):
    def inp(name, shape, dt=F32):
        return nc.dram_tensor(f"in_{name}_dram", shape, dt, kind="ExternalInput").ap()

    a = {n: inp(n, *shapes[n]) for n in _INS}
    io = Io()
    io.consts = inp("constants", [P, C_END])
    io.onehot = inp("onehot", [NBUCK, LINE])
    io.xp = a['x_prompt'].rearrange("a s d -> (a s) d")
    io.xs = a['x_sample'].rearrange("b t d -> (b t) d")
    io.sb_cache = a['cache_sb_kv'].rearrange("l n p a h d -> (l n) p (a h d)")
    io.dsa_cache = a['cache_dsa_kv'].rearrange("l n p a h d -> (l n) p (a h d)")
    io.idx_cache = a['cache_dsa_idx'].rearrange("l n p d -> (l n) p d")
    io.nsa_cache = a['cache_nsa_kv'].rearrange("l n p a h d -> (l n) p (a h d)")
    io.win_state = a['state_nsa_win'].rearrange("l b w a h d -> (l b) w (a h d)")
    io.page_table = a['page_table']
    io.w_in = a['w_in'].rearrange("l k n -> (l k) n")
    io.w_out = a['w_out'].rearrange("l k n -> (l k) n")
    io.norm_pre = a['norm_pre'].rearrange("l d -> (l d)")
    io.norm_post = a['norm_post']
    io.cmp_pe = a['cmp_pe'].rearrange("l r p k d -> (l r) (p k d)")
    io.cmp_w1 = a['cmp_w1'].rearrange("l p k (r d) e -> (l p k) d r e", d=DH)
    io.cmp_w2 = a['cmp_w2'].rearrange("l p k e f -> (l p k) e f")
    io.rel_bias = a['rel_bias']
    io.line = nc.dram_tensor("bias_line", [HB, LINE], F32).ap()
    io.lines = nc.dram_tensor("bias_lines", [P, HB, XL], F32).ap()
    io.proj = nc.dram_tensor("proj", [TOK, DIN], F32).ap()
    outs = [nc.dram_tensor(f"out_{i}_dram", shape, F32, kind="ExternalOutput").ap() for i, shape in enumerate(_OUTS)]
    io.y_p = outs[0].rearrange("a s d -> (a s) d")
    io.y_s = outs[1].rearrange("b t d -> (b t) d")
    io.new_rows = []
    for n, (col, width) in enumerate(((SB_K, 1024), (DSA_K, 512), (IDX_K, 64), (NSA_KC, 1024))):
        flat = "l b s d -> (l b s) d" if width == 64 else "l b s a h d -> (l b s) (a h d)"
        io.new_rows.append((outs[2 + 2 * n].rearrange(flat), outs[3 + 2 * n].rearrange(flat), col, width))
    io.win_p = outs[10].rearrange("l b s a h d -> (l b s) (a h d)")
    io.win_s = outs[11].rearrange("l b s a h d -> (l b) s (a h d)")
    io.n_pool = shapes['cache_sb_kv'][0][1]
    return io


def kernel(**inputs):
    import concourse.bacc as _bacc
    from concourse.bass_utils import run_bass_kernel_spmd as _run

    nc = _bacc.Bacc("TRN2", target_bir_lowering=False, num_devices=1)
    arrays, shapes = {}, {}
    for name in _INS:
        a = np.ascontiguousarray(inputs[name])
        arrays[f"in_{name}_dram"] = a
        shapes[name] = (a.shape, mybir.dt.from_np(a.dtype))
    arrays["in_constants_dram"], arrays["in_onehot_dram"] = constants()
    program(nc, describe(nc, shapes))
    r = _run(nc, [arrays], core_ids=[0])
    return tuple(r.results[0][f"out_{i}_dram"] for i in range(len(_OUTS)))
```

```python
import math
from contextlib import ExitStack

import numpy as np
import concourse.bass as bass
from concourse import mybir

F32 = mybir.dt.float32
BF16 = mybir.dt.bfloat16
F32R = mybir.dt.float32r
I32 = mybir.dt.int32
ALU = mybir.AluOpType
ACT = mybir.ActivationFunctionType
AX = mybir.AxisListType

P = 128
D = 2048
SEQ = 512
NB, NT = 8, 8
NS = NB * NT
PAST = 4096
NPG = PAST // P
KEYS = PAST + NT
DH = 128
NBUCK = 32
HB = 12
WIN = 512
CMPB, SLCB = 32, 64
NC = PAST // CMPB
NSB = 65
TOPK_S, TOPK_P = 256, 128
SLC_TOPN = 16
EPS = 1e-6
NEG = -1e30
GONE = -3e38
SCALE = DH ** -0.5
DIN = 7510
KT_IN = D // P
TOK = SEQ + NS
CH = 512
NCH = PAST // CH
PPC = CH // P

SB_Q, SB_K, SB_V, SB_G = 0, 512, 1024, 1536
DSA_Q, DSA_K, DSA_V, DSA_G = 2048, 2816, 3072, 3328
IDX_Q, IDX_K, IDX_W = 4096, 4352, 4416
NSA_Q, NSA_KC, NSA_KS, NSA_VS, NSA_KW, NSA_VW, NSA_G, NSA_BG = 4420, 5188, 5700, 5956, 6212, 6468, 6724, 7492

DMAX = PAST + NT - 1
LINE = DMAX + P
XW = SEQ + P
XL = XW + P - 1

C_ID = 0
C_NM = C_ID + P
C_STRICT = C_NM + NT
C_WM = C_STRICT + NT
C_SELI = C_WM + NT
C_SELG = C_SELI + 2 * NS
C_KEPT = C_SELG + 4 * P
C_SELE = C_KEPT
C_SELD = C_SELE + 4 * P
C_PM = C_SELD + 4 * P
C_CM = C_PM + XW
C_TRI = C_CM + 4 * 16
C_END = C_TRI + P


def bucket(dist):
    n = np.maximum(dist, 0)
    nf = np.maximum(n, 1).astype(np.float32)
    large = 16 + (np.log(nf / np.float32(16)) / np.float32(math.log(64)) * np.float32(16)).astype(np.int32)
    return np.where(n < 16, n, np.minimum(large, NBUCK - 1))


def constants():
    c = np.zeros((P, C_END), np.float32)
    p = np.arange(P)[:, None]
    c[:, C_ID:C_ID + P] = np.eye(P)
    x = np.arange(XW)[None]
    c[:, C_PM:C_PM + XW] = np.where((p - x + SEQ >= 0) & (p - x + SEQ < WIN), 0, NEG)
    t, j = p % NT, np.arange(NT)[None]
    c[:, C_NM:C_NM + NT] = np.where(j > t, NEG, 0)
    c[:, C_STRICT:C_STRICT + NT] = j < t
    c[:, C_WM:C_WM + NT] = np.where(j <= t, NEG, 0)
    for g in range(2):
        for r in range(P):
            b, _, tt = g * 4 + r // 32, r % 32 // 8, r % 8
            c[r, C_SELI + g * NS + b * NT + tt] = 1
    for g in range(4):
        for r in range(P):
            b2, q = divmod(r, 64)
            if q < 48:
                kv, tt = q // 24, q % 8
                b = 2 * g + b2
                c[r, C_SELG + g * P + b * 16 + kv * 8 + tt] = 1
                c[b * 16 + kv * 8 + tt, C_SELE + g * P + r] = 1
                c[b * NT + tt, C_SELD + g * P + r] = 1
    for i in range(4):
        e = np.arange(16)[None] * CMPB + CMPB - 1
        c[:, C_CM + i * 16:C_CM + i * 16 + 16] = e <= i * P + p
    c[:, C_TRI:C_TRI + P] = np.arange(P)[None] < p
    onehot = np.zeros((NBUCK, LINE), np.float32)
    y = np.arange(LINE)
    onehot[bucket(DMAX - y), y] = 1
    return c, onehot


class Kept:
    pass


class Io:
    pass


class Scope:

    def __init__(self, nc, ctx, tag):
        self.nc, self.ctx, self.tag, self.sems = nc, ctx, tag, []
        ctx.callback(self.clear)

    def sb(self, name, shape, dt=F32):
        return self.ctx.enter_context(self.nc.sbuf_tensor(f"{self.tag}_{name}", shape, dt))

    def ps(self, name, shape, dt=F32):
        return self.ctx.enter_context(self.nc.psum_tensor(f"{self.tag}_{name}", shape, dt))

    def sem(self, name):
        self.sems.append(self.nc.alloc_semaphore(f"{self.tag}_{name}"))
        return self.sems[-1]

    def clear(self):
        if self.sems:
            self.nc.clear_and_free_semaphores(self.sems)
            self.nc.all_engine_barrier()


def setup_and_norm(nc, io, kept, h_hi, h_lo):
    with ExitStack() as ctx:
        s = Scope(nc, ctx, "norm")
        x = s.sb("x", [P, 2, D])
        sq = s.sb("sq", [P, D])
        ss = s.sb("ss", [P, 5])
        rstd = s.sb("rstd", [P, 5])
        gcol = s.sb("gcol", [P, KT_IN])
        table = s.sb("table", [NBUCK, HB])
        choices = s.sb("choices", [P, 2, 4 * P])
        onehot = s.sb("onehot", [NBUCK, LINE])
        line = s.sb("line", [HB, LINE])
        hT = [s.sb(f"hT{i}", [P, 4, P]) for i in range(2)]
        tp = [s.ps(f"tp{i}", [P, 4, P]) for i in range(2)]
        lp = [s.ps(f"lp{i}", [HB, CH]) for i in range(2)]
        consts_in, gain_in, table_in, onehot_in = s.sem("consts_in"), s.sem("gain_in"), s.sem("table_in"), s.sem("onehot_in")
        x_in = [s.sem(f"x_in{i}") for i in range(2)]
        squared, rooted, scaled, normed = s.sem("squared"), s.sem("rooted"), s.sem("scaled"), s.sem("normed")
        turned, hT_written, hi_made, lo_made = s.sem("turned"), s.sem("hT_written"), s.sem("hi_made"), s.sem("lo_made")
        line_done, line_copied, line_out = s.sem("line_done"), s.sem("line_copied"), s.sem("line_out")
        choices_in = s.sem("choices_in")
        bf_ready, pt_in = s.sem("bf_ready"), s.sem("pt_in")
        block = ctx.enter_context(nc.Block())
        rows = [P, P, P, P, NS]
        pieces = [(c, min(CH, LINE - c)) for c in range(0, LINE, CH)]

        @block.sync
        def _(sp):
            sp.dma_start(kept.consts[:], io.consts[:, 0:C_KEPT]).then_inc(consts_in, 16)
            sp.dma_start(choices[:].rearrange("p a n -> p (a n)"), io.consts[:, C_SELE:C_PM]).then_inc(choices_in, 16)
            for m in range(5):
                if m >= 2:
                    sp.wait_ge(turned, 4 * (m - 1))
                src = io.xp[m * P:(m + 1) * P, :] if m < 4 else io.xs
                sp.dma_start(x[0:rows[m], m % 2, :], src).then_inc(x_in[m % 2], 16)
                if m == 1:
                    sp.dma_start(table[:], io.rel_bias).then_inc(table_in, 16)
                    sp.dma_start(onehot[:], io.onehot).then_inc(onehot_in, 16)
                    sp.dma_start(kept.pages[:], io.page_table.rearrange("b n -> (b n)").rearrange("(a n) -> a n", a=1)).then_inc(pt_in, 16)
                    for b in range(NB):
                        src = io.page_table[b:b + 1, :].rearrange("o (c q) -> o c q", q=PPC)
                        to = kept.paired[:].rearrange("o (g c b q) -> o g b c q", g=NB // 2, b=2, q=PPC)[:, b // 2, b % 2]
                        sp.dma_start(to, src).then_inc(pt_in, 16)
                        sp.dma_start(kept.by_chunk[:].rearrange("o (c b q) -> o b c q", b=NB, q=PPC)[:, b], src).then_inc(pt_in, 16)
            sp.wait_ge(line_copied, len(pieces))
            sp.dma_start(io.line, line[:]).then_inc(line_out, 16)
            sp.wait_ge(line_out, 16)
            sp.wait_ge(pt_in, 16 * (1 + 2 * NB))

        @block.gpsimd
        def _(pool):
            with nc.allow_non_contiguous_dma(reason="a small column"):
                pool.dma_start(gcol[:], io.norm_pre.rearrange("(k p) -> p k", p=P)).then_inc(gain_in, 16)
            pool.wait_ge(gain_in, 16)
            for m in range(5):
                for q in range(4):
                    n = 4 * m + q
                    at = (slice(None), slice(4 * q, 4 * q + 4), slice(m * P, m * P + rows[m]))
                    pool.wait_ge(hT_written, n + 1)
                    pool.tensor_copy(h_hi[at], hT[n % 2][:, :, 0:rows[m]]).then_inc(hi_made, 1)
                    pool.wait_ge(hi_made, n + 1)
                    pool.tensor_tensor(h_lo[at], hT[n % 2][:, :, 0:rows[m]], h_hi[at], ALU.subtract).then_inc(lo_made, 1)

        @block.scalar
        def _(act):
            act.preload_act_table_set("natural_log_exp_and_others")
            for m in range(5):
                act.wait_ge(x_in[m % 2], 16 * (m // 2 + 1))
                if m:
                    act.wait_ge(squared, m)
                act.activation(sq[0:rows[m], :], x[0:rows[m], m % 2, :], ACT.Square,
                               accum_out=ss[0:rows[m], m:m + 1]).then_inc(squared, 1)
                act.wait_ge(scaled, m + 1)
                act.activation(rstd[0:rows[m], m:m + 1], rstd[0:rows[m], m:m + 1], ACT.Ln).then_inc(rooted, 1)
                act.wait_ge(rooted, 2 * m + 1)
                act.activation(rstd[0:rows[m], m:m + 1], rstd[0:rows[m], m:m + 1], ACT.Exp, scale=-0.5).then_inc(rooted, 1)
            for n, (c, w) in enumerate(pieces):
                act.wait_ge(line_done, n + 1)
                act.copy(line[:, c:c + w], lp[n % 2][:, 0:w]).then_inc(line_copied, 1)

        @block.tensor
        def _(pe):
            pe.wait_ge(consts_in, 16)
            for m in range(5):
                pe.wait_ge(normed, m + 1)
                for q in range(4):
                    n = 4 * m + q
                    if n >= 2:
                        pe.wait_ge(hT_written, n - 1)
                    for k in range(4):
                        last = pe.transpose(tp[n % 2][:, k, 0:rows[m]], x[0:rows[m], m % 2, (4 * q + k) * P:(4 * q + k + 1) * P],
                                            kept.ident[0:rows[m], 0:rows[m]])
                    last.then_inc(turned, 1)
            pe.wait_ge(table_in, 16)
            pe.wait_ge(onehot_in, 16)
            for n, (c, w) in enumerate(pieces):
                if n >= 2:
                    pe.wait_ge(line_copied, n - 1)
                pe.matmul(lp[n % 2][:, 0:w], table[:], onehot[:, c:c + w], start=True, stop=True).then_inc(line_done, 1)

        @block.vector
        def _(dve):
            dve.wait_ge(consts_in, 16)
            dve.wait_ge(choices_in, 16)
            dve.tensor_copy(kept.sel_e[:], choices[:, 0]).then_inc(bf_ready, 1)
            dve.tensor_copy(kept.sel_d[:], choices[0:NS, 1]).then_inc(bf_ready, 1)
            dve.tensor_copy(kept.ident_b[:], kept.ident).then_inc(bf_ready, 1)

            def norm(m):
                r = rows[m]
                dve.wait_ge(squared, m + 1)
                dve.tensor_scalar(rstd[0:r, m:m + 1], ss[0:r, m:m + 1], 1.0 / D, EPS, ALU.mult, ALU.add).then_inc(scaled, 1)
                dve.wait_ge(rooted, 2 * m + 2)
                dve.tensor_scalar(x[0:r, m % 2, :], x[0:r, m % 2, :], rstd[0:r, m:m + 1], None, ALU.mult).then_inc(normed, 1)

            norm(0)
            dve.wait_ge(gain_in, 16)
            for m in range(5):
                if m < 4:
                    norm(m + 1)
                r = rows[m]
                for q in range(4):
                    n = 4 * m + q
                    dve.wait_ge(turned, n + 1)
                    if n >= 2:
                        dve.wait_ge(lo_made, n - 1)
                    dve.tensor_tensor(hT[n % 2][:, :, 0:r], tp[n % 2][:, :, 0:r],
                                      gcol[:, 4 * q:4 * q + 4].unsqueeze(2).to_broadcast([P, 4, r]), ALU.mult).then_inc(hT_written, 1)


def project_in(nc, io, h_hi, h_lo):
    with ExitStack() as ctx:
        s = Scope(nc, ctx, "proj")
        Q = KT_IN // 4
        w = [s.sb(f"w{q}", [P, Q, CH]) for q in range(4)]
        w_hi = [s.sb(f"w_hi{q}", [P, Q, CH], F32R) for q in range(4)]
        w_lo = [s.sb(f"w_lo{q}", [P, Q, CH], F32R) for q in range(4)]
        out = [s.sb(f"out{i}", [P, 5, CH]) for i in range(2)]
        acc = [s.ps(f"acc{m}", [P, CH]) for m in range(5)]
        w_in = [s.sem(f"w_in{q}") for q in range(4)]
        hi_made, lo_made, w_used, summed, copied = (s.sem(n) for n in ("hi_made", "lo_made", "w_used", "summed", "copied"))
        out_stored = [s.sem(f"out_stored{i}") for i in range(2)]
        state_copied = s.sem("state_copied")
        block = ctx.enter_context(nc.Block())
        rows = [P, P, P, P, NS]
        whole = DIN // CH
        tail = DIN - whole * CH
        assert whole % 2 == 0

        def wait_used(eng, q, n):
            if q < 3:
                eng.wait_ge(w_used, n * 3 + q + 1)
            else:
                eng.wait_ge(summed, n * 5 + 5)

        @block.sync
        def _(sp):
            def load(q, k, col, width):
                sp.wait_ge(lo_made, k + 1)
                sp.dma_start(w[q][:, :, 0:width], io.w_in[q * Q * P:(q + 1) * Q * P, col].rearrange("(k p) n -> p k n", p=P)).then_inc(w_in[q], 16)

            with sp.Fori(0, whole) as n:
                for q in range(4):
                    load(q, n * 4 + q, bass.ds(n * CH, CH), CH)
            for q in range(4):
                load(q, whole * 4 + q, slice(whole * CH, DIN), tail)
            sp.dma_start(io.win_s[:, 0:WIN - NT, :], io.win_state[:, NT:WIN, :]).then_inc(state_copied, 16)
            sp.wait_ge(state_copied, 16)

        @block.vector
        def _(dve):
            def split(q, n, width):
                dve.wait_ge(w_in[q], n * 16 + 16)
                wait_used(dve, q, n)
                dve.tensor_copy(w_hi[q][:, :, 0:width], w[q][:, :, 0:width]).then_inc(hi_made, 1)

            with dve.Fori(0, whole) as n:
                for q in range(4):
                    split(q, n, CH)
            for q in range(4):
                split(q, whole, tail)

        @block.gpsimd
        def _(pool):
            pool.nop().then_inc(lo_made, 4)

            def rest(q, n, width):
                pool.wait_ge(hi_made, n * 4 + q + 1)
                wait_used(pool, q, n)
                pool.tensor_tensor(w_lo[q][:, :, 0:width], w[q][:, :, 0:width], w_hi[q][:, :, 0:width], ALU.subtract).then_inc(lo_made, 1)

            with pool.Fori(0, whole) as n:
                for q in range(4):
                    rest(q, n, CH)
            for q in range(4):
                rest(q, whole, tail)

        @block.tensor
        def _(pe):
            pe.nop().then_inc(w_used, 3)
            pe.nop().then_inc(summed, 5)

            def chunk(n, width):
                for q in range(4):
                    pe.wait_ge(lo_made, n * 4 + q + 5)
                    for m in range(5):
                        if q == 0:
                            pe.wait_ge(copied, n * 5 + m + 1)
                        to, r = acc[m][0:rows[m], 0:width], slice(m * P, m * P + rows[m])
                        for k in range(Q):
                            kk = q * Q + k
                            pe.matmul(to, h_hi[:, kk, r], w_hi[q][:, k, 0:width], start=(kk == 0), stop=False)
                            pe.matmul(to, h_lo[:, kk, r], w_hi[q][:, k, 0:width], start=False, stop=False)
                            last = pe.matmul(to, h_hi[:, kk, r], w_lo[q][:, k, 0:width], start=False, stop=(kk == KT_IN - 1))
                        if q == 3:
                            last.then_inc(summed, 1)
                        elif m == 4:
                            last.then_inc(w_used, 1)

            with pe.Fori(0, whole) as n:
                chunk(n, CH)
            chunk(whole, tail)

        @block.scalar
        def _(act):
            act.nop().then_inc(copied, 5)
            for u in range(2):
                act.nop().then_inc(out_stored[u], 32)

            def store(u, n, fills, col, width):
                for m in range(5):
                    act.wait_ge(summed, n * 5 + m + 6)
                    if m == 0:
                        act.wait_ge(out_stored[u], fills * 32 + 32)
                    act.copy(out[u][0:rows[m], m, 0:width], acc[m][0:rows[m], 0:width]).then_inc(copied, 1)
                act.wait_ge(copied, n * 5 + 10)
                act.dma_start(io.proj[0:SEQ, col].rearrange("(m p) n -> p m n", p=P), out[u][:, 0:4, 0:width]).then_inc(out_stored[u], 16)
                act.dma_start(io.proj[SEQ:TOK, col], out[u][0:NS, 4, 0:width]).then_inc(out_stored[u], 16)

            with act.Fori(0, whole // 2) as i:
                for u in range(2):
                    store(u, i * 2 + u, i, bass.ds((i * 2 + u) * CH, CH), CH)
            store(0, whole, whole // 2, slice(whole * CH, DIN), tail)
            act.wait_ge(out_stored[0], 32 * (whole // 2 + 2))
            act.wait_ge(out_stored[1], 32 * (whole // 2 + 1))


def place_queries(kept, keep):
    kept.q_sb = keep.sb("q_sb", [P, NB, 4, 32])
    kept.q_dsa = keep.sb("q_dsa", [P, NB, 2, 64])
    kept.q_nsa = keep.sb("q_nsa", [P, NB, 2, 64])
    kept.q_idx = keep.sb("q_idx", [P, 2, NB, 32])
    kept.k_sb = keep.sb("k_sb", [P, 4, NS])
    kept.k_dsa = keep.sb("k_dsa", [P, 2, NS])
    kept.k_slc = keep.sb("k_slc", [P, 2, NS])
    kept.k_win = keep.sb("k_win", [P, 2, NS])
    kept.k_idx = keep.sb("k_idx", [64, NS])
    kept.w_idx = keep.sb("w_idx", [P, 2])
    kept.gates = keep.sb("gates", [P, 4, 3])


def prepare(nc, io, kept):
    with ExitStack() as ctx:
        s = Scope(nc, ctx, "prep")
        new = s.sb("new", [NS, DIN])
        tp = [s.ps(f"tp{i}", [P, 8, NS]) for i in range(4)]
        new_in, cols_in = s.sem("new_in"), s.sem("cols_in")
        zeroed, turned, copied, gated = s.sem("zeroed"), s.sem("turned"), s.sem("copied"), s.sem("gated")
        block = ctx.enter_context(nc.Block())

        items = [(SB_Q + h * DH, kept.q_sb[:, :, h, h * 8:h * 8 + 8], SCALE) for h in range(4)]
        for col, q in ((DSA_Q, kept.q_dsa), (NSA_Q, kept.q_nsa)):
            items += [(col + h * DH, q[:, :, h // 3, h * 8:h * 8 + 8], SCALE) for h in range(6)]
        for col, k, n in ((SB_K, kept.k_sb, 4), (DSA_K, kept.k_dsa, 2), (NSA_KS, kept.k_slc, 2), (NSA_KW, kept.k_win, 2)):
            items += [(col + h * DH, k[:, h, :], None) for h in range(n)]
        n_full = len(items)
        idx_cols = [IDX_Q, IDX_Q + DH, IDX_K]
        total = n_full + 3

        @block.sync
        def _(sp):
            sp.dma_start(new[:], io.proj[SEQ:TOK, :]).then_inc(new_in, 16)
            sp.wait_ge(zeroed, 5)
            with nc.allow_non_contiguous_dma(reason="a few numbers per row"):
                for b in range(NB):
                    rows = io.proj[SEQ + b * NT:SEQ + b * NT + NT, :]
                    sp.dma_start(kept.w_idx[b % 4 * 32:b % 4 * 32 + 32, b // 4:b // 4 + 1],
                                 rows[:, IDX_W:IDX_W + 4].rearrange("t h -> h t").unsqueeze(2)).then_inc(cols_in, 16)
                    for r in range(3):
                        sp.dma_start(kept.gates[b % 2 * 64:b % 2 * 64 + 48, b // 2, r:r + 1],
                                     rows[:, NSA_BG + 6 * r:NSA_BG + 6 * r + 6].rearrange("t h -> h t").unsqueeze(2)).then_inc(cols_in, 16)
            sp.wait_ge(cols_in, 64 * NB)

        @block.gpsimd
        def _(pool):
            for n, t in enumerate((kept.q_sb, kept.q_dsa, kept.q_nsa, kept.q_idx, kept.gates)):
                pool.memset(t[:], 0.0).then_inc(zeroed, 1)

        @block.scalar
        def _(act):
            act.wait_ge(cols_in, 64 * NB)
            act.activation(kept.gates[:], kept.gates[:], ACT.Exp, scale=-1.0).then_inc(gated, 1)
            act.wait_ge(zeroed, 5)
            for i, (_, to, scale) in enumerate(items):
                act.wait_ge(turned, i // 8 + 1)
                src = tp[i // 8][:, i % 8, :]
                if scale:
                    act.activation(to, src.rearrange("p (b t) -> p b t", t=NT), ACT.Copy, scale=scale).then_inc(copied, 1)
                else:
                    act.copy(to, src).then_inc(copied, 1)
            act.wait_ge(turned, 4)
            for j in range(2):
                src = tp[3][:, n_full - 24 + j, :].rearrange("p (b t) -> p b t", t=NT)
                for i in range(2):
                    h = 2 * j + i
                    for half in range(2):
                        act.copy(kept.q_idx[64 * half:64 * half + 64, half, :, h * 8:h * 8 + 8], src[64 * i:64 * i + 64]).then_inc(copied, 1)
            act.copy(kept.k_idx[:], tp[3][0:64, n_full - 24 + 2, :]).then_inc(copied, 1)

        @block.tensor
        def _(pe):
            pe.wait_ge(new_in, 16)
            cols = [c for c, _, _ in items] + idx_cols
            for i, c in enumerate(cols):
                last = pe.transpose(tp[i // 8][:, i % 8, :], new[:, c:c + DH], kept.ident[0:NS, 0:NS])
                if i % 8 == 7 or i == total - 1:
                    last.then_inc(turned, 1)

        @block.vector
        def _(dve):
            dve.wait_ge(gated, 1)
            dve.tensor_scalar(kept.gates[:], kept.gates[:], 1.0, None, ALU.add).then_inc(gated, 1)
            dve.wait_ge(gated, 2)
            dve.reciprocal(kept.gates[:], kept.gates[:]).then_inc(gated, 1)


def page_numbers(nc, io, table, first, count, engine=mybir.EngineType.SP):
    _, pages = nc.values_load_multi_w_load_instructions(table[0:1, bass.ds(first, count)], engines=(engine,),
                                                        min_val=0, max_val=io.n_pool - 1)
    return pages


def load_pages(sp, pages, to, cache, col, width, sem):
    for p, page in enumerate(pages):
        src = cache[bass.ds(page, 1), :, col:col + width].rearrange("o p c -> (o p) c")
        sp.dma_start(to[:, p], src).then_inc(sem, 16)


def compress(nc, io, kept):
    with ExitStack() as ctx:
        s = Scope(nc, ctx, "cmp")
        SLOTS = 4
        CREDIT = 4 * (SLOTS - 1)
        FEW = 32
        w1 = s.sb("w1", [P, 4, CMPB, DH])
        w2 = kept.q_sb[:].rearrange("p b h r -> p (b h r)")[:, 0:4 * DH].rearrange("p (a f) -> p a f", f=DH)
        pe_rows = kept.q_dsa[0:CMPB].rearrange("p b h r -> p (b h r)")[:, 0:4 * DH].rearrange("p (a f) -> p a f", f=DH)
        half = lambda x, i: x[:, i * 4 * NC:(i + 1) * 4 * NC].rearrange("p (a c) -> p a c", c=NC)
        spare_a, spare_b = kept.oTs[:].rearrange("p h t -> p (h t)"), kept.q_nsa[:].rearrange("p b h r -> p (b h r)")
        hid_e, hid_r, hid = half(spare_a, 0), half(spare_a, 1), half(spare_b, 0)
        shift = s.sb("shift", [P, 2, 4])
        rows = [s.sb(f"rows{i}", [P, PPC, 4, DH]) for i in range(SLOTS)]
        xT = s.sb("xT", [P, 4, PAST])
        tp = [s.ps(f"tp{a}", [P, CH]) for a in range(4)]
        hp = s.ps("hp", [P, 4, NC])
        kp = s.ps("kp", [P, 2, NC])
        few = s.sb("few", [P, DH])
        fp = s.ps("fp", [P, DH])
        vp = s.ps("vp", [P, 2, DH])
        pe_in, w_in, rows_in = s.sem("pe_in"), s.sem("w_in"), [s.sem(f"rows_in{i}") for i in range(SLOTS)]
        turned, x_copied = s.sem("turned"), [s.sem(f"x_copied{a}") for a in range(4)]
        hid_summed, hid_exp, hid_done, out_summed, out_copied = (
            s.sem("hid_summed"), s.sem("hid_exp"), s.sem("hid_done"), s.sem("out_summed"), s.sem("out_copied"))
        copies_out = s.sem("copies_out")
        zeroed, few_summed, few_copied = s.sem("zeroed"), s.sem("few_summed"), s.sem("few_copied")
        pe_turned, pe_copied, shift_done, hid_step = (
            s.sem("pe_turned"), s.sem("pe_copied"), s.sem("shift_done"), s.sem("hid_step"))
        block = ctx.enter_context(nc.Block())

        @block.sync
        def _(sp):
            sp.dma_start(pe_rows, io.cmp_pe).then_inc(pe_in, 16)
            sp.dma_start(w2, io.cmp_w2.rearrange("a e f -> e a f")).then_inc(w_in, 16)
            sp.dma_start(rows[0][:], io.proj[0:SEQ, NSA_KC:NSA_KC + 512].rearrange("(m p) n -> p m n", p=P)).then_inc(rows_in[0], 64)
            for a in range(4):
                sp.dma_start(w1[:, a], io.cmp_w1[a]).then_inc(w_in, 16)
            with sp.Fori(0, NB * NCH // SLOTS) as i:
                for u in range(SLOTS):
                    if u == 0:
                        pages = page_numbers(nc, io, kept.pages, i * (SLOTS * PPC), SLOTS * PPC)
                    sp.wait_ge(turned, i * 16 + 4 * u + 4)
                    v = (u + 1) % SLOTS
                    load_pages(sp, pages[u * PPC:(u + 1) * PPC], rows[v][:], io.nsa_cache, 0, 512, rows_in[v])
            n = 0
            for to_p, to_s, col, width in io.new_rows:
                sp.dma_start(to_p, io.proj[0:SEQ, col:col + width]).then_inc(copies_out, 16)
                sp.dma_start(to_s, io.proj[SEQ:TOK, col:col + width]).then_inc(copies_out, 16)
                n += 2
            sp.dma_start(io.win_p, io.proj[0:SEQ, NSA_KW:NSA_KW + 512]).then_inc(copies_out, 16)
            sp.dma_start(io.win_s[:, WIN - NT:WIN, :], io.proj[SEQ:TOK, NSA_KW:NSA_KW + 512].rearrange("(b t) n -> b t n", t=NT)).then_inc(copies_out, 16)
            first = DMAX - SEQ - (P - 1)
            sp.dma_start(io.lines, io.line[:, first:first + XL].unsqueeze(0).to_broadcast([P, HB, XL])).then_inc(copies_out, 16)
            sp.wait_ge(copies_out, 16 * (n + 3))

        @block.gpsimd
        def _(pool):
            pool.memset(xT[:, :, SEQ + CMPB:FEW * CMPB], 0.0).then_inc(zeroed, 1)

        def turn(pe, unit, u, filled):
            pe.wait_ge(rows_in[u], filled)
            for a in range(4):
                pe.wait_ge(x_copied[a], unit + 1)
                for p in range(PPC):
                    last = pe.transpose(tp[a][:, p * P:(p + 1) * P], rows[u][:, p, a, :], kept.ident)
                last.then_inc(turned, 1)

        def hidden(pe, blocks, units_copied):
            for a in range(4):
                pe.wait_ge(x_copied[a], units_copied + 1)
                xv = xT[:, a, 0:blocks * CMPB].rearrange("p (c r) -> p r c", r=CMPB)
                for r in range(CMPB):
                    last = pe.matmul(hp[:, a, 0:blocks], w1[:, a, r, :], xv[:, r, :], start=(r == 0), stop=(r == CMPB - 1))
            last.then_inc(hid_summed, 1)

        def outputs(pe, n, blocks):
            pe.wait_ge(hid_done, n + 1)
            pe.wait_ge(out_copied, n * 2 + 2)
            for kv in range(2):
                pe.matmul(kp[:, kv, 0:blocks], w2[:, kv, :], hid[:, kv, 0:blocks], start=True, stop=True)
            for kv in range(2):
                last = pe.matmul(vp[0:blocks, kv, :], hid[:, 2 + kv, 0:blocks], w2[:, 2 + kv, :], start=True, stop=True)
            last.then_inc(out_summed, 1)

        @block.tensor
        def _(pe):
            pe.nop().then_inc(turned, CREDIT)
            pe.wait_ge(pe_in, 16)
            for a in range(4):
                last = pe.transpose(tp[0][:, a * CMPB:(a + 1) * CMPB], pe_rows[:, a, :], kept.ident[0:CMPB, 0:CMPB])
            last.then_inc(pe_turned, 1)
            pe.wait_ge(pe_copied, 1)
            turn(pe, 0, 0, 64)
            pe.wait_ge(w_in, 80)
            pe.wait_ge(zeroed, 1)
            for a in range(4):
                pe.wait_ge(x_copied[a], 2)
            for r in range(CMPB):
                for a in range(4):
                    xv = xT[:, a, 0:FEW * CMPB].rearrange("p (c r) -> p r c", r=CMPB)
                    last = pe.matmul(fp[a * FEW:(a + 1) * FEW, :], xv[:, r, :], w1[:, a, r, :], start=(r == 0), stop=(r == CMPB - 1),
                                     tile_position=(0, a * FEW), skip_group_check=True)
            last.then_inc(few_summed, 1)
            pe.wait_ge(few_copied, 1)
            pe.transpose(hp[:, :, 0:FEW], few[:], kept.ident).then_inc(hid_summed, 1)
            outputs(pe, 0, SEQ // CMPB)

            def turns(b, units):
                for c in units:
                    turn(pe, b * 8 + (c + 1), (c + 1) % SLOTS, b * 128 + 64 * (1 + (c + 1) // SLOTS))

            turns(0, range(NCH))
            hidden(pe, NC, 9)
            with pe.Fori(0, NB - 1) as b:
                turns(b + 1, range(2))
                outputs(pe, b + 1, NC)
                turns(b + 1, range(2, NCH))
                hidden(pe, NC, b * 8 + 17)
            outputs(pe, NB, NC)

        def copy_part(eng, a, unit, at, last_mlp):
            eng.wait_ge(turned, unit * 4 + a + 1 + CREDIT)
            eng.wait_ge(hid_summed, last_mlp)
            copy = eng.copy if a % 2 else eng.tensor_copy
            copy(xT[:, a, at], tp[a][:]).then_inc(x_copied[a], 1)

        @block.vector
        def _(dve):
            for a in (0, 2):
                dve.nop().then_inc(x_copied[a], 1)
            dve.nop().then_inc(hid_summed, 1)
            dve.wait_ge(pe_turned, 1)
            dve.tensor_copy(xT[:, :, SEQ:SEQ + CMPB], tp[0][:, 0:4 * CMPB].rearrange("p (a r) -> p a r", r=CMPB)).then_inc(pe_copied, 1)

            def activate(n, blocks):
                dve.wait_ge(hid_exp, n + 1)
                dve.wait_ge(out_summed, n + 1)
                for a in range(4):
                    last = dve.scalar_tensor_tensor(hid[:, a, 0:blocks], hp[:, a, 0:blocks], shift[:, 0, a:a + 1], hid_r[:, a, 0:blocks], ALU.add, ALU.mult)
                last.then_inc(hid_done, 1)

            dve.nop().then_inc(out_summed, 1)
            for a in (0, 2):
                copy_part(dve, a, 0, slice(0, CH), 1)
            dve.wait_ge(few_summed, 1)
            dve.tensor_copy(few[:], fp[:]).then_inc(few_copied, 1)
            dve.wait_ge(hid_summed, 2)
            dve.tensor_copy(shift[:, 0, :], hp[:, :, SEQ // CMPB]).then_inc(shift_done, 1)
            dve.wait_ge(shift_done, 1)
            dve.tensor_scalar(shift[:, 1, :], shift[:, 0, :], -1.0, None, ALU.mult).then_inc(shift_done, 1)
            activate(0, SEQ // CMPB)

            def copies(b, units):
                for c in units:
                    for a in (0, 2):
                        copy_part(dve, a, b * 8 + c + 1, slice(c * CH, (c + 1) * CH), b + 2)

            copies(0, range(NCH))
            with dve.Fori(0, NB - 1) as b:
                activate(b + 1, NC)
                copies(b + 1, range(NCH))
            activate(NB, NC)

        @block.scalar
        def _(act):
            act.preload_act_table_set("natural_log_exp_and_others")
            for a in (1, 3):
                act.nop().then_inc(x_copied[a], 1)
            act.nop().then_inc(out_copied, 2)

            def exps(n, blocks):
                act.wait_ge(hid_summed, n + 2)
                if not isinstance(n, int) or n:
                    act.wait_ge(hid_done, n)
                for a in range(4):
                    last = act.activation(hid_e[:, a, 0:blocks], hp[:, a, 0:blocks], ACT.Exp, bias=shift[:, 1, a:a + 1], scale=-1.0)
                last.then_inc(hid_step, 1)
                act.wait_ge(hid_step, n * 2 + 1)
                act.activation(hid_r[:, :, 0:blocks], hid_e[:, :, 0:blocks], ACT.Ln, bias=1.0).then_inc(hid_step, 1)
                act.wait_ge(hid_step, n * 2 + 2)
                act.activation(hid_r[:, :, 0:blocks], hid_r[:, :, 0:blocks], ACT.Exp, scale=-1.0).then_inc(hid_exp, 1)

            def results(n, to_k, to_v, blocks):
                act.wait_ge(out_summed, n + 2)
                act.copy(to_k, kp[:, :, 0:blocks]).then_inc(out_copied, 1)
                act.copy(to_v, vp[0:blocks]).then_inc(out_copied, 1)

            for a in (1, 3):
                copy_part(act, a, 0, slice(0, CH), 1)
            act.wait_ge(shift_done, 2)
            exps(0, SEQ // CMPB)
            results(0, kept.cmp_kp[:], kept.cmp_vp[:], SEQ // CMPB)

            def copies(b, units):
                for c in units:
                    for a in (1, 3):
                        copy_part(act, a, b * 8 + c + 1, slice(c * CH, (c + 1) * CH), b + 2)

            def keep(b):
                results(b + 1, kept.cmp_k[:, bass.ds(b, 1)].rearrange("p o k c -> p (o k) c"),
                        kept.cmp_v[:, bass.ds(b, 1)].rearrange("p o k c -> p (o k) c"), NC)

            copies(0, range(NCH))
            exps(1, NC)
            with act.Fori(0, NB - 1) as b:
                copies(b + 1, range(2))
                keep(b)
                copies(b + 1, range(2, NCH))
                exps(b + 2, NC)
            keep(NB - 1)


def index_scores(nc, io, kept):
    with ExitStack() as ctx:
        s = Scope(nc, ctx, "idx")
        rows = [s.sb(f"rows{i}", [P, NB, PPC, 64]) for i in range(2)]
        kT = [s.sb(f"kT{i}", [P, 2, P]) for i in range(2)]
        relu = [s.sb(f"relu{g}", [P, CH]) for g in range(2)]
        tp = [s.ps(f"tp{i}", [P, 2, P]) for i in range(2)]
        sp_ = [s.ps(f"sc{g}", [P, CH]) for g in range(2)]
        total = s.ps("total", [NS, CH])
        rows_in = [[s.sem(f"rows_in{i}_{b}") for b in range(NB)] for i in range(2)]
        turned, even_copied, odd_copied, multiplied = s.sem("turned"), s.sem("even_copied"), s.sem("odd_copied"), s.sem("multiplied")
        weighted, summed, total_copied, masked = s.sem("weighted"), s.sem("summed"), s.sem("total_copied"), s.sem("masked")
        copied_by = (even_copied, odd_copied)
        block = ctx.enter_context(nc.Block())
        seli = [kept.consts[:, C_SELI + g * NS:C_SELI + (g + 1) * NS] for g in range(2)]

        def numbers(engine, half, i, u):
            return page_numbers(nc, io, kept.by_chunk, i * (2 * NB * PPC) + (u * NB + half * 4) * PPC, 4 * PPC, engine)

        def load(eng, pages, b, i, u):
            eng.wait_ge(turned, i * (2 * NB) + u * NB + b + 1)
            load_pages(eng, pages[b % 4 * PPC:(b % 4 + 1) * PPC], rows[u][:, b], io.idx_cache, 0, 64, rows_in[u][b])

        @block.sync
        def _(sp):
            with sp.Fori(0, NCH // 2) as i:
                for u in range(2):
                    pages = numbers(mybir.EngineType.SP, 0, i, u)
                    for b in range(4):
                        load(sp, pages, b, i, u)

        @block.tensor
        def _(pe):
            pe.nop().then_inc(turned, 2 * NB)
            pe.nop().then_inc(multiplied, 2)

            def product(b, n):
                g, r = divmod(b, 4)
                pe.wait_ge(copied_by[b % 2], n + 2)
                for half in range(2):
                    to = sp_[g][32 * r:32 * r + 32, :].rearrange("p (q a k) -> p a q k", a=2, k=P)[:, half]
                    last = pe.matmul(to, kept.q_idx[:, half, b, :], kT[b % 2][:], start=(half == 0), stop=(half == 1),
                                     tile_position=(0, 32 * r), skip_group_check=True)
                last.then_inc(multiplied, 1)

            def add_up(g, c):
                pe.wait_ge(weighted, c * 2 + g + 3)
                pe.matmul(total[:], seli[g], relu[g][:], start=(g == 0), stop=(g == 1)).then_inc(summed, 1)

            def chunk(u, fills, c):
                for b in range(NB):
                    pe.wait_ge(rows_in[u][b], fills * 64 + 64)
                    pe.wait_ge(copied_by[b % 2], c * 4 + (b // 2 + 1))
                    for q in range(2):
                        last = pe.transpose(tp[b % 2][:, q, :], rows[u][:, b, 2 * q:2 * q + 2, :].rearrange("p a d -> p (a d)"), kept.ident)
                    last.then_inc(turned, 1)
                    if b == 1 or b == 5:
                        pe.wait_ge(weighted, c * 2 + b // 4 + 1)
                    if b:
                        product(b - 1, c * 4 + (b - 1) // 2)
                    if b == 6:
                        pe.wait_ge(total_copied, c + 1)
                        add_up(0, c)
                product(NB - 1, c * 4 + (NB - 1) // 2)
                add_up(1, c)

            with pe.Fori(0, NCH // 2) as i:
                for u in range(2):
                    chunk(u, i, i * 2 + u)
            n = NCH * NB
            for g in range(2):
                pe.wait_ge(weighted, NCH * 2 + g + 1)
                for r in range(4):
                    b = 4 * g + r
                    last = pe.matmul(sp_[g][32 * r:32 * r + 32, 0:NT], kept.q_idx[0:64, 0, b, :], kept.k_idx[:, b * NT:b * NT + NT],
                                     start=True, stop=True, tile_position=(0, 32 * r))
                last.then_inc(multiplied, 4)
            pe.wait_ge(total_copied, NCH + 1)
            for g in range(2):
                pe.wait_ge(weighted, NCH * 2 + g + 3)
                pe.matmul(total[:, 0:NT], seli[g], relu[g][:, 0:NT], start=(g == 0), stop=(g == 1)).then_inc(summed, 1)

        def copy_keys(eng, n, b):
            eng.wait_ge(turned, n + 1 + 2 * NB)
            eng.wait_ge(multiplied, n + 1)
            copy = eng.copy if b % 2 else eng.tensor_copy
            copy(kT[b % 2][:], tp[b % 2][:]).then_inc(copied_by[b % 2], 1)

        @block.vector
        def _(dve):
            dve.nop().then_inc(even_copied, 1)
            dve.nop().then_inc(weighted, 2)

            def weigh(g, c, width):
                dve.wait_ge(multiplied, c * NB + 4 * g + 4 + 2)
                dve.wait_ge(summed, c * 2 + g + 1)
                dve.tensor_scalar(relu[g][:, 0:width], sp_[g][:, 0:width], 0.0, kept.w_idx[:, g:g + 1], ALU.max, ALU.mult).then_inc(weighted, 1)

            with dve.Fori(0, NCH) as c:
                for b in range(NB):
                    if b % 2 == 0:
                        copy_keys(dve, c * NB + b, b)
                    if b == 5:
                        weigh(0, c, CH)
                weigh(1, c, CH)
            weigh(0, NCH, NT)
            weigh(1, NCH, NT)
            dve.wait_ge(summed, 2 * NCH + 2 + 2)
            dve.tensor_tensor(kept.scores[:, PAST:KEYS], total[:, 0:NT], kept.consts[0:NS, C_NM:C_NM + NT], ALU.add).then_inc(masked, 1)

        @block.scalar
        def _(act):
            act.nop().then_inc(odd_copied, 1)
            act.nop().then_inc(summed, 2)
            act.nop().then_inc(total_copied, 1)
            for u in range(2):
                pages = numbers(mybir.EngineType.Activation, 1, 0, u)
                for b in range(4, NB):
                    load(act, pages, b, 0, u)

            after = {1: (), 3: (4,), 5: (5, 6), 7: (7,)}

            def chunk(c, at, ahead=None):
                if ahead is not None:
                    pages = numbers(mybir.EngineType.Activation, 1, *ahead)
                for b in range(1, NB, 2):
                    copy_keys(act, c * NB + b, b)
                    for other in after[b] if ahead is not None else ():
                        load(act, pages, other, *ahead)
                act.wait_ge(summed, c * 2 + 4)
                act.copy(kept.scores[:, at], total[:]).then_inc(total_copied, 1)

            with act.Fori(0, NCH // 2 - 1) as i:
                for u in range(2):
                    chunk(i * 2 + u, bass.ds((i * 2 + u) * CH, CH), (i + 1, u))
            for c in range(NCH - 2, NCH):
                chunk(c, slice(c * CH, (c + 1) * CH))


def stream(nc, io, kept, tag, *, cache, col, proj_v, heads, per, q, k_new, select=None, dropped_keys=None, bias=None,
           new_biases=(), head0, state=None, gate=None, add=False, stick=False):
    groups = NB // per
    stride = P // per
    nch = 1 if state is not None else NCH
    past = nch * CH
    width = heads * DH
    items = per * heads
    SLOTS = 2 if stick or nch == 1 else 4
    per_bank = CH // width
    with ExitStack() as ctx:
        s = Scope(nc, ctx, tag)
        if stick:
            k_rows = [s.sb(f"k_rows{i}", [P, per, PPC, width]) for i in range(SLOTS)]
            v_rows = [s.sb(f"v_rows{i}", [P, per, PPC, width]) for i in range(SLOTS)]
        else:
            rows = [s.sb(f"rows{i}", [P, per, PPC, 2 * width]) for i in range(SLOTS)]
            k_rows = [r[:, :, :, 0:width] for r in rows]
            v_rows = [r[:, :, :, width:] for r in rows]
        q_now = s.sb("q_now", [P, per, heads, stride])
        v_new = (v_rows if stick else rows)[SLOTS - 1][0:NT].rearrange("p b m c -> p (b m c)")[:, 0:NB * width].rearrange("p (b c) -> p b c", b=NB)
        kT = [s.sb(f"kT{i}", [P, CH]) for i in range(2)]
        prob = [s.sb(f"prob{i}", [P, CH]) for i in range(2)]
        pT = [s.sb(f"pT{i}", [P, PPC, P]) for i in range(2)]
        log_new = s.sb("log_new", [P, groups, NT])
        prob_new = s.sb("prob_new", [P, groups, P])
        pT_new = s.sb("pT_new", [NT, groups, P])
        acc = s.sb("acc", [P, groups, width])
        if stick:
            soft = [s.sb(f"soft{i}", [P, CH]) for i in range(2)]
            soft_new = s.sb("soft_new", [P, groups, NT])
            top8 = s.sb("top8", [NS, 8])
        else:
            nstep = s.sb("nstep", [P, groups, nch + 1])
            nmax = s.sb("nmax", [P, groups, nch + 1])
            shrink = s.sb("shrink", [P, groups, nch + 1])
            share = s.sb("share", [P, groups, nch + 1])
            sums = s.sb("sums", [P, groups, nch + 1])
            rcp = s.sb("rcp", [P, groups])
        if select is not None:
            sel_now = s.sb("sel_now", [select.shape[0], P], BF16)
        tp = [s.ps(f"tp{i}", [P, CH]) for i in range(2)]
        sc = [s.ps(f"sc{i}", [P, CH]) for i in range(2)]
        sc_new = s.ps("sc_new", [P, groups, NT])
        qp = s.ps("qp", [P, PPC, P])
        pv = [s.ps(f"pv{i}", [P, CH]) for i in range(2)]

        k_in = [[s.sem(f"k_in{i}_{b}") for b in range(per)] for i in range(SLOTS)]
        v_in = [[s.sem(f"v_in{i}_{b}") for b in range(per)] for i in range(SLOTS)] if stick else k_in
        small_in, bias_in, zeroed, staged = s.sem("small_in"), s.sem("bias_in"), s.sem("zeroed"), s.sem("staged")
        k_turned, kT_copied, scored, sc_read = s.sem("k_turned"), s.sem("kT_copied"), s.sem("scored"), s.sem("sc_read")
        maxed, probs, probs_turned, pT_copied, v_used, acc_done = (
            s.sem("maxed"), s.sem("probs"), s.sem("probs_turned"), s.sem("pT_copied"), s.sem("v_used"), s.sem("acc_done"))
        new_scored, new_prob, new_turned, new_copied, new_summed, new_acc = (
            s.sem("new_scored"), s.sem("new_prob"), s.sem("new_turned"), s.sem("new_copied"), s.sem("new_summed"), s.sem("new_acc"))
        step_dve, step_act, acc_ready, acc_turned, out_done, shrunk = (
            s.sem("step_dve"), s.sem("step_act"), s.sem("acc_ready"), s.sem("acc_turned"), s.sem("out_done"), s.sem("shrunk"))
        later_in = s.sem("later_in")
        if stick:
            soft_step, soft_done, top_step = s.sem("soft_step"), s.sem("soft_done"), s.sem("top_step")
        block = ctx.enter_context(nc.Block())

        def each_group(eng, body, unroll=False):
            if nch == 1 or unroll:
                for g in range(groups):
                    body(g)
            else:
                with eng.Fori(0, groups) as g:
                    body(g)

        def slot(g, c):
            return (c % SLOTS, g * (nch // SLOTS) + c // SLOTS + 1) if nch > 1 else (g % SLOTS, g // SLOTS + 1)

        def parity(g, c):
            return c % 2 if nch > 1 else g % 2

        def before(g, c):
            return (g, c - 1) if c else (g - 1, 0) if nch == 1 and g else None

        def ends(g):
            return nch > 1 or g == groups - 1

        def data(c):
            return nch - 1 - c if stick else c

        def load_biases(eng, biases, sem):
            for to, first in biases:
                for b in range(per):
                    for t in range(NT):
                        eng.dma_start(to[b * stride + t:b * stride + t + 41:8, :],
                                      io.line[first:first + 6, NT - 1 - t:NT - 1 - t + KEYS]).then_inc(sem, 16)

        def mask_new(to):
            return nc.vector.tensor_tensor(to[:, PAST:], to[:, PAST:], kept.consts[:, C_NM:C_NM + NT], ALU.add)

        @block.sync
        def _(sp):
            sp.dma_start(v_new, io.proj[SEQ:TOK, proj_v:proj_v + width].rearrange("(b t) c -> t b c", t=NT)).then_inc(small_in, 16)

            def new_values_used(i):
                if i == SLOTS - 1:
                    sp.wait_ge(new_summed, 1)

            def rows_of(g):
                for c in range(nch):
                    n = c + g * nch
                    i, _ = slot(g, c)
                    new_values_used(i)
                    if state is None and c % 2 == 0:
                        pages = page_numbers(nc, io, kept.paired, g * (2 * NPG) + c * (2 * PPC), 4 * PPC)
                    for b in range(per):
                        sp.wait_ge(v_used, n * per + b + 1)
                        if state is not None:
                            sp.dma_start(rows[i][:, b], state[g * per + b].rearrange("(m p) c -> p m c", p=P)).then_inc(k_in[i][b], 64)
                        else:
                            first = (c % 2 * per + b) * PPC
                            load_pages(sp, pages[first:first + PPC], rows[i][:, b], cache, col, 2 * width, k_in[i][b])

            def pages_of(g, c):
                return page_numbers(nc, io, kept.by_chunk, g * (per * PPC) + data(c) * (NB * PPC), per * PPC)

            def keys_of(g, c, pages):
                i, _ = slot(g, c)
                for b in range(per):
                    sp.wait_ge(k_turned, (c + g * nch) * items + (b + 1) * heads)
                    load_pages(sp, pages[b * PPC:(b + 1) * PPC], k_rows[i][:, b], cache, col, width, k_in[i][b])

            def values_of(g, c, pages):
                i, _ = slot(g, c)
                new_values_used(i)
                for b in range(per):
                    sp.wait_ge(v_used, (c + g * nch) * per + b + 1)
                    load_pages(sp, pages[b * PPC:(b + 1) * PPC], v_rows[i][:, b], cache, col + width, width, v_in[i][b])

            if stick:
                steps = [(g, c) for g in range(groups) for c in range(nch)]
                pages = pages_of(0, 0)
                keys_of(0, 0, pages)
                for n, (g, c) in enumerate(steps):
                    if n + 1 < len(steps):
                        next_pages = pages_of(*steps[n + 1])
                        keys_of(*steps[n + 1], next_pages)
                    values_of(g, c, pages)
                    pages = next_pages
            else:
                each_group(sp, rows_of)
            if new_biases[1:]:
                sp.wait_ge(zeroed, 3)
                load_biases(sp, new_biases[1:], later_in)

        @block.gpsimd
        def _(pool):
            for to, _ in new_biases[:1]:
                pool.memset(to, 0.0).then_inc(zeroed, 1)
            pool.memset(prob_new[:], 0.0).then_inc(zeroed, 1)
            for to, _ in new_biases[1:]:
                pool.memset(to, 0.0).then_inc(zeroed, 1)

            def stage(g):
                pool.wait_ge(scored, g * nch * items + 2)
                pool.tensor_copy(q_now[:], q[:, bass.ds(g * per, per)]).then_inc(staged, 1)
                if select is not None:
                    pool.tensor_copy(sel_now[:], select[:, bass.ds(g * P, P)]).then_inc(staged, 1)

            each_group(pool, stage)

        @block.tensor
        def _(pe):
            pe.nop().then_inc(k_turned, SLOTS * items)
            pe.nop().then_inc(scored, 2)
            pe.nop().then_inc(probs_turned, 2)
            pe.nop().then_inc(v_used, SLOTS * per)

            def turn(g, c, j):
                n = c + g * nch
                i, filled = slot(g, c)
                b, h = divmod(j, heads)
                if h == 0:
                    pe.wait_ge(k_in[i][b], filled * 64)
                pe.wait_ge(kT_copied, n * items + j + 1)
                for p in range(PPC):
                    last = pe.transpose(tp[j % 2][:, p * P:(p + 1) * P], k_rows[i][:, b, p, h * DH:(h + 1) * DH], kept.ident)
                last.then_inc(k_turned, 1)

            def score(g, c, j):
                n = c + g * nch
                b, h = divmod(j, heads)
                to = sc[parity(g, c)]
                if j == 0:
                    pe.wait_ge(sc_read, n + 1)
                    if c == 0:
                        pe.wait_ge(staged, (1 if select is None else 2) * (g + 1))
                    if select is not None:
                        pe.matmul(to[:], sel_now[:], dropped_keys(data(c)), start=True, stop=False, skip_group_check=True)
                pe.wait_ge(kT_copied, n * items + j + 3)
                pe.matmul(to[b * stride:(b + 1) * stride, :], q_now[:, b, h, :], kT[j % 2][:],
                          start=(select is None and h == 0), stop=(h == heads - 1), skip_group_check=True,
                          tile_position=(0, b * stride)).then_inc(scored, 1)

            def turn_probs(g, c):
                n = c + g * nch
                pe.wait_ge(probs, n + 3)
                pe.wait_ge(pT_copied, n + 1)
                for p in range(PPC):
                    last = pe.transpose(qp[:, p, :], prob[parity(g, c)][:, p * P:(p + 1) * P], kept.ident)
                last.then_inc(probs_turned, 1)

            def values(g, c):
                n = c + g * nch
                i, filled = slot(g, c)
                at = parity(g, c)
                pe.wait_ge(pT_copied, n + 2)
                if c == 0 or nch == 1:
                    pe.wait_ge(new_acc, 2)
                pe.wait_ge(acc_done, n + 1)
                for b in range(per):
                    if stick:
                        pe.wait_ge(v_in[i][b], filled * 64)
                    for p in range(PPC):
                        last = pe.matmul(pv[at][b * stride:(b + 1) * stride, 0:width], pT[at][:, p, b * stride:(b + 1) * stride],
                                         v_rows[i][:, b, p, :], start=(p == 0), stop=(p == PPC - 1), skip_group_check=True,
                                         tile_position=(0, b * stride))
                    last.then_inc(v_used, 1)

            for g in range(groups):
                if select is not None:
                    pe.matmul(sc_new[:, g, :], select[:, g * P:(g + 1) * P], dropped_keys(None), start=True, stop=False, skip_group_check=True)
                for j in range(items):
                    b, h = divmod(j, heads)
                    gb = g * per + b
                    last = pe.matmul(sc_new[b * stride:(b + 1) * stride, g, :], q[:, gb, h, :], k_new[:, h, gb * NT:(gb + 1) * NT],
                                     start=(select is None and h == 0), stop=(h == heads - 1), skip_group_check=True,
                                     tile_position=(0, b * stride))
            last.then_inc(new_scored, 1)
            pe.wait_ge(new_prob, groups if not stick else 1)
            for g in range(groups):
                last = pe.transpose(qp[:, g, :], prob_new[:, g, :], kept.ident)
            last.then_inc(new_turned, 1)
            pe.wait_ge(new_copied, 1)
            pe.wait_ge(small_in, 16)
            for g in range(groups):
                at = g % per_bank * width
                for b in range(per):
                    last = pe.matmul(pv[g // per_bank][b * stride:(b + 1) * stride, at:at + width], pT_new[:, g, b * stride:(b + 1) * stride],
                                     v_new[:, g * per + b, :], start=True, stop=True, skip_group_check=True, tile_position=(0, b * stride))
            last.then_inc(new_summed, 1)

            late = items - max(1, items // 4)

            def group(g):
                for c in range(nch):
                    for j in range(items + 1):
                        if j < items:
                            turn(g, c, j)
                        if j:
                            score(g, c, j - 1)
                        if before(g, c) and j == late:
                            turn_probs(*before(g, c))
                    if before(g, c):
                        values(*before(g, c))
                if ends(g):
                    turn_probs(g, nch - 1)
                    values(g, nch - 1)

            each_group(pe, group)
            pe.wait_ge(acc_ready, 1)
            for g in range(groups):
                for h in range(heads):
                    i = g * heads + h
                    last = pe.transpose(tp[i // 4][:, i % 4 * P:(i % 4 + 1) * P], acc[:, g, h * DH:(h + 1) * DH], kept.ident)
            last.then_inc(acc_turned, 1)

        @block.scalar
        def _(act):
            act.preload_act_table_set("natural_log_exp_and_others")
            act.nop().then_inc(kT_copied, 2)
            act.nop().then_inc(probs, 2)
            if not stick:
                act.wait_ge(zeroed, len(new_biases[:1]) + 1)
                load_biases(act, new_biases[:1], bias_in)
                act.wait_ge(maxed, 1)
                for g in range(groups):
                    act.activation(prob_new[:, g, 0:NT], log_new[:, g, :], ACT.Exp, bias=nmax[:, g, 0:1],
                                   accum_out=sums[:, g, 0:1]).then_inc(new_prob, 1)
            else:
                act.wait_ge(new_scored, 1)
                act.activation(soft_new[:], sc_new[:], ACT.Abs).then_inc(step_act, 1)
                act.wait_ge(step_act, 1)
                act.activation(soft_new[:], soft_new[:], ACT.Exp, scale=-1.0).then_inc(step_act, 1)
                act.wait_ge(step_act, 2)
                act.activation(soft_new[:], soft_new[:], ACT.Ln, bias=1.0).then_inc(step_act, 1)
                act.wait_ge(step_dve, 2 + groups + 1)
                act.wait_ge(zeroed, 1)
                act.activation(prob_new[:, :, 0:NT], log_new[:], ACT.Exp).then_inc(step_act, 1)

            def copy_key(g, c, j):
                n = c + g * nch
                act.wait_ge(k_turned, n * items + j + 1 + SLOTS * items)
                act.wait_ge(scored, n * items + j + 1)
                act.copy(kT[j % 2][:], tp[j % 2][:]).then_inc(kT_copied, 1)

            def exps(g, c):
                n = c + g * nch
                act.wait_ge(maxed, n + 2)
                at = parity(g, c)
                one = lambda x, k: x[:, bass.ds(g, 1), k:k + 1].rearrange("p o k -> p (o k)")
                act.activation(prob[at][:], prob[at][:], ACT.Exp, bias=one(nmax, c + 1), accum_out=one(sums, c + 1)).then_inc(probs, 1)
                act.activation(one(shrink, c + 1), one(nmax, c), ACT.Exp, bias=one(nmax, c + 1), scale=-1.0).then_inc(shrunk, 1)

            def soften(g, c, part):
                n = c + g * nch
                at = parity(g, c)
                if part == 0:
                    act.wait_ge(scored, (n + 1) * items + 2)
                    act.wait_ge(soft_done, n + 1)
                    act.activation(soft[at][:], sc[at][:], ACT.Abs).then_inc(soft_step, 1)
                elif part == 1:
                    act.wait_ge(soft_step, n * 3 + 1)
                    act.activation(soft[at][:], soft[at][:], ACT.Exp, scale=-1.0).then_inc(soft_step, 1)
                elif part == 2:
                    act.wait_ge(soft_step, n * 3 + 2)
                    act.activation(soft[at][:], soft[at][:], ACT.Ln, bias=1.0).then_inc(soft_step, 1)
                else:
                    act.wait_ge(soft_done, n + 2)
                    act.activation(prob[at][:], prob[at][:], ACT.Exp).then_inc(probs, 1)

            when = {0: 0, 1: 1, 2: 2, 3: 8} if stick else {0: 1}

            def group(g):
                for c in range(nch):
                    for j in range(items):
                        copy_key(g, c, j)
                        for part, after in when.items():
                            if before(g, c) and after == j:
                                soften(g, c - 1, part) if stick else exps(*before(g, c))
                for part in when if ends(g) else ():
                    soften(g, nch - 1, part) if stick else exps(g, nch - 1)

            each_group(act, group)
            if not stick:
                for g in range(groups):
                    act.activation(share[:, g, :], nmax[:, g, :], ACT.Exp, bias=nmax[:, g, nch:nch + 1], scale=-1.0).then_inc(step_act, 1)

        @block.vector
        def _(dve):
            dve.nop().then_inc(pT_copied, 1)
            dve.nop().then_inc(acc_done, 2)
            dve.nop().then_inc(sc_read, 2)
            strict = kept.consts[:, C_STRICT:C_STRICT + NT]
            if stick:
                dve.nop().then_inc(soft_done, 1)
                dve.wait_ge(step_act, 3)
                dve.scalar_tensor_tensor(soft_new[:], sc_new[:], 0.0, soft_new[:], ALU.max, ALU.add).then_inc(step_dve, 1)
                dve.wait_ge(step_dve, 1)
                dve.tensor_tensor(soft_new[:], soft_new[:], strict.unsqueeze(1).to_broadcast([P, groups, NT]), ALU.mult).then_inc(step_dve, 1)
                dve.wait_ge(step_dve, 2)
                for g in range(groups):
                    back = soft_new[:, g, ::-1]
                    dve.tensor_tensor_scan(back, back, back, 0.0, ALU.add, ALU.bypass).then_inc(step_dve, 1)
                dve.wait_ge(step_dve, 2 + groups)
                dve.tensor_tensor(log_new[:], sc_new[:], soft_new[:], ALU.subtract).then_inc(step_dve, 1)
                dve.wait_ge(step_act, 4)
                dve.tensor_tensor(prob_new[:, :, 0:NT], prob_new[:, :, 0:NT], strict.unsqueeze(1).to_broadcast([P, groups, NT]), ALU.mult).then_inc(new_prob, 1)
            else:
                for i in range(2):
                    if i == 0 and new_biases:
                        dve.wait_ge(bias_in, 16 * per * NT)
                        mask_new(bias).then_inc(step_dve, 1)
                    elif i == 0 and nch == 1:
                        dve.tensor_tensor(bias[:, 0:NT], bias[:, 0:NT], kept.consts[:, C_WM:C_WM + NT], ALU.add).then_inc(step_dve, 1)
                    else:
                        dve.nop().then_inc(step_dve, 1)
                dve.wait_ge(step_dve, 2)
                dve.wait_ge(new_scored, 1)
                dve.tensor_tensor(log_new[:], sc_new[:], bias[:, past:].unsqueeze(1).to_broadcast([P, groups, NT]), ALU.add).then_inc(step_dve, 1)
                dve.wait_ge(step_dve, 3)
                dve.tensor_reduce(nmax[:, :, 0], log_new[:], AX.X, ALU.max, negate=True).then_inc(maxed, 1)
            dve.wait_ge(new_turned, 1)
            dve.tensor_copy(pT_new[:], qp[0:NT, 0:groups, :]).then_inc(new_copied, 1)
            dve.wait_ge(new_summed, 1)
            half = groups // 2
            for i in range(2):
                dve.tensor_copy(acc[:, i * half:(i + 1) * half, :], pv[i][:].rearrange("p (g c) -> p g c", c=width)).then_inc(new_acc, 1)
            dve.wait_ge(new_acc, 2)

            def limit(g, c):
                n = c + g * nch
                at = parity(g, c)
                here = slice(data(c) * CH, (data(c) + 1) * CH)
                one = lambda x, k: x[:, bass.ds(g, 1), k:k + 1].rearrange("p o k -> p (o k)")
                dve.wait_ge(scored, (n + 1) * items + 2)
                dve.wait_ge(probs_turned, n + 1)
                dve.tensor_tensor(prob[at][:], sc[at][:], bias[:, here], ALU.add).then_inc(sc_read, 1)
                dve.wait_ge(sc_read, n + 3)
                dve.tensor_reduce(one(nstep, c + 1), prob[at][:], AX.X, ALU.max, negate=True).then_inc(step_dve, 1)
                dve.wait_ge(step_dve, n + 4)
                dve.wait_ge(maxed, n + 1)
                dve.tensor_tensor(one(nmax, c + 1), one(nstep, c + 1), one(nmax, c), ALU.min).then_inc(maxed, 1)

            def sum_back(g, c):
                n = c + g * nch
                at = parity(g, c)
                carried = soft[1 - at][:, 0:1] if c else soft_new[:, g, 0:1]
                dve.wait_ge(soft_step, n * 3 + 3)
                k = n * 2 + 2 + groups + 1
                dve.scalar_tensor_tensor(soft[at][:], sc[at][:], 0.0, soft[at][:], ALU.max, ALU.add).then_inc(step_dve, 1)
                dve.wait_ge(step_dve, k + 1)
                dve.tensor_tensor_scan(soft[at][:, ::-1], soft[at][:, ::-1], soft[at][:, ::-1], carried, ALU.add, ALU.bypass).then_inc(step_dve, 1)
                dve.wait_ge(step_dve, k + 2)
                dve.wait_ge(probs_turned, n + 1)
                dve.tensor_tensor(prob[at][:], sc[at][:], soft[at][:], ALU.subtract).then_inc(sc_read, 1)
                dve.wait_ge(sc_read, n + 3)
                dve.nop().then_inc(soft_done, 1)

            def copy_probs(g, c):
                n = c + g * nch
                dve.wait_ge(probs_turned, n + 3)
                dve.wait_ge(v_used, (n - 1 + SLOTS) * per)
                dve.tensor_copy(pT[parity(g, c)][:], qp[:]).then_inc(pT_copied, 1)

            def add_up(g, c):
                n = c + g * nch
                dve.wait_ge(v_used, (n + 1 + SLOTS) * per)
                to = acc[:, bass.ds(g, 1), :].rearrange("p o c -> p (o c)")
                new = pv[parity(g, c)][:, 0:width]
                dve.wait_ge(acc_done, n + 2)
                if stick:
                    dve.tensor_tensor(to, to, new, ALU.add).then_inc(acc_done, 1)
                else:
                    dve.wait_ge(shrunk, n + 1)
                    by = shrink[:, bass.ds(g, 1), c + 1:c + 2].rearrange("p o k -> p (o k)")
                    dve.scalar_tensor_tensor(to, to, by, new, ALU.mult, ALU.add).then_inc(acc_done, 1)

            def best(steps):
                for i in steps:
                    if i:
                        dve.wait_ge(top_step, i)
                    if i % 2 == 0:
                        dve.max(top8[:], kept.scores[:]).then_inc(top_step, 1)
                    else:
                        dve.match_replace(kept.scores[:], top8[:], kept.scores[:], GONE).then_inc(top_step, 1)

            def group(g):
                for c in range(nch):
                    if not stick:
                        if before(g, c):
                            copy_probs(*before(g, c))
                        limit(g, c)
                        if before(g, c):
                            add_up(*before(g, c))
                    else:
                        first = (g * nch + c) * 4
                        if c:
                            sum_back(g, c - 1)
                        best([first])
                        if c:
                            copy_probs(g, c - 1)
                        best([first + 1])
                        if c:
                            add_up(g, c - 1)
                        best([first + 2, first + 3])
                if stick:
                    sum_back(g, nch - 1)
                if ends(g):
                    copy_probs(g, nch - 1)
                    add_up(g, nch - 1)

            each_group(dve, group, unroll=stick)
            if stick:
                dve.wait_ge(top_step, TOPK_S // 4)
                dve.tensor_scalar(kept.drop[:], kept.scores[:], GONE / 2, NEG, ALU.is_gt, ALU.mult)
                dve.wait_ge(acc_done, groups * nch + 2)
                dve.nop().then_inc(acc_ready, 1)
            else:
                k = groups * nch + 3
                dve.wait_ge(step_act, groups)
                dve.wait_ge(probs, groups * nch + 2)
                dve.wait_ge(new_prob, groups)
                dve.tensor_tensor(sums[:], sums[:], share[:], ALU.mult).then_inc(step_dve, 1)
                dve.wait_ge(step_dve, k + 1)
                dve.tensor_reduce(rcp[:], sums[:], AX.X, ALU.add).then_inc(step_dve, 1)
                dve.wait_ge(step_dve, k + 2)
                dve.tensor_scalar(rcp[:], rcp[:], 1e-30, None, ALU.max).then_inc(step_dve, 1)
                dve.wait_ge(step_dve, k + 3)
                dve.reciprocal(rcp[:], rcp[:]).then_inc(step_dve, 1)
                dve.wait_ge(step_dve, k + 4)
                if gate is not None:
                    dve.tensor_tensor(rcp[:], rcp[:], kept.gates[:, :, gate], ALU.mult).then_inc(step_dve, 1)
                    dve.wait_ge(step_dve, k + 5)
                dve.wait_ge(acc_done, groups * nch + 2)
                dve.tensor_tensor(acc[:], acc[:], rcp[:].unsqueeze(2).to_broadcast([P, groups, width]), ALU.mult).then_inc(acc_ready, 1)
            dve.wait_ge(acc_turned, 1)
            each = (stride // heads) // NT if stick else 3
            for g in range(groups):
                for h in range(heads):
                    i = g * heads + h
                    n = each * NT
                    got = tp[i // 4][:, i % 4 * P:(i % 4 + 1) * P].rearrange("p (b r) -> p b r", b=per)[:, :, h * n:(h + 1) * n]
                    got = got.rearrange("p b (j t) -> p b j t", t=NT)
                    to = kept.oTs[:, head0 + h * each:head0 + (h + 1) * each, g * per * NT:(g + 1) * per * NT].rearrange("p j (b t) -> p b j t", t=NT)
                    if add:
                        last = dve.tensor_tensor(to, to, got, ALU.add)
                    else:
                        last = dve.tensor_copy(to, got)
            last.then_inc(out_done, 1)
            for to, _ in new_biases[1:]:
                dve.wait_ge(later_in, 16 * per * NT)
                mask_new(to).then_inc(out_done, 1)


def stick_breaking(nc, io, kept):
    stream(nc, io, kept, "sb", cache=io.sb_cache, col=0, proj_v=SB_V, heads=4, per=4, q=kept.q_sb, k_new=kept.k_sb,
           head0=0, stick=True)


def dsa_sample(nc, io, kept):
    def keys(c):
        return kept.drop[:, PAST:KEYS] if c is None else kept.drop[:, c * CH:(c + 1) * CH]

    stream(nc, io, kept, "dsa", cache=io.dsa_cache, col=0, proj_v=DSA_V, heads=2, per=2, q=kept.q_dsa, k_new=kept.k_dsa,
           select=kept.sel_d, dropped_keys=keys, bias=kept.bias_dsa, new_biases=((kept.bias_dsa, 0), (kept.bias_nsa, 6)), head0=4)


def cmp_sample(nc, io, kept):
    with ExitStack() as ctx:
        s = Scope(nc, ctx, "ca")
        bias = s.sb("bias", [P, PAST])
        prob = s.sb("prob", [P, 4, NC])
        gated = s.sb("gated", [P, 4, NC])
        pT = s.sb("pT", [P, 4, P])
        nmax, sums, rcp = s.sb("nmax", [P, 4]), s.sb("sums", [P, 4]), s.sb("rcp", [P, 4])
        imp = s.sb("imp", [P, NSB])
        top8 = s.sb("top8", [P, 8])
        sc = s.ps("sc", [P, 4, NC])
        ip = s.ps("ip", [P, NC])
        tp = s.ps("tp", [P, 4, P])
        ov = s.ps("ov", [P, 4, P])
        zeroed, bias_in, scored, step, exped, normed, gate_done, imp_summed, turned, copied, out_summed, out_done = (
            s.sem(n) for n in ("zeroed", "bias_in", "scored", "step", "exped", "normed", "gate_done", "imp_summed", "turned",
                               "copied", "out_summed", "out_done"))
        block = ctx.enter_context(nc.Block())

        @block.gpsimd
        def _(pool):
            pool.memset(bias[:], 0.0).then_inc(zeroed, 1)

        @block.sync
        def _(sp):
            sp.wait_ge(zeroed, 1)
            for b in range(2):
                for t in range(NT):
                    sp.dma_start(bias[b * 64 + t:b * 64 + t + 41:8, :], io.line[6:12, NT - 1 - t:NT - 1 - t + PAST]).then_inc(bias_in, 16)

        @block.tensor
        def _(pe):
            for g in range(4):
                for j in range(4):
                    b, kv = divmod(j, 2)
                    last = pe.matmul(sc[b * 64:b * 64 + 64, g, :], kept.q_nsa[:, 2 * g + b, kv, :], kept.cmp_k[:, 2 * g + b, kv, :],
                                     start=(kv == 0), stop=(kv == 1), skip_group_check=True, tile_position=(0, b * 64))
            last.then_inc(scored, 1)
            pe.wait_ge(normed, 1)
            for g in range(4):
                last = pe.matmul(ip[:], kept.consts[:, C_SELG + g * P:C_SELG + (g + 1) * P], prob[:, g, :], start=(g == 0), stop=(g == 3))
            last.then_inc(imp_summed, 1)
            pe.wait_ge(gate_done, 1)
            for g in range(4):
                last = pe.transpose(tp[:, g, :], gated[:, g, :], kept.ident)
            last.then_inc(turned, 1)
            pe.wait_ge(copied, 1)
            for g in range(4):
                for j in range(4):
                    b, kv = divmod(j, 2)
                    r = b * 64 + kv * 24
                    last = pe.matmul(ov[:, g, r:r + 24], kept.cmp_v[:, 2 * g + b, kv, :], pT[:, g, r:r + 24], start=True, stop=True, skip_group_check=True)
            last.then_inc(out_summed, 1)

        @block.scalar
        def _(act):
            act.wait_ge(step, 2)
            for g in range(4):
                last = act.activation(prob[:, g, :], prob[:, g, :], ACT.Exp, bias=nmax[:, g:g + 1], accum_out=sums[:, g:g + 1])
            last.then_inc(exped, 1)
            act.wait_ge(turned, 1)
            act.copy(pT[:], tp[:]).then_inc(copied, 1)

        @block.vector
        def _(dve):
            dve.wait_ge(bias_in, 16 * 16)
            dve.wait_ge(scored, 1)
            ends = bias[:, CMPB - 1::CMPB].unsqueeze(1).to_broadcast([P, 4, NC])
            dve.tensor_tensor(prob[:], sc[:], ends, ALU.add).then_inc(step, 1)
            dve.wait_ge(step, 1)
            dve.tensor_reduce(nmax[:], prob[:], AX.X, ALU.max, negate=True).then_inc(step, 1)
            dve.wait_ge(exped, 1)
            dve.tensor_scalar(rcp[:], sums[:], 1e-30, None, ALU.max).then_inc(step, 1)
            dve.wait_ge(step, 3)
            dve.reciprocal(rcp[:], rcp[:]).then_inc(step, 1)
            dve.wait_ge(step, 4)
            dve.tensor_tensor(prob[:], prob[:], rcp[:].unsqueeze(2).to_broadcast([P, 4, NC]), ALU.mult).then_inc(normed, 1)
            dve.wait_ge(normed, 1)
            dve.tensor_tensor(gated[:], prob[:], kept.gates[:, :, 0:1].to_broadcast([P, 4, NC]), ALU.mult).then_inc(gate_done, 1)
            dve.memset(imp[:], 1e4).then_inc(step, 1)
            dve.wait_ge(imp_summed, 1)
            dve.wait_ge(step, 5)
            dve.tensor_reduce(imp[:, 1:NSB - 2], ip[:].rearrange("p (n a) -> p n a", a=2)[:, 1:NSB - 2, :], AX.X, ALU.add).then_inc(step, 1)
            for n in range(SLC_TOPN // 8):
                dve.wait_ge(step, 6 + 2 * n)
                dve.max(top8[:], imp[:]).then_inc(step, 1)
                dve.wait_ge(step, 7 + 2 * n)
                dve.match_replace(imp[:], top8[:], imp[:], GONE).then_inc(step, 1)
            dve.wait_ge(step, 10)
            dve.tensor_scalar(kept.drop_blk[:], imp[:], GONE / 2, NEG, ALU.is_gt, ALU.mult).then_inc(step, 1)
            dve.wait_ge(out_summed, 1)
            for b in range(NB):
                r = b % 2 * 64
                last = dve.tensor_copy(kept.oTs[:, 10:16, b * NT:(b + 1) * NT], ov[:, b // 2, r:r + 48].rearrange("p (h t) -> p h t", t=NT))
            last.then_inc(out_done, 1)


def slc_sample(nc, io, kept):
    def keys(c):
        if c is None:
            return kept.drop_blk[:, NSB - 1:NSB].to_broadcast([P, NT])
        return kept.drop_blk[:, c * 8:(c + 1) * 8].unsqueeze(2).to_broadcast([P, 8, SLCB])

    stream(nc, io, kept, "slc", cache=io.nsa_cache, col=512, proj_v=NSA_VS, heads=2, per=2, q=kept.q_nsa, k_new=kept.k_slc,
           select=kept.sel_e, dropped_keys=keys, bias=kept.bias_nsa, head0=10, gate=1, add=True)


def win_sample(nc, io, kept):
    stream(nc, io, kept, "win", cache=None, state=io.win_state, col=0, proj_v=NSA_VW, heads=2, per=2, q=kept.q_nsa,
           k_new=kept.k_win, bias=kept.bias_nsa[:, PAST - WIN:], head0=10, gate=2, add=True)


def prompt_prepare(nc, io, kept, keep):
    kept.qT = keep.sb("qT", [P, 16, SEQ])
    kept.kT = keep.sb("kT", [P, 10, SEQ])
    kept.v = keep.sb("v", [P, 4, 10 * DH])
    kept.bias = keep.sb("bias", [P, HB, XW])
    kept.dropp = keep.sb("dropp", [P, 4, SEQ], BF16)
    kept.score = keep.sb("score", [P, 4, SEQ])
    kept.pgates = keep.sb("pgates", [P, 4, 18])
    kept.pmask = keep.sb("pmask", [P, C_END - C_PM])
    with ExitStack() as ctx:
        s = Scope(nc, ctx, "pp")
        rows = [s.sb(f"rows{i}", [P, 4, 2 * DH]) for i in range(3)]
        iq = s.sb("iq", [64, 4, SEQ])
        ik = s.sb("ik", [64, SEQ])
        iw = s.sb("iw", [P, 4, 4])
        relu = [s.sb(f"relu{i}", [P, SEQ]) for i in range(2)]
        score = kept.score
        tp = [s.ps(f"tp{i}", [P, SEQ]) for i in range(4)]
        sc = [s.ps(f"sc{i}", [P, SEQ]) for i in range(2)]
        pairs = [SB_Q, SB_Q + 256] + [DSA_Q + 256 * i for i in range(3)] + [NSA_Q + 256 * i for i in range(3)]
        n_q = len(pairs)
        pairs += [SB_K, SB_K + 256, DSA_K, NSA_KS, NSA_KW, IDX_Q, IDX_K]
        n_full = len(pairs) - 2
        rows_in = [s.sem(f"rows_in{i}") for i in range(3)]
        v_in, bias_in, small_in, mask_in = s.sem("v_in"), s.sem("bias_in"), s.sem("small_in"), s.sem("mask_in")
        turned, copied_a, copied_d, gated, biased = s.sem("turned"), s.sem("copied_a"), s.sem("copied_d"), s.sem("gated"), s.sem("biased")
        scored, rectified, weighted, idx_copied = (s.sem("scored"), s.sem("rectified"), s.sem("weighted"), s.sem("idx_copied"))
        block = ctx.enter_context(nc.Block())
        n_items = 2 * len(pairs) - 1
        idx_units = [(i, h) for i in range(1, 4) for h in range(4)]

        @block.sync
        def _(sp):
            for i, col in enumerate(pairs):
                if i >= 3:
                    sp.wait_ge(turned, 2 * (i - 2))
                width = 2 * DH if i < len(pairs) - 1 else DH
                sp.dma_start(rows[i % 3][:, :, 0:width], io.proj[0:SEQ, col:col + width].rearrange("(m p) n -> p m n", p=P)).then_inc(rows_in[i % 3], 16)
            sp.wait_ge(v_in, 16 * 4)
            sp.wait_ge(small_in, 32)

        @block.gpsimd
        def _(pool):
            with nc.allow_non_contiguous_dma(reason="a few numbers per row"):
                pool.dma_start(iw[:], io.proj[0:SEQ, IDX_W:IDX_W + 4].rearrange("(m p) n -> p m n", p=P)).then_inc(small_in, 16)
                pool.dma_start(kept.pgates[:], io.proj[0:SEQ, NSA_BG:NSA_BG + 18].rearrange("(m p) n -> p m n", p=P)).then_inc(small_in, 16)

        @block.scalar
        def _(act):
            act.preload_act_table_set("natural_log_exp_and_others")
            act.dma_start(kept.pmask[:], io.consts[:, C_PM:C_END]).then_inc(mask_in, 16)
            src = bass.AP(io.lines.tensor, P - 1, [[HB * XL - 1, P], [XL, HB], [1, XW]])
            act.dma_start(kept.bias[:], src).then_inc(bias_in, 16)
            for to, col, n in ((0, SB_V, 4), (4, DSA_V, 2), (6, NSA_VS, 2), (8, NSA_VW, 2)):
                act.dma_start(kept.v[:, :, to * DH:(to + n) * DH], io.proj[0:SEQ, col:col + n * DH].rearrange("(m p) n -> p m n", p=P)).then_inc(v_in, 16)
            for n in range(1, 2 * n_full, 2):
                act.wait_ge(turned, n + 1)
                if n // 2 < n_q:
                    act.activation(kept.qT[:, n, :], tp[n % 4][:], ACT.Copy, scale=SCALE).then_inc(copied_a, 1)
                else:
                    act.copy(kept.kT[:, n - 2 * n_q, :], tp[n % 4][:]).then_inc(copied_a, 1)
            act.wait_ge(small_in, 32)
            act.activation(kept.pgates[:], kept.pgates[:], ACT.Exp, scale=-1.0).then_inc(gated, 1)
            for u in range(len(idx_units)):
                i, h = idx_units[u]
                w = (i + 1) * P
                act.wait_ge(scored, u + 1)
                if u >= 2:
                    act.wait_ge(weighted, u - 1)
                act.activation(relu[u % 2][:, 0:w], sc[u % 2][:, 0:w], ACT.Relu).then_inc(rectified, 1)

        @block.tensor
        def _(pe):
            for n in range(n_items):
                i, j = divmod(n, 2)
                if j == 0:
                    pe.wait_ge(rows_in[i % 3], 16 * (i // 3 + 1))
                if n >= 4:
                    pe.wait_ge(copied_a if n % 2 else copied_d, (n - 4) // 2 + 1)
                for m in range(4):
                    last = pe.transpose(tp[n % 4][:, m * P:(m + 1) * P], rows[i % 3][:, m, j * DH:(j + 1) * DH], kept.ident)
                last.then_inc(turned, 1)
            pe.wait_ge(idx_copied, 5)
            for u, (i, h) in enumerate(idx_units):
                w = (i + 1) * P
                if u >= 2:
                    pe.wait_ge(rectified, u - 1)
                pe.matmul(sc[u % 2][:, 0:w], iq[:, h, i * P:(i + 1) * P], ik[:, 0:w], start=True, stop=True).then_inc(scored, 1)

        @block.vector
        def _(dve):
            for n in range(0, 2 * n_full, 2):
                dve.wait_ge(turned, n + 1)
                if n // 2 < n_q:
                    dve.tensor_scalar(kept.qT[:, n, :], tp[n % 4][:], SCALE, None, ALU.mult).then_inc(copied_d, 1)
                else:
                    dve.tensor_copy(kept.kT[:, n - 2 * n_q, :], tp[n % 4][:]).then_inc(copied_d, 1)
            for n in range(2 * n_full, n_items):
                j = n - 2 * n_full
                dve.wait_ge(turned, n + 1)
                for half in range(2 if j < 2 else 1):
                    to = iq[:, 2 * j + half, :] if j < 2 else ik[:]
                    dve.tensor_copy(to, tp[n % 4][64 * half:64 * half + 64, :]).then_inc(idx_copied, 1)
            dve.wait_ge(mask_in, 16)
            dve.wait_ge(small_in, 32)
            pm = kept.pmask[:, 0:XW]
            for u, (i, h) in enumerate(idx_units):
                w = (i + 1) * P
                dve.wait_ge(rectified, u + 1)
                if h:
                    dve.wait_ge(weighted, u)
                before = score[:, i, 0:w] if h else pm[:, SEQ - i * P:SEQ - i * P + w]
                dve.scalar_tensor_tensor(score[:, i, 0:w], relu[u % 2][:, 0:w], iw[:, i, h:h + 1], before, ALU.mult, ALU.add).then_inc(weighted, 1)
            dve.wait_ge(gated, 1)
            dve.tensor_scalar(kept.pgates[:], kept.pgates[:], 1.0, None, ALU.add).then_inc(gated, 1)
            dve.wait_ge(gated, 2)
            dve.reciprocal(kept.pgates[:], kept.pgates[:]).then_inc(gated, 1)
            dve.wait_ge(bias_in, 16)
            dve.tensor_tensor(kept.bias[:], kept.bias[:], pm.unsqueeze(1).to_broadcast([P, HB, XW]), ALU.add).then_inc(biased, 1)


class Unit:

    def __init__(self, kind, out, tile, q, k, v, bias, gate, first, last):
        self.kind, self.out, self.tile, self.q, self.k, self.v = kind, out, tile, q, k, v
        self.bias, self.gate, self.first, self.last = bias, gate, first, last
        self.off = SEQ - tile * P
        self.w = (tile + 1) * P
        self.blocks = self.w // CMPB
        self.u = None


class Links:

    def __init__(self, sem):
        self.sem, self.n = sem, 0

    def step(self, ins):
        self.n += 1
        ins.then_inc(self.sem, 1)
        return self.n


def prompt_attention(nc, io, kept, keep):
    units = []
    for h in range(4):
        for i in range(4):
            units.append(Unit("stick", h, i, h, h, h, None, None, True, True))
    n_stick = len(units)
    for h in range(6):
        for i in range(4):
            units.append(Unit("dsa", 4 + h, i, 4 + h, 4 + h // 3, 4 + h // 3, h, None, True, True))
    for h in range(6):
        for i in range(4):
            units.append(Unit("slc", 10 + h, i, 10 + h, 6 + h // 3, 6 + h // 3, 6 + h, 6 + h, True, False))
            units.append(Unit("win", 10 + h, i, 10 + h, 8 + h // 3, 8 + h // 3, 6 + h, 12 + h, False, False))
            units.append(Unit("cmp", 10 + h, i, 10 + h, h // 3, h // 3, 6 + h, h, False, True))
    N = len(units)
    for u, x in enumerate(units):
        x.u = u
    outs = [x.u for x in units if x.last and x.tile == 3]

    with ExitStack() as ctx:
        s = Scope(nc, ctx, "pa")
        L = [s.sb(f"logits{i}", [P, XW]) for i in range(4)]
        soft = s.sb("soft", [P, SEQ])
        top8 = s.sb("top8", [P, 3, 8])
        pT = [s.sb(f"pT{i}", [P, 4, P]) for i in range(2)]
        nmax, sums, rcp = s.sb("nmax", [P, N]), s.sb("sums", [P, N]), s.sb("rcp", [P, N])
        sc = [s.ps(f"sc{i}", [P, SEQ]) for i in range(2)]
        tp = [s.ps(f"tp{i}", [P, 4, P]) for i in range(2)]
        ov = [s.ps(f"ov{i}", [P, 4, P]) for i in range(2)]
        cleared, scored, added, padded, maxed, exped, rcp_ready, ready_stick, ready = (
            s.sem(n) for n in ("cleared", "scored", "added", "padded", "maxed", "exped", "rcp_ready", "ready_stick", "ready"))
        turned, copied, multiplied, out_done = s.sem("turned"), [s.sem("copied_even"), s.sem("copied_odd")], s.sem("multiplied"), s.sem("out_done")
        soft_act, soft_dve, small = s.sem("soft_act"), s.sem("soft_dve"), s.sem("small")
        top_step, dropped = s.sem("top_step"), s.sem("dropped")
        block = ctx.enter_context(nc.Block())
        assert n_stick >= TOPK_P // 8
        wins = [x.u for x in units if x.kind == "win"]

        def view(x):
            if x.kind == "cmp":
                return L[x.u % 4][:, 0:x.blocks]
            return L[x.u % 4][:, x.off:x.off + x.w]

        def all_of(x):
            return L[x.u % 4][:, 0:XW] if x.kind == "win" else view(x)

        @block.tensor
        def _(pe):
            def score(x):
                if x.u >= 2:
                    pe.wait_ge(added, x.u - 1)
                q = kept.qT[:, x.q, x.tile * P:(x.tile + 1) * P]
                if x.kind == "cmp":
                    pe.matmul(sc[x.u % 2][:, 0:x.blocks], q, kept.cmp_kp[:, x.k, 0:x.blocks], start=True, stop=True).then_inc(scored, 1)
                    return
                dropping = x.kind == "dsa" and x.tile > 0
                if dropping:
                    pe.wait_ge(dropped, 3)
                    pe.matmul(sc[x.u % 2][:, 0:x.w], kept.ident_b[:], kept.dropp[:, x.tile, 0:x.w], start=True, stop=False)
                pe.matmul(sc[x.u % 2][:, 0:x.w], q, kept.kT[:, x.k, 0:x.w], start=not dropping, stop=True).then_inc(scored, 1)

            def turn(x):
                if x.kind == "stick":
                    pe.wait_ge(ready_stick, x.u + 1)
                else:
                    pe.wait_ge(ready, x.u - n_stick + 1)
                if x.u >= 2:
                    pe.wait_ge(copied[x.u % 2], x.u // 2)
                if x.kind == "cmp":
                    last = pe.transpose(tp[x.u % 2][:, 0, :], L[x.u % 4][:, 0:P], kept.ident)
                else:
                    for j in range(x.tile + 1):
                        last = pe.transpose(tp[x.u % 2][:, j, :], view(x)[:, j * P:(j + 1) * P], kept.ident)
                last.then_inc(turned, 1)

            def product(x):
                pe.wait_ge(copied[x.u % 2], x.u // 2 + 1)
                if x.tile == 0 and x.first and x.out >= 2:
                    pe.wait_ge(out_done, x.out - 1)
                to = ov[x.out % 2][:, x.tile, :]
                if x.kind == "cmp":
                    last = pe.matmul(to, kept.cmp_vp[0:x.blocks, x.v, :], pT[x.u % 2][0:x.blocks, 0, :], start=False, stop=True, skip_group_check=True)
                else:
                    for j in range(x.tile + 1):
                        last = pe.matmul(to, kept.v[:, j, x.v * DH:(x.v + 1) * DH], pT[x.u % 2][:, j, :],
                                         start=(x.first and j == 0), stop=(x.last and j == x.tile), skip_group_check=True)
                last.then_inc(multiplied, 1)

            pe.wait_ge(cleared, 4)
            for u in range(N + 3):
                if u < N:
                    score(units[u])
                if 2 <= u < N + 2:
                    turn(units[u - 2])
                if u >= 3:
                    product(units[u - 3])

        def copy(eng, x):
            eng.wait_ge(turned, x.u + 1)
            if x.u >= 2:
                eng.wait_ge(multiplied, x.u - 1)
            do = eng.copy if x.u % 2 else eng.tensor_copy
            n = 1 if x.kind == "cmp" else x.tile + 1
            rows = x.blocks if x.kind == "cmp" else P
            do(pT[x.u % 2][0:rows, 0:n, :], tp[x.u % 2][0:rows, 0:n, :]).then_inc(copied[x.u % 2], 1)

        @block.gpsimd
        def _(pool):
            for i in range(4):
                pool.memset(L[i][:], 0.0).then_inc(cleared, 1)
            pool.wait_ge(cleared, 4)

            def normalise(x):
                if x.kind == "stick":
                    return
                pool.wait_ge(rcp_ready, x.u - n_stick + 1)
                v = view(x)
                pool.tensor_scalar(v, v, rcp[:, x.u:x.u + 1], 1.0, ALU.mult, ALU.mult).then_inc(ready, 1)

            for u in range(N + 1):
                if u < N and units[u].kind == "win":
                    pool.wait_ge(turned, u - 3)
                    x = units[u]
                    if x.off:
                        pool.tensor_copy(L[u % 4][:, 0:x.off], kept.bias[:, x.bias, 0:x.off]).then_inc(padded, 1)
                if u:
                    normalise(units[u - 1])

        @block.scalar
        def _(act):
            act.preload_act_table_set("natural_log_exp_and_others")
            chain = Links(soft_act)

            def exp(x):
                if x.kind == "stick":
                    act.wait_ge(scored, x.u + 1)
                    if x.u:
                        act.wait_ge(soft_dve, 4 * x.u)
                    t = soft[:, 0:x.w]
                    act.wait_ge(soft_act, chain.step(act.activation(t, sc[x.u % 2][:, 0:x.w], ACT.Abs)))
                    act.wait_ge(soft_act, chain.step(act.activation(t, t, ACT.Exp, scale=-1.0)))
                    chain.step(act.activation(t, t, ACT.Ln, bias=1.0))
                    return
                act.wait_ge(maxed, x.u - n_stick + 1)
                act.activation(all_of(x), all_of(x), ACT.Exp, bias=nmax[:, x.u:x.u + 1], accum_out=sums[:, x.u:x.u + 1]).then_inc(exped, 1)

            def exp_stick(x):
                act.wait_ge(soft_dve, 4 * x.u + 4)
                act.activation(view(x), view(x), ACT.Exp).then_inc(exped, 1)

            for u in range(N + 3):
                if 1 <= u <= n_stick:
                    exp_stick(units[u - 1])
                if u < N:
                    exp(units[u])
                if 2 <= u < N + 2 and u % 2:
                    copy(act, units[u - 2])

        @block.vector
        def _(dve):
            chain = Links(small)
            tri = kept.pmask[:, C_TRI - C_PM:C_TRI - C_PM + P]
            dve.wait_ge(cleared, 4)

            def add(x):
                if x.u >= 4:
                    dve.wait_ge(turned, x.u - 3)
                v = view(x)
                if x.kind == "stick":
                    t = soft[:, 0:x.w]
                    z = sc[x.u % 2][:, 0:x.w]
                    dve.wait_ge(soft_act, 3 * x.u + 3)
                    dve.scalar_tensor_tensor(t, z, 0.0, t, ALU.max, ALU.add).then_inc(soft_dve, 1)
                    dve.wait_ge(soft_dve, 4 * x.u + 1)
                    d = soft[:, x.w - P:x.w]
                    dve.tensor_tensor(d, d, tri, ALU.mult).then_inc(soft_dve, 1)
                    dve.wait_ge(soft_dve, 4 * x.u + 2)
                    dve.tensor_tensor_scan(t[:, ::-1], t[:, ::-1], t[:, ::-1], 0.0, ALU.add, ALU.bypass).then_inc(soft_dve, 1)
                    dve.wait_ge(soft_dve, 4 * x.u + 3)
                    dve.tensor_tensor(v, z, t, ALU.subtract).then_inc(soft_dve, 1)
                    dve.wait_ge(soft_dve, 4 * x.u + 4)
                    dve.nop().then_inc(added, 1)
                    return
                dve.wait_ge(scored, x.u + 1)
                if x.kind == "cmp":
                    b = kept.bias[:, x.bias, x.off + CMPB - 1:x.off + x.w:CMPB]
                    dve.tensor_tensor(v, sc[x.u % 2][:, 0:x.blocks], b, ALU.add).then_inc(added, 1)
                else:
                    dve.tensor_tensor(v, sc[x.u % 2][:, 0:x.w], kept.bias[:, x.bias, x.off:x.off + x.w], ALU.add).then_inc(added, 1)
                dve.wait_ge(added, x.u + 1)
                if x.kind == "win":
                    dve.wait_ge(padded, wins.index(x.u) + 1)
                dve.tensor_reduce(nmax[:, x.u:x.u + 1], all_of(x), AX.X, ALU.max, negate=True).then_inc(maxed, 1)

            def invert(x):
                dve.wait_ge(exped, x.u + 1)
                if x.kind == "stick":
                    d = view(x)[:, x.w - P:x.w]
                    dve.tensor_tensor(d, d, tri, ALU.mult).then_inc(ready_stick, 1)
                    return
                r = rcp[:, x.u:x.u + 1]
                if x.kind == "cmp" and x.tile == 0:
                    v = view(x)
                    cm = kept.pmask[:, C_CM - C_PM:C_CM - C_PM + x.blocks]
                    dve.wait_ge(small, chain.step(dve.scalar_tensor_tensor(v, v, 1.0, cm, ALU.mult, ALU.mult, accum_out=sums[:, x.u:x.u + 1])))
                dve.wait_ge(small, chain.step(dve.tensor_scalar(r, sums[:, x.u:x.u + 1], 1e-30, None, ALU.max)))
                if x.gate is None:
                    dve.reciprocal(r, r).then_inc(rcp_ready, 1)
                else:
                    dve.wait_ge(small, chain.step(dve.reciprocal(r, r)))
                    dve.tensor_tensor(r, r, kept.pgates[:, x.tile, x.gate:x.gate + 1], ALU.mult).then_inc(rcp_ready, 1)

            def best(r):
                if r:
                    dve.wait_ge(top_step, r * 6)
                for i in range(1, 4):
                    dve.max(top8[:, i - 1, :], kept.score[:, i, 0:(i + 1) * P]).then_inc(top_step, 1)
                for i in range(1, 4):
                    dve.wait_ge(top_step, r * 6 + i)
                    dve.match_replace(kept.score[:, i, 0:(i + 1) * P], top8[:, i - 1, :], kept.score[:, i, 0:(i + 1) * P], GONE).then_inc(top_step, 1)

            for u in range(N + 4):
                if u < N:
                    add(units[u])
                if u < TOPK_P // 8:
                    best(u)
                if u == TOPK_P // 8 - 1:
                    dve.wait_ge(top_step, TOPK_P // 8 * 6)
                    for i in range(1, 4):
                        dve.tensor_scalar(kept.dropp[:, i, 0:(i + 1) * P], kept.score[:, i, 0:(i + 1) * P], GONE / 2, NEG, ALU.is_gt, ALU.mult).then_inc(dropped, 1)
                if 1 <= u <= N:
                    invert(units[u - 1])
                if 2 <= u < N + 2 and u % 2 == 0:
                    copy(dve, units[u - 2])
                if u - 4 in outs:
                    dve.wait_ge(multiplied, u - 3)
                    h = units[u - 4].out
                    dve.tensor_copy(kept.oT[:, h, :].rearrange("p (m t) -> p m t", m=4), ov[h % 2][:]).then_inc(out_done, 1)


def finish(nc, io, kept, keep):
    with ExitStack() as ctx:
        s = Scope(nc, ctx, "fin")
        w = s.sb("w", [P, 16, D])
        gate = s.sb("gate", [P, D])
        sig = s.sb("sig", [P, D])
        gain = s.sb("gain", [P, D])
        y = s.sb("y", [P, D])
        x = sig
        sq = s.sb("sq", [P, CH])
        ss, rstd = s.sb("ss", [P, 5, 4]), s.sb("rstd", [P, 5])
        tp = [s.ps(f"tp{i}", [P, 4, P]) for i in range(2)]
        yp = [s.ps(f"yp{i}", [P, CH]) for i in range(4)]
        w_in = [s.sem(f"w_in{c}") for c in range(4)]
        gain_in, gate_in, x_in = s.sem("gain_in"), s.sem("gate_in"), s.sem("x_in")
        sig_exp, sig_step, gate_ready, turned, gated = s.sem("sig_exp"), s.sem("sig_step"), s.sem("gate_ready"), s.sem("turned"), s.sem("gated")
        projected, squared, moved, var, rooted, scaled, summed, stored = (
            s.sem(n) for n in ("projected", "squared", "moved", "var", "rooted", "scaled", "summed", "stored"))
        block = ctx.enter_context(nc.Block())
        rows = [P, P, P, P, NS]
        first_rows = [0, P, 2 * P, 3 * P, SEQ]

        def heads_at(m, h, n):
            return kept.oT[:, h:h + n, m * P:(m + 1) * P] if m < 4 else kept.oTs[:, h:h + n, :]

        def load_x(sp, m):
            sp.wait_ge(gate_ready, min(m + 2, 5))
            if m:
                sp.wait_ge(summed, m)
            sp.dma_start(x[0:rows[m], :], io.xp[m * P:(m + 1) * P, :] if m < 4 else io.xs).then_inc(x_in, 16)

        @block.sync
        def _(sp):
            src = io.w_out.rearrange("(h p) n -> p h n", p=P)
            for m in range(5):
                if m:
                    sp.wait_ge(turned, 4 * m)
                r = slice(first_rows[m], first_rows[m] + rows[m])
                sp.dma_start(gate[0:rows[m], 0:512], io.proj[r, SB_G:SB_G + 512]).then_inc(gate_in, 16)
                sp.dma_start(gate[0:rows[m], 512:1280], io.proj[r, DSA_G:DSA_G + 768]).then_inc(gate_in, 16)
                sp.dma_start(gate[0:rows[m], 1280:2048], io.proj[r, NSA_G:NSA_G + 768]).then_inc(gate_in, 16)
                if m == 0:
                    for c in range(4):
                        sp.dma_start(w[:, :, c * CH:(c + 1) * CH], src[:, :, c * CH:(c + 1) * CH]).then_inc(w_in[c], 16)
                    sp.dma_start(gain[:], io.norm_post.to_broadcast([P, D])).then_inc(gain_in, 16)
                if m:
                    load_x(sp, m - 1)
            load_x(sp, 4)

        @block.gpsimd
        def _(pool):
            for m in range(5):
                pool.wait_ge(summed, m + 1)
                pool.dma_start(io.y_p[m * P:(m + 1) * P, :] if m < 4 else io.y_s, y[0:rows[m], :]).then_inc(stored, 16)
            pool.wait_ge(stored, 80)

        @block.scalar
        def _(act):
            act.preload_act_table_set("natural_log_exp_and_others")

            def sigmoid(m):
                act.wait_ge(gate_in, 48 * (m + 1))
                if m:
                    act.wait_ge(gate_ready, m)
                if m > 1:
                    act.wait_ge(summed, m - 1)
                r = sig[0:rows[m], :]
                act.activation(r, gate[0:rows[m], :], ACT.Exp, scale=-1.0).then_inc(sig_step, 1)
                act.wait_ge(sig_step, 2 * m + 1)
                act.activation(r, r, ACT.Ln, bias=1.0).then_inc(sig_step, 1)
                act.wait_ge(sig_step, 2 * m + 2)
                act.activation(r, r, ACT.Exp, scale=-1.0).then_inc(sig_exp, 1)

            sigmoid(0)
            for m in range(5):
                if m < 4:
                    sigmoid(m + 1)
                for c in range(4):
                    k = 4 * m + c
                    act.wait_ge(moved, k + 1)
                    if k:
                        act.wait_ge(squared, k)
                    act.activation(sq[0:rows[m], :], y[0:rows[m], c * CH:(c + 1) * CH], ACT.Square, accum_out=ss[0:rows[m], m, c:c + 1]).then_inc(squared, 1)
                act.wait_ge(var, 2 * m + 2)
                r = rstd[0:rows[m], m:m + 1]
                act.activation(r, r, ACT.Ln).then_inc(rooted, 1)
                act.wait_ge(rooted, 2 * m + 1)
                act.activation(r, r, ACT.Exp, scale=-0.5).then_inc(rooted, 1)

        @block.tensor
        def _(pe):
            def turn(m):
                pe.wait_ge(gate_ready, m + 1)
                for q in range(4):
                    n = 4 * m + q
                    if n >= 2:
                        pe.wait_ge(gated, n - 1)
                    for k in range(4):
                        last = pe.transpose(tp[n % 2][:, k, 0:rows[m]], gate[0:rows[m], (4 * q + k) * P:(4 * q + k + 1) * P], kept.ident[0:rows[m], 0:rows[m]])
                    last.then_inc(turned, 1)

            turn(0)
            for m in range(5):
                pe.wait_ge(gated, 4 * m + 4)
                for c in range(4):
                    k = 4 * m + c
                    pe.wait_ge(w_in[c], 16)
                    if k >= 4:
                        pe.wait_ge(moved, k - 3)
                    for h in range(16):
                        last = pe.matmul(yp[k % 4][0:rows[m], :], heads_at(m, h, 1)[:, 0, :], w[:, h, c * CH:(c + 1) * CH], start=(h == 0), stop=(h == 15))
                    last.then_inc(projected, 1)
                    if c == 1 and m < 4:
                        turn(m + 1)

        @block.vector
        def _(dve):
            def multiply(m):
                r = rows[m]
                dve.wait_ge(sig_exp, m + 1)
                dve.tensor_tensor(gate[0:r, :], gate[0:r, :], sig[0:r, :], ALU.mult).then_inc(gate_ready, 1)

            def apply(m):
                for q in range(4):
                    n = 4 * m + q
                    dve.wait_ge(turned, n + 1)
                    o = heads_at(m, 4 * q, 4)
                    dve.tensor_tensor(o, o, tp[n % 2][:, :, 0:rows[m]], ALU.mult).then_inc(gated, 1)

            multiply(0)
            apply(0)
            dve.wait_ge(gain_in, 16)
            for m in range(5):
                r = rows[m]
                if m < 4:
                    multiply(m + 1)
                for c in range(4):
                    k = 4 * m + c
                    dve.wait_ge(projected, k + 1)
                    if m:
                        dve.wait_ge(stored, 16 * m)
                    dve.tensor_copy(y[0:r, c * CH:(c + 1) * CH], yp[k % 4][0:r, :]).then_inc(moved, 1)
                    if c == 1 and m < 4:
                        apply(m + 1)
                dve.wait_ge(squared, 4 * m + 4)
                dve.tensor_reduce(rstd[0:r, m:m + 1], ss[0:r, m, :], AX.X, ALU.add).then_inc(var, 1)
                dve.wait_ge(var, 2 * m + 1)
                dve.tensor_scalar(rstd[0:r, m:m + 1], rstd[0:r, m:m + 1], 1.0 / D, EPS, ALU.mult, ALU.add).then_inc(var, 1)
                dve.wait_ge(rooted, 2 * m + 2)
                dve.wait_ge(moved, 4 * m + 4)
                dve.scalar_tensor_tensor(y[0:r, :], y[0:r, :], rstd[0:r, m:m + 1], gain[0:r, :], ALU.mult, ALU.mult).then_inc(scaled, 1)
                dve.wait_ge(scaled, m + 1)
                dve.wait_ge(x_in, 16 * (m + 1))
                dve.tensor_tensor(y[0:r, :], y[0:r, :], x[0:r, :], ALU.add).then_inc(summed, 1)


def program(nc, io):
    with ExitStack() as ctx:
        s = Scope(nc, ctx, "kept")
        kept = Kept()
        kept.consts = s.sb("consts", [P, C_KEPT])
        kept.ident = kept.consts[:, C_ID:C_ID + P]
        kept.sel_e = s.sb("sel_e", [P, 4 * P], BF16)
        kept.sel_d = s.sb("sel_d", [NS, 4 * P], BF16)
        kept.ident_b = s.sb("ident_b", [P, P], BF16)
        kept.pages = s.sb("pages", [1, NB * NPG], I32)
        kept.paired = s.sb("paired", [1, NB * NPG], I32)
        kept.by_chunk = s.sb("by_chunk", [1, NB * NPG], I32)
        with nc.sbuf_tensor("h_hi", [P, KT_IN, TOK], F32R) as h_hi, nc.sbuf_tensor("h_lo", [P, KT_IN, TOK], F32R) as h_lo:
            setup_and_norm(nc, io, kept, h_hi, h_lo)
            project_in(nc, io, h_hi, h_lo)
        kept.cmp_kp = s.sb("cmp_kp", [P, 2, 16])
        kept.cmp_vp = s.sb("cmp_vp", [16, 2, DH])
        kept.oTs = s.sb("oTs", [P, 16, NS])
        with ExitStack() as sample_ctx:
            sample = Scope(nc, sample_ctx, "kept")
            place_queries(kept, sample)
            kept.drop_blk = sample.sb("drop_blk", [P, NSB], BF16)
            with nc.sbuf_tensor("cmp_k", [P, NB, 2, NC], F32) as kept.cmp_k, nc.sbuf_tensor("cmp_v", [P, NB, 2, DH], F32) as kept.cmp_v:
                compress(nc, io, kept)
                prepare(nc, io, kept)
                cmp_sample(nc, io, kept)
            kept.drop = sample.sb("drop", [NS, KEYS], BF16)
            with nc.sbuf_tensor("scores", [NS, KEYS], F32) as kept.scores:
                index_scores(nc, io, kept)
                stick_breaking(nc, io, kept)
            kept.bias_nsa = sample.sb("bias_nsa", [P, KEYS])[:]
            with nc.sbuf_tensor("bias_dsa", [P, KEYS], F32) as bias_dsa:
                kept.bias_dsa = bias_dsa[:]
                dsa_sample(nc, io, kept)
            slc_sample(nc, io, kept)
            win_sample(nc, io, kept)
        kept.oT = s.sb("oT", [P, 16, SEQ])
        with ExitStack() as prompt_ctx:
            prompt = Scope(nc, prompt_ctx, "kept")
            prompt_prepare(nc, io, kept, prompt)
            prompt_attention(nc, io, kept, prompt)
        finish(nc, io, kept, s)


_INS = ['x_prompt', 'x_sample', 'cache_sb_kv', 'cache_dsa_kv', 'cache_dsa_idx', 'cache_nsa_kv', 'state_nsa_win', 'page_table',
        'w_in', 'w_out', 'norm_pre', 'norm_post', 'cmp_pe', 'cmp_w1', 'cmp_w2', 'rel_bias']
_OUTS = [(1, SEQ, D), (NB, NT, D), (1, 1, SEQ, 2, 4, DH), (1, NB, NT, 2, 4, DH), (1, 1, SEQ, 2, 2, DH), (1, NB, NT, 2, 2, DH),
         (1, 1, SEQ, 64), (1, NB, NT, 64), (1, 1, SEQ, 4, 2, DH), (1, NB, NT, 4, 2, DH),
         (1, 1, WIN, 2, 2, DH), (1, NB, WIN, 2, 2, DH)]


def describe(nc, shapes):
    def inp(name, shape, dt=F32):
        return nc.dram_tensor(f"in_{name}_dram", shape, dt, kind="ExternalInput").ap()

    a = {n: inp(n, *shapes[n]) for n in _INS}
    io = Io()
    io.consts = inp("constants", [P, C_END])
    io.onehot = inp("onehot", [NBUCK, LINE])
    io.xp = a['x_prompt'].rearrange("a s d -> (a s) d")
    io.xs = a['x_sample'].rearrange("b t d -> (b t) d")
    io.sb_cache = a['cache_sb_kv'].rearrange("l n p a h d -> (l n) p (a h d)")
    io.dsa_cache = a['cache_dsa_kv'].rearrange("l n p a h d -> (l n) p (a h d)")
    io.idx_cache = a['cache_dsa_idx'].rearrange("l n p d -> (l n) p d")
    io.nsa_cache = a['cache_nsa_kv'].rearrange("l n p a h d -> (l n) p (a h d)")
    io.win_state = a['state_nsa_win'].rearrange("l b w a h d -> (l b) w (a h d)")
    io.page_table = a['page_table']
    io.w_in = a['w_in'].rearrange("l k n -> (l k) n")
    io.w_out = a['w_out'].rearrange("l k n -> (l k) n")
    io.norm_pre = a['norm_pre'].rearrange("l d -> (l d)")
    io.norm_post = a['norm_post']
    io.cmp_pe = a['cmp_pe'].rearrange("l r p k d -> (l r) (p k d)")
    io.cmp_w1 = a['cmp_w1'].rearrange("l p k (r d) e -> (l p k) d r e", d=DH)
    io.cmp_w2 = a['cmp_w2'].rearrange("l p k e f -> (l p k) e f")
    io.rel_bias = a['rel_bias']
    io.line = nc.dram_tensor("bias_line", [HB, LINE], F32).ap()
    io.lines = nc.dram_tensor("bias_lines", [P, HB, XL], F32).ap()
    io.proj = nc.dram_tensor("proj", [TOK, DIN], F32).ap()
    outs = [nc.dram_tensor(f"out_{i}_dram", shape, F32, kind="ExternalOutput").ap() for i, shape in enumerate(_OUTS)]
    io.y_p = outs[0].rearrange("a s d -> (a s) d")
    io.y_s = outs[1].rearrange("b t d -> (b t) d")
    io.new_rows = []
    for n, (col, width) in enumerate(((SB_K, 1024), (DSA_K, 512), (IDX_K, 64), (NSA_KC, 1024))):
        flat = "l b s d -> (l b s) d" if width == 64 else "l b s a h d -> (l b s) (a h d)"
        io.new_rows.append((outs[2 + 2 * n].rearrange(flat), outs[3 + 2 * n].rearrange(flat), col, width))
    io.win_p = outs[10].rearrange("l b s a h d -> (l b s) (a h d)")
    io.win_s = outs[11].rearrange("l b s a h d -> (l b) s (a h d)")
    io.n_pool = shapes['cache_sb_kv'][0][1]
    return io


def kernel(**inputs):
    import concourse.bacc as _bacc
    from concourse.bass_utils import run_bass_kernel_spmd as _run

    nc = _bacc.Bacc("TRN2", target_bir_lowering=False, num_devices=1)
    arrays, shapes = {}, {}
    for name in _INS:
        a = np.ascontiguousarray(inputs[name])
        arrays[f"in_{name}_dram"] = a
        shapes[name] = (a.shape, mybir.dt.from_np(a.dtype))
    arrays["in_constants_dram"], arrays["in_onehot_dram"] = constants()
    program(nc, describe(nc, shapes))
    r = _run(nc, [arrays], core_ids=[0])
    return tuple(r.results[0][f"out_{i}_dram"] for i in range(len(_OUTS)))
```
